# Optimizing a Trainium2 kernel written in Bass

```python
import math
import jax, jax.numpy as jnp
from jax import lax
import numpy as np

D_MODEL = 1024
BATCH = 1
SEQ = 256
DEPTH = 1
DEC_BATCH = 8
DEC_SEQ = 4
PAST_LEN = 1024
PAGE_SIZE = 128

ATTN_WIDTH = D_MODEL // 2
SSM_WIDTH = D_MODEL - ATTN_WIDTH
HEAD_DIM = 64
N_HEADS = ATTN_WIDTH // HEAD_DIM
DILATED_GROUPS = ((128, 1), (512, 4), (2048, 16))
MAX_WINDOW = max(w for w, _ in DILATED_GROUPS)
SSM_GROUP = 16
N_SSM_GROUPS = SSM_WIDTH // SSM_GROUP
SSM_STATE = 64
MIX_IN = 3 * ATTN_WIDTH + SSM_WIDTH
N_EXPERTS = 32
TOP_K = 4
D_FF = D_MODEL
SWIGLU_LIMIT = 7.0
SWIGLU_ALPHA = 1.702
MOE_BLOCK = 128
RMS_EPS = 1e-5
NEG_INF = -1e30

kernel_name = "hymba_dilated_s5_moe_step"

def rmsnorm(x, g):
    xf = x.astype(jnp.float32)
    y = xf * lax.rsqrt(jnp.mean(xf * xf, axis=-1, keepdims=True) + RMS_EPS)
    return (y * g.astype(jnp.float32)).astype(x.dtype)

def combine_groups(outs, lses):
    w = jax.nn.softmax(jnp.stack(lses, 0), axis=0)
    return jnp.sum(w[..., None] * jnp.stack(outs, 0), axis=0)

def dilated_attention_prompt(q, k, v):
    B, S, H, E = q.shape
    scale = HEAD_DIM ** -0.5
    outs, lses = [], []
    for w, d in DILATED_GROUPS:
        nb = w // d
        span = d * nb
        sp = -(-S // span) * span
        nblk = sp // span
        m_len = sp // d

        def to_blocks(t):
            t = jnp.pad(t, ((0, 0), (0, sp - S), (0, 0), (0, 0)))
            t = t.reshape(B, m_len, d, H, E).transpose(0, 2, 1, 3, 4)
            return t.reshape(B, d, nblk, nb, H, E)

        def with_prev(t):
            prev = jnp.pad(t, ((0, 0), (0, 0), (1, 0), (0, 0), (0, 0), (0, 0)))[:, :, :-1]
            return jnp.concatenate([prev, t], axis=3)

        qb = to_blocks(q)
        kk = with_prev(to_blocks(k))
        vv = with_prev(to_blocks(v))
        s = jnp.einsum('brnqhe,brnkhe->brnhqk', qb, kk,
                       preferred_element_type=jnp.float32) * scale
        qi = jnp.arange(nb)[:, None]
        kj = jnp.arange(2 * nb)[None, :]
        rel = nb + qi - kj
        band = (rel >= 0) & (rel <= nb)
        not_before_start = (jnp.arange(nblk)[:, None, None] > 0) | (kj[None] >= nb)
        valid = band[None] & not_before_start
        s = jnp.where(valid[:, None], s, NEG_INF)
        m = jnp.max(s, axis=-1, keepdims=True)
        p = jnp.exp(s - m)
        l = jnp.sum(p, axis=-1, keepdims=True)
        o = jnp.einsum('brnhqk,brnkhe->brnqhe', p, vv.astype(jnp.float32))
        o = o / jnp.swapaxes(l[..., 0], 3, 4)[..., None]
        lse = jnp.swapaxes((m + jnp.log(l))[..., 0], 3, 4)
        o = o.reshape(B, d, m_len, H, E).transpose(0, 2, 1, 3, 4).reshape(B, sp, H, E)[:, :S]
        lse = lse.reshape(B, d, m_len, H).transpose(0, 2, 1, 3).reshape(B, sp, H)[:, :S]
        outs.append(o)
        lses.append(lse)
    return combine_groups(outs, lses)

def dilated_attention_sample(q, k_all, v_all, n_buf):
    T = q.shape[1]
    scale = HEAD_DIM ** -0.5
    outs, lses = [], []
    for w, d in DILATED_GROUPS:
        nb = w // d
        idx = n_buf + jnp.arange(T)[:, None] - d * jnp.arange(nb + 1)[None, :]
        valid = idx >= 0
        idx = jnp.maximum(idx, 0)
        kg = k_all[:, idx]
        vg = v_all[:, idx]
        s = jnp.einsum('bthe,btjhe->bthj', q, kg,
                       preferred_element_type=jnp.float32) * scale
        s = jnp.where(valid[None, :, None, :], s, NEG_INF)
        m = jnp.max(s, axis=-1, keepdims=True)
        p = jnp.exp(s - m)
        l = jnp.sum(p, axis=-1, keepdims=True)
        o = jnp.einsum('bthj,btjhe->bthe', p, vg.astype(jnp.float32)) / l
        outs.append(o)
        lses.append((m + jnp.log(l))[..., 0])
    return combine_groups(outs, lses)

def s5_ssm(u, h0, a_re, a_im, log_dt, b_re, b_im, c_re, c_im, d_skip):
    f32 = jnp.float32
    uf = u.astype(f32)
    lam = lax.complex(a_re.astype(f32), a_im.astype(f32))
    dt = jnp.exp(log_dt.astype(f32))[:, None]
    a_bar = jnp.exp(lam * dt)
    b_bar = ((a_bar - 1.0) / lam)[..., None] * lax.complex(b_re.astype(f32), b_im.astype(f32))
    bu = jnp.einsum('gnc,bsgc->bsgn', b_bar, uf.astype(jnp.complex64))
    bu = bu.at[:, 0].add(a_bar * h0)
    a_seq = jnp.broadcast_to(a_bar, bu.shape)

    def combine(left, right):
        a1, b1 = left
        a2, b2 = right
        return a1 * a2, a2 * b1 + b2

    _, states = lax.associative_scan(combine, (a_seq, bu), axis=1)
    c = lax.complex(c_re.astype(f32), c_im.astype(f32))
    y = jnp.einsum('gcn,bsgn->bsgc', c, states).real + d_skip.astype(f32) * uf
    return y, states[:, -1]

def moe(h, w_router, b_router, w1, b1, w2, b2):
    N, D = h.shape
    logits = jnp.dot(h.astype(jnp.float32), w_router.astype(jnp.float32)) + b_router.astype(jnp.float32)
    top_v, top_i = lax.top_k(logits, TOP_K)
    gates = jax.nn.softmax(top_v, axis=-1)
    n_assign = N * TOP_K
    e_flat = top_i.reshape(-1)
    tok = jnp.repeat(jnp.arange(N, dtype=jnp.int32), TOP_K)
    g_flat = gates.reshape(-1)
    order = jnp.argsort(e_flat)
    e_sorted = e_flat[order]
    sizes = jnp.bincount(e_flat, length=N_EXPERTS)
    padded = (sizes + MOE_BLOCK - 1) // MOE_BLOCK * MOE_BLOCK
    start = jnp.cumsum(sizes) - sizes
    pend = jnp.cumsum(padded)
    pstart = pend - padded
    dest = pstart[e_sorted] + (jnp.arange(n_assign) - start[e_sorted])
    n_blocks = -(-n_assign // MOE_BLOCK) + N_EXPERTS
    rows = n_blocks * MOE_BLOCK
    row_tok = jnp.full((rows,), N, jnp.int32).at[dest].set(tok[order])
    row_gate = jnp.zeros((rows,), jnp.float32).at[dest].set(g_flat[order])
    block_exp = jnp.clip(jnp.searchsorted(pend, jnp.arange(n_blocks) * MOE_BLOCK, side='right'),
                         0, N_EXPERTS - 1)
    xs = jnp.concatenate([h, jnp.zeros((1, D), h.dtype)], axis=0)[row_tok]
    xs = xs.reshape(n_blocks, MOE_BLOCK, D)

    def expert_block(args):
        xb, e = args
        a = jnp.dot(xb, w1[e]) + b1[e]
        x_glu = jnp.minimum(a[:, :D_FF], SWIGLU_LIMIT)
        x_lin = jnp.clip(a[:, D_FF:], -SWIGLU_LIMIT, SWIGLU_LIMIT)
        mid = x_glu * jax.nn.sigmoid(SWIGLU_ALPHA * x_glu) * (x_lin + 1.0)
        return jnp.dot(mid, w2[e]) + b2[e]

    ys = lax.map(expert_block, (xs, block_exp)).reshape(rows, D)
    out = jnp.zeros((N + 1, D), jnp.float32).at[row_tok].add(ys.astype(jnp.float32) * row_gate[:, None])
    return out[:N].astype(h.dtype)

def project(x, norm_g, w_in):
    B, S, _ = x.shape
    z = jnp.dot(rmsnorm(x, norm_g), w_in)
    A = ATTN_WIDTH
    q = z[..., :A].reshape(B, S, N_HEADS, HEAD_DIM)
    k = z[..., A:2 * A].reshape(B, S, N_HEADS, HEAD_DIM)
    v = z[..., 2 * A:3 * A].reshape(B, S, N_HEADS, HEAD_DIM)
    u = z[..., 3 * A:].reshape(B, S, N_SSM_GROUPS, SSM_GROUP)
    return q, k, v, u

def finish_layer(x, attn, ssm_y, attn_out_norm_g, w_glu, b_glu, ssm_out_norm_g, w_out,
                 norm_ffn_g, w_router, b_router, w1, b1, w2, b2):
    B, S, D = x.shape
    attn = attn.reshape(B, S, ATTN_WIDTH).astype(x.dtype)
    ssm_y = ssm_y.reshape(B, S, SSM_WIDTH).astype(x.dtype)
    g = jax.nn.gelu(ssm_y)
    ssm_o = g * jax.nn.sigmoid(jnp.dot(g, w_glu) + b_glu)
    mixed = jnp.concatenate([rmsnorm(attn, attn_out_norm_g), rmsnorm(ssm_o, ssm_out_norm_g)], axis=-1)
    x = x + jnp.dot(mixed, w_out)
    f = moe(rmsnorm(x, norm_ffn_g).reshape(B * S, D), w_router, b_router, w1, b1, w2, b2)
    return x + f.reshape(B, S, D)

def setup_inputs(seed: int = 0) -> dict:
    key = jax.random.key(seed)
    ks = jax.random.split(key, 32)
    f32 = jnp.float32
    nrm = lambda k, shape, s: jax.random.normal(k, shape, f32) * s
    w_buf = min(MAX_WINDOW, PAST_LEN)
    L = DEPTH
    return {
        "x_prompt": nrm(ks[0], (BATCH, SEQ, D_MODEL), 1.0),
        "x_sample": nrm(ks[1], (DEC_BATCH, DEC_SEQ, D_MODEL), 1.0),
        "cache_k": nrm(ks[2], (L, DEC_BATCH, w_buf, N_HEADS, HEAD_DIM), 1.0),
        "cache_v": nrm(ks[3], (L, DEC_BATCH, w_buf, N_HEADS, HEAD_DIM), 1.0),
        "state_ssm_re": nrm(ks[4], (L, DEC_BATCH, N_SSM_GROUPS, SSM_STATE), 1.0),
        "state_ssm_im": nrm(ks[5], (L, DEC_BATCH, N_SSM_GROUPS, SSM_STATE), 1.0),
        "norm_mix_g": 1.0 + nrm(ks[6], (L, D_MODEL), 0.02),
        "w_in": nrm(ks[7], (L, D_MODEL, MIX_IN), D_MODEL ** -0.5),
        "attn_out_norm_g": 1.0 + nrm(ks[8], (L, ATTN_WIDTH), 0.02),
        "ssm_a_re": -0.5 + nrm(ks[9], (L, N_SSM_GROUPS, SSM_STATE), 0.01),
        "ssm_a_im": math.pi * jnp.arange(SSM_STATE, dtype=f32) + nrm(ks[10], (L, N_SSM_GROUPS, SSM_STATE), 0.01),
        "ssm_log_dt": jax.random.uniform(ks[11], (L, N_SSM_GROUPS), f32, math.log(1e-3), math.log(1e-1)),
        "ssm_b_re": nrm(ks[12], (L, N_SSM_GROUPS, SSM_STATE, SSM_GROUP), (2 * SSM_GROUP) ** -0.5),
        "ssm_b_im": nrm(ks[13], (L, N_SSM_GROUPS, SSM_STATE, SSM_GROUP), (2 * SSM_GROUP) ** -0.5),
        "ssm_c_re": nrm(ks[14], (L, N_SSM_GROUPS, SSM_GROUP, SSM_STATE), (2 * SSM_STATE) ** -0.5),
        "ssm_c_im": nrm(ks[15], (L, N_SSM_GROUPS, SSM_GROUP, SSM_STATE), (2 * SSM_STATE) ** -0.5),
        "ssm_d": nrm(ks[16], (L, N_SSM_GROUPS, SSM_GROUP), 1.0),
        "w_glu": nrm(ks[17], (L, SSM_WIDTH, SSM_WIDTH), SSM_WIDTH ** -0.5),
        "b_glu": nrm(ks[18], (L, SSM_WIDTH), 0.01),
        "ssm_out_norm_g": 1.0 + nrm(ks[19], (L, SSM_WIDTH), 0.02),
        "w_out": nrm(ks[20], (L, D_MODEL, D_MODEL), D_MODEL ** -0.5),
        "norm_ffn_g": 1.0 + nrm(ks[21], (L, D_MODEL), 0.02),
        "w_router": nrm(ks[22], (L, D_MODEL, N_EXPERTS), D_MODEL ** -0.5),
        "b_router": nrm(ks[23], (L, N_EXPERTS), 0.01),
        "w_moe1": nrm(ks[24], (L, N_EXPERTS, D_MODEL, 2 * D_FF), D_MODEL ** -0.5),
        "b_moe1": nrm(ks[25], (L, N_EXPERTS, 2 * D_FF), 0.01),
        "w_moe2": nrm(ks[26], (L, N_EXPERTS, D_FF, D_MODEL), D_FF ** -0.5),
        "b_moe2": nrm(ks[27], (L, N_EXPERTS, D_MODEL), 0.01),
        "norm_final_g": 1.0 + nrm(ks[28], (D_MODEL,), 0.02),
    }

def reference(x_prompt, x_sample, cache_k, cache_v, state_ssm_re, state_ssm_im,
              norm_mix_g, w_in, attn_out_norm_g, ssm_a_re, ssm_a_im, ssm_log_dt,
              ssm_b_re, ssm_b_im, ssm_c_re, ssm_c_im, ssm_d, w_glu, b_glu, ssm_out_norm_g,
              w_out, norm_ffn_g, w_router, b_router, w_moe1, b_moe1, w_moe2, b_moe2,
              norm_final_g):
    hp, hs = x_prompt, x_sample
    Bp, S, _ = x_prompt.shape
    n_buf = cache_k.shape[2]
    keep = min(MAX_WINDOW, S)
    kp_l, vp_l, rep_l, imp_l, ks_l, vs_l, res_l, ims_l = [], [], [], [], [], [], [], []
    for l in range(DEPTH):
        ssm_p = (ssm_a_re[l], ssm_a_im[l], ssm_log_dt[l], ssm_b_re[l], ssm_b_im[l],
                 ssm_c_re[l], ssm_c_im[l], ssm_d[l])
        tail = (attn_out_norm_g[l], w_glu[l], b_glu[l], ssm_out_norm_g[l], w_out[l],
                norm_ffn_g[l], w_router[l], b_router[l], w_moe1[l], b_moe1[l], w_moe2[l], b_moe2[l])
        q, k, v, u = project(hp, norm_mix_g[l], w_in[l])
        attn = dilated_attention_prompt(q, k, v)
        h0 = jnp.zeros((Bp, N_SSM_GROUPS, SSM_STATE), jnp.complex64)
        ssm_y, h_last = s5_ssm(u, h0, *ssm_p)
        hp = finish_layer(hp, attn, ssm_y, *tail)
        kp_l.append(k[:, S - keep:])
        vp_l.append(v[:, S - keep:])
        rep_l.append(jnp.real(h_last))
        imp_l.append(jnp.imag(h_last))
        q, k, v, u = project(hs, norm_mix_g[l], w_in[l])
        k_all = jnp.concatenate([cache_k[l].astype(k.dtype), k], axis=1)
        v_all = jnp.concatenate([cache_v[l].astype(v.dtype), v], axis=1)
        attn = dilated_attention_sample(q, k_all, v_all, n_buf)
        h0 = lax.complex(state_ssm_re[l].astype(jnp.float32), state_ssm_im[l].astype(jnp.float32))
        ssm_y, h_last = s5_ssm(u, h0, *ssm_p)
        hs = finish_layer(hs, attn, ssm_y, *tail)
        ks_l.append(k)
        vs_l.append(v)
        res_l.append(jnp.real(h_last))
        ims_l.append(jnp.imag(h_last))
    y_prompt = rmsnorm(hp, norm_final_g)
    y_sample = rmsnorm(hs, norm_final_g)
    return (y_prompt, y_sample,
            jnp.stack(kp_l, 0), jnp.stack(vp_l, 0), jnp.stack(rep_l, 0), jnp.stack(imp_l, 0),
            jnp.stack(ks_l, 0), jnp.stack(vs_l, 0), jnp.stack(res_l, 0), jnp.stack(ims_l, 0))


_drawn_inputs = setup_inputs


def setup_inputs(seed=0):
    import zlib

    import numpy as np

    out = dict(_drawn_inputs(seed))
    spreads = {}
    factors = {'attn_out_norm_g': 2.849,
     'ssm_a_re': 73.458,
     'b_glu': 17.93,
     'b_router': 8.532,
     'b_moe1': 21.511,
     'b_moe2': 25.152,
     'norm_final_g': 20.343,
     'ssm_out_norm_g': 4.016,
     'norm_ffn_g': 2.86}
    for name, (base, spread) in spreads.items():
        noise = np.random.default_rng([zlib.crc32(name.encode()), seed]).standard_normal(out[name].shape)
        drawn = base * np.exp(spread * noise) if base else spread * noise
        out[name] = __import__('jax').numpy.asarray(drawn.astype(out[name].dtype))
    for name, factor in factors.items():
        out[name] = (out[name] * factor).astype(out[name].dtype)
    return out
```

```python
from contextlib import ExitStack

import numpy as np

import concourse.bass as bass
from concourse import mybir

F32 = mybir.dt.float32
I32 = mybir.dt.int32
U32 = mybir.dt.uint32
ALU = mybir.AluOpType
ACT = mybir.ActivationFunctionType
AX = mybir.AxisListType.X

P = 128
D = 1024
J = D // P
SEQ, NB, NSEQ = 256, 8, 4
NS = NB * NSEQ
NTOK = SEQ + NS
TILES = [(0, P), (P, P), (SEQ, NS)]
H, HD = 8, 64
SCALE = HD ** -0.5
PAST = 1024
NEXP, TOPK, DFF = 32, 4, 1024
CAP = 64
CHUNKS = -(-NTOK // CAP)
NI = 16
HALF = SEQ // 2
EPS = 1e-5
ALPHA, LIMIT = 1.702, 7.0
NEG = -1e30
TWO_PI = 6.283185307179586
TP_HI = 6.28125
TP_LO = TWO_PI - TP_HI
ROUND = 1.5 * 2.0 ** 23
PI_IN = 3.1415925
G_A = 0.7978845608028654 * 2.0
G_B = 0.044715

C_ID, C_TRI, C_BP, C_BS, C_IOTA, C_GM = 0, 128, 256, 640, 1472, 1792
C_ALL = 1920


def window_bias(delta):
    n = (((delta >= 0) & (delta <= 128)).astype(int)
         + ((delta >= 0) & (delta <= 512) & (delta % 4 == 0))
         + ((delta >= 0) & (delta <= 2048) & (delta % 16 == 0)))
    return np.where(n > 0, np.log(np.maximum(n, 1)), NEG)


def constants():
    c = np.zeros((P, C_ALL), np.float32)
    p = np.arange(P)[:, None]
    f = np.arange(P)[None, :]
    c[:, C_ID:C_ID + P] = p == f
    c[:, C_TRI:C_TRI + P] = p < f
    c[:, C_BP:C_BP + P] = window_bias(p - f)
    c[:, C_BP + P:C_BP + 3 * P] = window_bias(P + p - np.arange(SEQ)[None, :])
    qpos = PAST + p % NSEQ
    r = np.arange(P)
    for rt in range(4):
        c[:, C_BS + rt * P:C_BS + (rt + 1) * P] = window_bias(qpos - (512 + 4 * r + rt)[None, :])
    for half in range(2):
        at = C_BS + 512 + 160 * half
        c[:, at:at + P] = window_bias(qpos - (16 * (r % 32) + r // 32)[None, :])
        s = np.arange(NS)[None, :]
        same = (half * 4 + p // 32) == s // NSEQ
        c[:, at + P:at + 160] = np.where(same, window_bias(qpos - (PAST + s % NSEQ)), NEG)
    c[:, C_IOTA:C_IOTA + 320] = np.arange(320)
    c[:, C_GM:C_GM + P] = (f // 16) % 2 == p // 64
    return c


def decoder_step(nc, I, O):
    with ExitStack() as ctx:
        def sb(name, shape, dt=F32):
            return ctx.enter_context(nc.sbuf_tensor(name, shape, dt))

        def sem(name):
            return ctx.enter_context(nc.semaphore(name))

        ring = sb("ring", [P, 6, 4096])
        w_in = ring[:, 0:4, :].rearrange("p s n -> p (s n)").rearrange("p (g j n) -> p g j n", g=4, j=J)
        kv = ring[:, 0:4, :].rearrange("p s n -> p (s n)")
        k_cache = kv[:, 0:2 * 2560].rearrange("p (s n) -> p s n", s=2)
        v_cache = kv[:, 2 * 2560:6 * 2560].rearrange("p (s n) -> p s n", s=4)
        w_out = ring[:, 4:6, :].rearrange("p s n -> p (s n)").rearrange("p (j n) -> p j n", j=J)

        con = sb("con", [P, C_ALL])
        ident = con[:, C_ID:C_ID + P]
        tri = con[:, C_TRI:C_TRI + P]
        iota = con[:, C_IOTA:C_IOTA + 320]
        gmask = con[:, C_GM:C_GM + P]
        x = sb("x", [P, 3, D])
        accT = sb("accT", [P, J, NTOK])
        uni = sb("uni", [P, 8704])
        qkvu = uni[:, 0:16 * NTOK].rearrange("p (c t) -> p c t", c=16)
        xn = uni[:, 0:3 * D].rearrange("p (t d) -> p t d", t=3)
        e_tab = uni[:, 4608:8704].rearrange("p (r i t) -> p r i t", r=2, i=NI)
        h = uni[:, 0:3072].rearrange("p (t d) -> p t d", t=3)
        o = 3072
        xe = uni[:, o:o + 512].rearrange("p (j s) -> p j s", j=J)
        act_in = uni[:, o + 512:o + 1536].rearrange("p (b g m s) -> p b g m s", b=2, g=2, m=4)
        sig = uni[:, o + 1536:o + 2048].rearrange("p (b m s) -> p b m s", b=2, m=4)
        mid = uni[:, o + 2048:o + 2560].rearrange("p (b m s) -> p b m s", b=2, m=4)
        yT = uni[:, o + 2560:o + 3072]
        y = uni[0:CAP, o + 3072:o + 4096]
        sel = uni[:, o + 4096:o + 4288].rearrange("p (t s) -> p t s", t=3)
        selg = uni[:, o + 4288:o + 4480].rearrange("p (t s) -> p t s", t=3)
        selT = uni[0:CAP, o + 4480:o + 4768]
        b1T = uni[:, o + 4768:o + 5280].rearrange("p (e m) -> p e m", e=NEXP)
        posm = uni[:, o + 5280:o + 5376].rearrange("p (e t) -> p e t", e=NEXP)
        gate = uni[:, o + 5376:o + 5472].rearrange("p (e t) -> p e t", e=NEXP)

        tmp = sb("tmp", [P, 4096])
        e_tmp = tmp[:, 0:2048].rearrange("p (a i t) -> p a i t", a=2, i=NI)
        scb = tmp[:, 0:768].rearrange("p (b n) -> p b n", b=2)
        prb = tmp[:, 768:1536].rearrange("p (b n) -> p b n", b=2)
        ptb = tmp[:, 1536:2304].rearrange("p (b n) -> p b n", b=2)
        sT = tmp[:, 0:768]
        s_s = tmp[:, 768:1440]
        p_s = tmp[:, 1440:2112]
        p_T = tmp[:, 2112:2880]
        kT_s = tmp[:, 2880:3904].rearrange("p (b n) -> p b n", b=2)
        b1_rows = tmp[0:NEXP, 0:2048]
        b2_rows = tmp[0:NEXP, 2048:3072]
        g_row = tmp[:, 3072:4096]

        kv_rows = sb("kv_rows", [P, 2, 3, 512])
        aT = sb("aT", [P, 4, NTOK])
        yS = sb("yS", [P, 4, NTOK])
        w_glu = sb("w_glu", [P, 4, 512])
        par = sb("par", [P, 256])
        ld = sb("ld", [P, 4])
        prm = sb("prm", [P, 24, NI])
        PA_LR, PA_LI, PA_RD, PA_TH, PA_R, PA_C, PA_S, PA_AR, PA_AI, PA_FR, PA_FI = range(11)
        s5 = ring[:, 4:6, :].rearrange("p s n -> p (s n)")
        s5_at = [0]

        def s5_buf(n):
            s5_at[0] += n
            return s5[:, s5_at[0] - n:s5_at[0]]

        bnat = s5_buf(512).rearrange("p (r n) -> p r n", r=2)
        xb = tmp[:, 2048:3072].rearrange("p (r n) -> p r n", r=2)
        cnat = tmp[:, 3072:4096].rearrange("p (r b n) -> p r b n", r=2, b=4)
        bT = s5_buf(1024).rearrange("p (r n) -> p r n", r=2)
        cT = s5_buf(1024).rearrange("p (r n) -> p r n", r=2)
        h0row = sb("h0row", [P, 2, P])
        h0 = s5_buf(256).rearrange("p (r n) -> p r n", r=2)
        hs = s5_buf(1024).rearrange("p (r i n) -> p r i n", r=2, i=NI)
        bus = aT[:, :, :].rearrange("p a t -> p (a t)")[:, 0:1024]
        ssm_a = s5_buf(512).rearrange("p (a t) -> p a t", a=4)
        ssm_b = s5_buf(512).rearrange("p (a t) -> p a t", a=4)
        ssm_g = s5_buf(1024).rearrange("p (b r a t) -> p b r a t", b=2, r=2, a=2)
        ssm_h = s5_buf(1024).rearrange("p (b r t) -> p b r t", b=2, r=2)
        ssm_p = s5_buf(512).rearrange("p (a t) -> p a t", a=4)
        hf = sb("hf", [P, 2, NI])
        sf = h0row
        st_out = sb("st_out", [P, 4, P])
        qbd = sb("qbd", [P, 4, NB, 8])
        wr = sb("wr", [P, J, NEXP])
        vec = sb("vec", [P, 64])
        gmx, dsk, bgl, gat, gss = (vec[:, 0:8], vec[:, 8:12], vec[:, 12:16], vec[:, 16:20], vec[:, 20:24])
        bro = sb("bro", [P, NEXP])
        ones = sb("ones", [P, P])
        kvg = uni[:, 4608:5760]
        sqa = uni[:, 5760:6912].rearrange("p (b t) -> p b t", b=4)
        sqs = uni[:, 6912:8064].rearrange("p (b t) -> p b t", b=4)
        st = sb("st", [P, 96])
        gT = sb("gT", [NEXP, NTOK])
        rt_s = sb("rt_s", [P, 3, 6, NEXP])
        top = sb("top", [P, 3, 32])
        tidx = sb("tidx", [P, 3, 8], U32)
        oh = sb("oh", [P, 3, 2, TOPK, NEXP])
        cnt = sb("cnt", [P, NEXP], I32)
        ps = ctx.enter_context(nc.psum_tensor("ps", [P, 8, 512], F32))

        names = """x con prm win0 win1 wglu wout late gff gfi b1 kload0 kload1 vload0 vload1 vload2 vload3
            out ss ms rt xn rows dt prmT exps sin red crev xT_ps xT_d xT_a proj proj_ev etab fdone bT_ps bT
            bu bu_used hlo g1 hhi yps yblk bus_ps bus hs ysps yS_ready kvr_ps kvr qbd s_ps nm ex pn pt_ps pt o_ps aT
            kt_ps ktA ktD st_ps stE ts_ps nms exs pns pts_ps pts pv aTs sto_ps sto hfin sfin
            gel1 gel2 gg glu_ps glu sq sqA ssq ms2 rt2 mix wo_ps x2 ss3 ms3 rt3 h hT_ps hT lg rout posps posm cntr gT_ps gT b2ps acc0 b1T_ps b1T
            init wfree sel gath xe selT_ps selT mm1 glin sgm midr mm2 yTr y_ps yr comb acc chain_a chain_v chain_p swc gex ysv
            fin_ps x3 ss4 ms4 rt4 yfin""".split()
        S = {n: sem("s_" + n) for n in names}
        s_w = [sem(f"s_w{k}") for k in range(6)]
        NPRM = 17

        def bc(ap, shape):
            return ap.broadcast_to(shape)

        block = ctx.enter_context(nc.Block())

        def piece(e, k):
            if k < 4:
                src = I["w_moe1"][0, e, :, :] if isinstance(e, int) else I["w_moe1"][0, bass.ds(e, 1), :, :].rearrange("a d f -> (a d) f")
                return ring[:, k, :].rearrange("p (j n) -> p j n", j=2), src.rearrange("(p j) n -> p j n", j=J)[:, 2 * k:2 * k + 2, :]
            src = I["w_moe2"][0, e, :, :] if isinstance(e, int) else I["w_moe2"][0, bass.ds(e, 1), :, :].rearrange("a d f -> (a d) f")
            return ring[:, k, :].rearrange("p (m n) -> p m n", m=4), src.rearrange("(m q) n -> q m n", q=P)[:, 4 * (k - 4):4 * (k - 3), :]

        def run_experts(eng, chunk):
            done = eng.alloc_register()
            eng.reg_mov(done, 0)
            with eng.Fori(0, NEXP) as e:
                count = eng.value_load(cnt[0:1, bass.ds(e, 1)], min_val=0, max_val=NTOK)
                with eng.If(count > CAP):
                    with eng.Fori(1, CHUNKS) as c:
                        with eng.If(count > c * CAP):
                            chunk(eng.snap(done, min_val=0, max_val=NEXP * CHUNKS), e, c * CAP, False)
                            eng.reg_add(done, done, 1)
                chunk(eng.snap(done, min_val=0, max_val=NEXP * CHUNKS), e, 0, True)
                eng.reg_add(done, done, 1)
            return eng.snap(done, min_val=0, max_val=NEXP * CHUNKS)

        @block.sync
        def _(sp):
            sp.dma_start(x[:, 0:2, :], I["x_prompt"][0].rearrange("(t p) d -> p t d", p=P)).then_inc(S["x"], 16)
            sp.dma_start(x[0:NS, 2, :], I["x_sample"].rearrange("b t d -> (b t) d")).then_inc(S["x"], 16)
            wv = I["w_in"][0].rearrange("(p j) (g n) -> p g j n", j=J, g=4)
            sp.dma_start(w_in[:, 3, :, :], wv[:, 3]).then_inc(S["win0"], 16)
            sp.dma_start(con[:, :], I["con"]).then_inc(S["con"], 16)
            for g in range(3):
                sp.dma_start(w_in[:, g, :, :], wv[:, g]).then_inc(S["win1"], 16)
            sp.dma_start(w_glu[:, :, :], I["w_glu"][0].rearrange("(j p) n -> p j n", p=P)).then_inc(S["wglu"], 16)
            sp.dma_start(wr[:, :, :], I["w_router"][0].rearrange("(p j) n -> p j n", j=J)).then_inc(S["wglu"], 16)

            def load_cache(name, dst, b, sm):
                c = I[name][0, b].rearrange("r h e -> r (h e)")
                sp.dma_start(dst[:, 0:2048], c[512:1024].rearrange("(p j) n -> p (j n)", j=4)).then_inc(sm, 16)
                lo = c[0:512].rearrange("(i s) n -> s i n", s=16)
                for s in range(4):
                    sp.dma_start(dst[32 * s:32 * s + 32, 2048:2560], lo[s]).then_inc(sm, 16)

            sp.wait_ge(S["proj"], 16)
            for b in range(NB):
                if b >= 2:
                    sp.wait_ge(S["kt_ps"], 5 * (b - 1))
                load_cache("cache_k", k_cache[:, b % 2, :], b, S[f"kload{b % 2}"])
                if b >= 4:
                    sp.wait_ge(S["pv"], 1)
                load_cache("cache_v", v_cache[:, b % 4, :], b, S[f"vload{b % 4}"])
                if b == 1:
                    sp.wait_ge(S["sto_ps"], 1)
                    sp.dma_start(w_out, I["w_out"][0].rearrange("(j p) n -> p j n", p=P)).then_inc(S["wout"], 16)
            sp.wait_ge(S["kvr"], 6)
            for a, nm in enumerate("kv"):
                sp.dma_start(O[nm + "_p"].rearrange("a b (t p) h e -> p (a b t) (h e)", p=P), kv_rows[:, a, 0:2, :]).then_inc(S["out"], 16)
                sp.dma_start(O[nm + "_s"].rearrange("a b t h e -> (a b t) (h e)"), kv_rows[0:NS, a, 2, :]).then_inc(S["out"], 16)
            sp.wait_ge(S["sto"], 1)
            for r, nm in enumerate(("re_p", "im_p")):
                sp.dma_start(O[nm].rearrange("a b (i g) n -> (a b i) (g n)", g=2), st_out[0:NI, r, :]).then_inc(S["out"], 16)
            for r, nm in enumerate(("re_s", "im_s")):
                sp.dma_start(O[nm].rearrange("a b (i g) n -> (a b i) (g n)", g=2), st_out[:, 2 + r, :]).then_inc(S["out"], 16)
            sp.wait_ge(S["pv"], 2)
            sp.dma_start(b1_rows, I["b_moe1"][0]).then_inc(S["b1"], 16)
            sp.dma_start(b2_rows, I["b_moe2"][0]).then_inc(S["b1"], 16)
            sp.dma_start(g_row, I["norm_ffn_g"].broadcast_to([P, D])).then_inc(S["gff"], 16)
            for k in range(4):
                sp.dma_start(*piece(0, k)).then_inc(s_w[k], 16)
            sp.wait_ge(S["wo_ps"], 3)
            for k in range(4, 6):
                sp.dma_start(*piece(0, k)).then_inc(s_w[k], 16)
            sp.wait_ge(S["h"], 3)
            sp.dma_start(g_row, I["norm_final_g"].rearrange("(a d) -> a d", a=1).broadcast_to([P, D])).then_inc(S["gfi"], 16)
            with sp.Fori(1, NEXP) as e:
                for k in range(6):
                    sp.wait_ge(S["wfree"], e * 6 + (k - 5))
                    sp.dma_start(*piece(e, k)).then_inc(s_w[k], 16)
            sp.wait_ge(S["yfin"], 3)
            sp.dma_start(O["y_p"][0].rearrange("(t p) d -> p t d", p=P), x[:, 0:2, :]).then_inc(S["out"], 16)
            sp.dma_start(O["y_s"].rearrange("b t d -> (b t) d"), x[0:NS, 2, :]).then_inc(S["out"], 16)
            sp.wait_ge(S["out"], 16 * 10)

        @block.gpsimd
        def _(pool):
            chain = [0]

            def link(ins):
                chain[0] += 1
                ins.then_inc(S["chain_p"], 1)
                pool.wait_ge(S["chain_p"], chain[0])

            tt = pool.tensor_tensor
            pool.wait_ge(S["exps"], 1)
            link(pool.tensor_copy(e_tab[:, 0, :, 0:1], prm[:, PA_C, :].unsqueeze(2)))
            link(pool.tensor_copy(e_tab[:, 1, :, 0:1], prm[:, PA_S, :].unsqueeze(2)))
            m = 1
            while m < HALF:
                re, im = e_tab[:, 0, :, 0:m], e_tab[:, 1, :, 0:m]
                cr = bc(e_tab[:, 0, :, m - 1:m], [P, NI, m])
                ci = bc(e_tab[:, 1, :, m - 1:m], [P, NI, m])
                t1, t2 = e_tmp[:, 0, :, 0:m], e_tmp[:, 1, :, 0:m]
                link(tt(t1, re, cr, ALU.mult))
                link(tt(t2, im, ci, ALU.mult))
                link(tt(e_tab[:, 0, :, m:2 * m], t1, t2, ALU.subtract))
                link(tt(t1, re, ci, ALU.mult))
                link(tt(t2, im, cr, ALU.mult))
                ins = tt(e_tab[:, 1, :, m:2 * m], t1, t2, ALU.add)
                m *= 2
                if m < HALF:
                    link(ins)
            ins.then_inc(S["etab"], 1)
            pool.wait_ge(S["etab"], 1)
            for i in range(NI):
                b = i % 2
                er, ei = e_tab[:, 0, i, :], e_tab[:, 1, i, :]
                pool.wait_ge(S["g1"], i + 1)
                if i >= 1:
                    pool.wait_ge(S["hhi"], i)
                if i >= 2:
                    pool.wait_ge(S["yps"], i - 1)
                gr, gi = ssm_g[:, b, 0, 1, :], ssm_g[:, b, 1, 1, :]
                tt(ssm_p[:, 0, :], gr, er, ALU.mult)
                tt(ssm_p[:, 1, :], gi, er, ALU.mult)
                tt(ssm_p[:, 2, :], gi, ei, ALU.mult)
                link(tt(ssm_p[:, 3, :], gr, ei, ALU.mult))
                tt(ssm_h[:, b, 0, HALF:], ssm_p[:, 0, :], ssm_p[:, 2, :], ALU.subtract)
                tt(ssm_h[:, b, 1, HALF:], ssm_p[:, 1, :], ssm_p[:, 3, :], ALU.add).then_inc(S["hhi"], 1)
                pool.wait_ge(S["hhi"], i + 1)
                ins = pool.tensor_copy(hf[:, :, i:i + 1], ssm_h[:, b, :, SEQ - 1:SEQ])
            ins.then_inc(S["hfin"], 1)

        @block.scalar
        def _(act):
            chain = [0]

            def link(ins):
                chain[0] += 1
                ins.then_inc(S["chain_a"], 1)
                act.wait_ge(S["chain_a"], chain[0])

            def small(dst, src):
                act.dma_start(dst, src).then_inc(S["prm"], 16)

            A = act.activation
            with nc.allow_non_contiguous_dma(reason="parameters of a few hundred words"):
                small(ld[0:NI, 0:2], I["ssm_log_dt"][0].rearrange("(i g) -> i g", g=2))
                small(par[0:NI, 0:P], I["ssm_a_re"][0].rearrange("(i g) n -> i (g n)", g=2))
                small(par[0:NI, P:2 * P], I["ssm_a_im"][0].rearrange("(i g) n -> i (g n)", g=2))
                small(gmx, I["norm_mix_g"][0].rearrange("(p j) -> p j", j=J))
                for r, nm in enumerate(("state_ssm_re", "state_ssm_im")):
                    small(h0row[:, r, :], I[nm][0].rearrange("b (i g) n -> (b i) (g n)", g=2))
                for r, nm in enumerate(("ssm_b_re", "ssm_b_im")):
                    small(bnat[:, r, :].rearrange("p (i c) -> p i c", i=NI), I[nm][0].rearrange("(i g) n c -> (g n) i c", g=2))
                for r, nm in enumerate(("ssm_c_re", "ssm_c_im")):
                    for dup in range(2):
                        small(cnat[:, r, :, 64 * dup:64 * dup + 64], I[nm][0].rearrange("g c n -> (g c) n").rearrange("(b p) n -> p b n", p=P))
                small(dsk, I["ssm_d"][0].rearrange("(b g) c -> (g c) b", g=8))
                small(bgl, I["b_glu"][0].rearrange("(b p) -> p b", p=P))
                small(gat, I["attn_out_norm_g"][0].rearrange("(b p) -> p b", p=P))
                small(gss, I["ssm_out_norm_g"][0].rearrange("(b p) -> p b", p=P))
                small(bro[:, :], I["b_router"].broadcast_to([P, NEXP]))
            act.wait_ge(S["prm"], 16 * NPRM)
            A(ld[0:NI, 0:2], ld[0:NI, 0:2], ACT.Exp).then_inc(S["dt"], 1)
            act.wait_ge(S["x"], 32)
            act.wait_ge(S["init"], 1)
            for t, (_, n) in enumerate(TILES):
                ins = A(xn[0:n, t, :], x[0:n, t, :], ACT.Square, accum_out=st[0:n, t:t + 1])
            ins.then_inc(S["ss"], 1)
            act.wait_ge(S["ms"], 1)
            A(st[:, 3:6], st[:, 3:6], ACT.Sqrt).then_inc(S["rt"], 1)
            act.wait_ge(S["red"], 1)
            A(prm[:, PA_R, :], prm[:, PA_RD, :], ACT.Exp)
            A(prm[:, PA_C, :], prm[:, 11, :], ACT.Sin)
            A(prm[:, PA_S, :], prm[:, 12, :], ACT.Sin).then_inc(S["exps"], 1)
            for n, j in enumerate(range(1, J, 2)):
                act.wait_ge(S["xT_ps"], j + 1)
                A(accT[:, j, :], ps[:, 4 + j % 4, 0:NTOK], ACT.Copy, scale=gmx[:, j:j + 1]).then_inc(S["xT_a"], 1)
            for n, c in enumerate([12, 13, 14, 15] + list(range(12))):
                act.wait_ge(S["proj"], n + 1)
                A(qkvu[:, c, :], ps[:, 4 + n % 2, 0:NTOK], ACT.Copy).then_inc(S["proj_ev"], 1)
            act.wait_ge(S["proj_ev"], 16)
            for g in range(2):
                rows = slice(64 * g, 64 * g + 64)
                ins = A(qbd[rows, :, :, 4 * g:4 * g + 4], qkvu[rows, 0:4, SEQ:].rearrange("p c (b t) -> p c b t", t=NSEQ), ACT.Copy)
            ins.then_inc(S["qbd"], 1)
            act.wait_ge(S["bu"], NI)
            for n in range(2):
                ins = A(bus.rearrange("p (k n c) -> p n k c", k=8, n=2)[:, n], ps[:, n, :].rearrange("p (k c) -> p k c", k=8), ACT.Copy)
            ins.then_inc(S["bus"], 1)
            for n in range(6):
                a, t = divmod(n, 3)
                rows = TILES[t][1]
                act.wait_ge(S["kvr_ps"], n + 1)
                A(kv_rows[0:rows, a, t, :], ps[0:rows, 4 + n % 2, :], ACT.Copy).then_inc(S["kvr"], 1)
            act.wait_ge(S["sto_ps"], 1)
            A(st_out[0:NI, 0:2, :], ps[0:NI, 5, 0:2 * P].rearrange("p (r n) -> p r n", r=2), ACT.Copy)
            A(st_out[:, 2:4, :], ps[:, 5, 2 * P:4 * P].rearrange("p (r n) -> p r n", r=2), ACT.Copy).then_inc(S["sto"], 1)
            for hh in range(H + 1):
                if hh < H:
                    b = hh % 2
                    act.wait_ge(S["nm"], hh + 1)
                    A(prb[:, b, 0:P], scb[:, b, 0:P], ACT.Exp, bias=st[:, 12 + 2 * b:13 + 2 * b], accum_out=st[:, 16 + 2 * b:17 + 2 * b])
                    A(prb[:, b, P:], scb[:, b, P:], ACT.Exp, bias=st[:, 13 + 2 * b:14 + 2 * b], accum_out=st[:, 17 + 2 * b:18 + 2 * b]).then_inc(S["ex"], 1)
                if hh >= 1:
                    b = (hh - 1) % 2
                    act.wait_ge(S["pt_ps"], hh)
                    A(ptb[:, b, :], ps[:, b, 0:3 * P], ACT.Copy).then_inc(S["pt"], 1)
            for half in range(2):
                for n in range(0, 20, 2):
                    act.wait_ge(S["kt_ps"], 20 * half + n + 1)
                    if half == 0 and n == 0:
                        act.wait_ge(S["o_ps"], H)
                    A(kT_s[:, 0, :], ps[:, 4, :], ACT.Copy).then_inc(S["ktA"], 1)
                act.wait_ge(S["st_ps"], half + 1)
                A(sT[:, 0:512], ps[:, 6, :], ACT.Copy)
                A(sT[:, 512:640], ps[:, 7, 0:P], ACT.Copy)
                A(sT[0:NS, 640:768], ps[0:NS, 7, P:2 * P], ACT.Copy).then_inc(S["stE"], 1)
                act.wait_ge(S["nms"], half + 1)
                A(p_s, s_s, ACT.Exp, bias=st[:, 24:25], accum_out=st[:, 25:26]).then_inc(S["exs"], 1)
                act.wait_ge(S["pts_ps"], half + 1)
                A(p_T[:, 0:512], ps[:, 6, :], ACT.Copy)
                A(p_T[:, 512:640], ps[:, 7, 0:P], ACT.Copy)
                A(p_T[0:NS, 640:768], ps[0:NS, 7, P:2 * P], ACT.Copy).then_inc(S["pts"], 1)
            act.wait_ge(S["gel1"], 1)
            A(kvg, kvg, ACT.Sigmoid, scale=G_A).then_inc(S["gel2"], 1)
            for b in range(4):
                act.wait_ge(S["glu_ps"], b + 1)
                A(kvg.rearrange("p (b t) -> p b t", b=4)[:, b, :], ps[:, 4 + b, 0:NTOK], ACT.Sigmoid, bias=bgl[:, b:b + 1]).then_inc(S["glu"], 1)
            act.wait_ge(S["aTs"], 2)
            act.wait_ge(S["sq"], 1)
            A(sqa, aT[:, :, :], ACT.Square).then_inc(S["sqA"], 1)
            act.wait_ge(S["ms2"], 1)
            A(st[:, 36:42], st[:, 36:42], ACT.Sqrt).then_inc(S["rt2"], 1)
            for t, (_, n) in enumerate(TILES):
                act.wait_ge(S["x2"], t + 1)
                ins = A(h[0:n, t, :], x[0:n, t, :], ACT.Square, accum_out=st[0:n, 48 + t:49 + t])
            ins.then_inc(S["ss3"], 1)
            act.wait_ge(S["ms3"], 1)
            A(st[:, 51:54], st[:, 51:54], ACT.Sqrt).then_inc(S["rt3"], 1)
            for j in range(1, J, 2):
                act.wait_ge(S["hT_ps"], j + 1)
                A(accT[:, j, :], ps[:, j, 0:NTOK], ACT.Copy).then_inc(S["xT_a"], 1)
            for t, (_, n) in enumerate(TILES):
                act.wait_ge(S["rout"], t + 1)
                A(top[0:n, t, 12:16], top[0:n, t, 8:12], ACT.Exp, accum_out=top[0:n, t, 20:21]).then_inc(S["gex"], 1)
            act.wait_ge(S["gT_ps"], 1)
            A(gT[:, :], ps[0:NEXP, 4, 0:NTOK], ACT.Copy).then_inc(S["gT"], 1)
            act.wait_ge(S["b1T_ps"], 1)
            for gl in range(2):
                for hf_ in range(2):
                    src = ps[:, 5, 256 * gl + 128 * hf_:256 * gl + 128 * hf_ + 128].rearrange("p (m e) -> p e m", m=4)
                    ins = A(b1T[:, :, 8 * hf_ + 4 * gl:8 * hf_ + 4 * gl + 4], src, ACT.Copy)
            ins.then_inc(S["b1T"], 1)
            for j in range(J):
                act.wait_ge(S["b2ps"], j + 1)
                A(accT[:, j, :], ps[:, 6 + j % 2, 0:NTOK], ACT.Copy).then_inc(S["acc0"], 1)

            def chunk(n, e, first, last):
                act.wait_ge(S["gath"], n + 1)
                A(xe, ps[:, 0, :].rearrange("p (j s) -> p j s", j=J), ACT.Copy).then_inc(S["xe"], 1)
                act.wait_ge(S["selT_ps"], n + 2)
                A(selT, ps[0:CAP, 4, 0:NTOK], ACT.Copy).then_inc(S["selT"], 1)
                for b in range(2):
                    act.wait_ge(S["glin"], n * 2 + (b + 1))
                    A(sig[:, b], act_in[:, b, 0], ACT.Sigmoid, scale=ALPHA).then_inc(S["sgm"], 1)
                act.wait_ge(S["mm2"], n + 1)
                A(yT, ps[:, 3, :], ACT.Copy).then_inc(S["yTr"], 1)
                act.wait_ge(S["y_ps"], n + 1)
                A(y.rearrange("p (a n) -> p a n", a=2), ps[0:CAP, 5:7, :], ACT.Copy).then_inc(S["yr"], 1)

            act.wait_ge(S["cntr"], 1)
            run_experts(act, chunk)

            for t, (_, n) in enumerate(TILES):
                act.wait_ge(S["x3"], t + 1)
                ins = A(h[0:n, t, :], x[0:n, t, :], ACT.Square, accum_out=st[0:n, 60 + t:61 + t])
            ins.then_inc(S["ss4"], 1)
            act.wait_ge(S["ms4"], 1)
            A(st[:, 63:66], st[:, 63:66], ACT.Sqrt).then_inc(S["rt4"], 1)

        @block.vector
        def _(dve):
            chain = [0]

            def link(ins):
                chain[0] += 1
                ins.then_inc(S["chain_v"], 1)
                dve.wait_ge(S["chain_v"], chain[0])

            tt, ts, stt = dve.tensor_tensor, dve.tensor_scalar, dve.scalar_tensor_tensor
            dve.memset(ones[:, :], 1.0)
            dve.memset(xb[:, :, :], 0.0)
            dve.memset(st[:, :], 1.0)
            dve.memset(qbd[:, :, :, :], 0.0).then_inc(S["init"], 1)
            dve.wait_ge(S["prm"], 16 * NPRM)
            dve.wait_ge(S["dt"], 1)
            dtb = bc(ld[0:NI, 0:2].unsqueeze(2), [NI, 2, 64])
            tt(st_out[0:NI, 0, :].rearrange("p (g n) -> p g n", g=2), par[0:NI, 0:P].rearrange("p (g n) -> p g n", g=2), dtb, ALU.mult)
            tt(st_out[0:NI, 1, :].rearrange("p (g n) -> p g n", g=2), par[0:NI, P:2 * P].rearrange("p (g n) -> p g n", g=2), dtb, ALU.mult).then_inc(S["rows"], 1)
            dve.wait_ge(S["ss"], 1)
            ts(st[:, 3:6], st[:, 0:3], 1.0 / D, EPS, ALU.mult, ALU.add).then_inc(S["ms"], 1)
            dve.wait_ge(S["rt"], 1)
            link(dve.reciprocal(st[:, 6:9], st[:, 3:6]))
            for t, (_, n) in enumerate(TILES):
                ins = ts(xn[0:n, t, :], x[0:n, t, :], st[0:n, 6 + t:7 + t], None, ALU.mult)
            ins.then_inc(S["xn"], 1)
            dve.wait_ge(S["prmT"], 1)
            link(dve.tensor_copy(prm[:, 0:4, :], ps[:, 0, 0:64].rearrange("p (a i) -> p a i", a=4)))
            link(ts(prm[:, 11, :], prm[:, PA_TH, :], TWO_PI / 4, None, ALU.add))
            link(dve.tensor_copy(prm[:, 12, :], prm[:, PA_TH, :]))
            two = prm[:, 11:13, :]
            kk = prm[:, 13:15, :]
            link(ts(kk, two, 1.0 / TWO_PI, ROUND, ALU.mult, ALU.add))
            link(ts(kk, kk, -ROUND, None, ALU.add))
            link(stt(two, kk, -TP_HI, two, ALU.mult, ALU.add))
            link(stt(two, kk, -TP_LO, two, ALU.mult, ALU.add))
            ts(two, two, PI_IN, -PI_IN, ALU.min, ALU.max).then_inc(S["red"], 1)
            link(dve.tensor_copy(h0[:, :, :], ps[:, 1, 0:2 * P].rearrange("p (r n) -> p r n", r=2)))
            gm4 = bc(gmask.unsqueeze(1), [P, 4, P])
            tt(cT[:, 0, :].rearrange("p (b n) -> p b n", b=4), ps[:, 2, :].rearrange("p (b n) -> p b n", b=4), gm4, ALU.mult)
            stt(cT[:, 1, :].rearrange("p (b n) -> p b n", b=4), ps[:, 3, :].rearrange("p (b n) -> p b n", b=4), -1.0, gm4, ALU.mult, ALU.mult).then_inc(S["crev"], 1)
            for j in range(0, J, 2):
                dve.wait_ge(S["xT_ps"], j + 1)
                ts(accT[:, j, :], ps[:, 4 + j % 4, 0:NTOK], gmx[:, j:j + 1], None, ALU.mult).then_inc(S["xT_d"], 1)
            dve.wait_ge(S["exps"], 1)
            q = lambda n: prm[:, n, :]
            tt(q(PA_AR), q(PA_R), q(PA_C), ALU.mult)
            link(tt(q(PA_AI), q(PA_R), q(PA_S), ALU.mult))
            ts(q(15), q(PA_AR), -1.0, None, ALU.add)
            tt(q(16), q(PA_LR), q(PA_LR), ALU.mult)
            link(tt(q(17), q(PA_LI), q(PA_LI), ALU.mult))
            link(tt(q(16), q(16), q(17), ALU.add))
            dve.reciprocal(q(16), q(16))
            tt(q(18), q(15), q(PA_LR), ALU.mult)
            tt(q(19), q(PA_AI), q(PA_LI), ALU.mult)
            tt(q(20), q(PA_AI), q(PA_LR), ALU.mult)
            link(tt(q(21), q(15), q(PA_LI), ALU.mult))
            tt(q(18), q(18), q(19), ALU.add)
            link(tt(q(20), q(20), q(21), ALU.subtract))
            tt(q(PA_FR), q(18), q(16), ALU.mult)
            link(tt(q(PA_FI), q(20), q(16), ALU.mult))
            v3 = lambda r: bnat[:, r, :].rearrange("p (i c) -> p i c", i=NI)
            fr, fi = (bc(q(n).unsqueeze(2), [P, NI, 16]) for n in (PA_FR, PA_FI))
            s3 = lambda n: ssm_a[:, 2 * n:2 * n + 2, :].rearrange("p a t -> p (a t)").rearrange("p (i c) -> p i c", i=NI)
            s4 = lambda n: ssm_b[:, 2 * n:2 * n + 2, :].rearrange("p a t -> p (a t)").rearrange("p (i c) -> p i c", i=NI)
            tt(s3(0), v3(0), fr, ALU.mult)
            tt(s3(1), v3(1), fi, ALU.mult)
            tt(s4(0), v3(1), fr, ALU.mult)
            link(tt(s4(1), v3(0), fi, ALU.mult))
            for g in range(2):
                rows = slice(64 * g, 64 * g + 64)
                dst = lambda r: xb[rows, r, :].rearrange("p (i g c) -> p i g c", i=NI, g=2)[:, :, g, :]
                tt(dst(0), s3(0)[rows], s3(1)[rows], ALU.subtract)
                ins = tt(dst(1), s4(0)[rows], s4(1)[rows], ALU.add)
            ins.then_inc(S["fdone"], 1)
            dve.wait_ge(S["bT_ps"], 1)
            dve.tensor_copy(bT[:, 0, :], ps[:, 0, :])
            dve.tensor_copy(bT[:, 1, :], ps[:, 1, :]).then_inc(S["bT"], 1)
            dve.wait_ge(S["etab"], 1)
            for i in range(NI):
                b = i % 2
                er, ei = e_tab[:, 0, i, :], e_tab[:, 1, i, :]
                buf = ps[:, 6 + b, :].rearrange("p (r t) -> p r t", r=4)
                dve.wait_ge(S["bu"], i + 1)
                if i >= 1:
                    dve.wait_ge(S["g1"], i)
                tt(ssm_a[:, :, :], buf, bc(er.unsqueeze(1), [P, 4, HALF]), ALU.mult)
                tt(ssm_b[:, 0:2, :], buf[:, 2:4, :], bc(ei.unsqueeze(1), [P, 2, HALF]), ALU.mult)
                tt(ssm_b[:, 2:4, :], buf[:, 0:2, :], bc(ei.unsqueeze(1), [P, 2, HALF]), ALU.mult).then_inc(S["bu_used"], 1)
                dve.wait_ge(S["bu_used"], i + 1)
                tt(ssm_a[:, 0:2, :], ssm_a[:, 0:2, :], ssm_b[:, 0:2, :], ALU.add)
                link(tt(ssm_a[:, 2:4, :], ssm_a[:, 2:4, :], ssm_b[:, 2:4, :], ALU.subtract))
                decay = bc(prm[:, PA_R, i:i + 1], [P, HALF])
                if i >= 2:
                    dve.wait_ge(S["hhi"], i - 1)
                    dve.wait_ge(S["yps"], i - 1)
                dve.tensor_tensor_scan(ssm_g[:, b, 0, 0, :], decay, ssm_a[:, 0, :], 0.0, ALU.mult, ALU.add)
                link(dve.tensor_tensor_scan(ssm_g[:, b, 1, 0, :], decay, ssm_a[:, 2, :], 0.0, ALU.mult, ALU.add))
                gr, gi = ssm_g[:, b, 0, 0, :], ssm_g[:, b, 1, 0, :]
                tt(ssm_b[:, 0, :], gr, er, ALU.mult)
                tt(ssm_b[:, 1, :], gi, er, ALU.mult)
                tt(ssm_b[:, 2, :], gi, ei, ALU.mult)
                link(tt(ssm_b[:, 3, :], gr, ei, ALU.mult))
                tt(ssm_h[:, b, 0, 0:HALF], ssm_b[:, 0, :], ssm_b[:, 2, :], ALU.subtract)
                tt(ssm_h[:, b, 1, 0:HALF], ssm_b[:, 1, :], ssm_b[:, 3, :], ALU.add).then_inc(S["hlo"], 1)
                dve.wait_ge(S["hlo"], i + 1)
                dve.tensor_tensor_scan(ssm_g[:, b, 0, 1, :], decay, ssm_a[:, 1, :], ssm_h[:, b, 0, HALF - 1:HALF], ALU.mult, ALU.add)
                dve.tensor_tensor_scan(ssm_g[:, b, 1, 1, :], decay, ssm_a[:, 3, :], ssm_h[:, b, 1, HALF - 1:HALF], ALU.mult, ALU.add).then_inc(S["g1"], 1)
                if i % 4 == 1 and i >= 4:
                    blk = i // 4 - 1
                    dve.wait_ge(S["yps"], 4 * (blk + 1))
                    stt(yS[:, blk, 0:SEQ], qkvu[:, 12 + blk, 0:SEQ], dsk[:, blk:blk + 1], ps[:, 2 + blk % 2, 0:SEQ], ALU.mult, ALU.add).then_inc(S["yS_ready"], 1)
            dve.wait_ge(S["bus"], 1)
            dve.wait_ge(S["g1"], NI)
            ar, ai = (bc(prm[:, n, :].unsqueeze(2), [P, NI, NB]) for n in (PA_AR, PA_AI))
            hv = hs[:, :, :, :].rearrange("p r i (b t) -> p r i b t", t=NSEQ)
            buv = bus.rearrange("p (i r b t) -> p r i b t", i=NI, r=2, t=NSEQ)
            h0v = h0[:, :, :].rearrange("p r (b i) -> p r i b", b=NB)
            tq = lambda n: (ssm_a, ssm_b)[n // 4][:, n % 4, :].rearrange("p (i b) -> p i b", i=NI)
            for t in range(NSEQ):
                pr, pi = (h0v[:, 0], h0v[:, 1]) if t == 0 else (hv[:, 0, :, :, t - 1], hv[:, 1, :, :, t - 1])
                tt(tq(0), pr, ar, ALU.mult)
                tt(tq(1), pi, ai, ALU.mult)
                tt(tq(2), pi, ar, ALU.mult)
                link(tt(tq(3), pr, ai, ALU.mult))
                tt(tq(4), tq(0), tq(1), ALU.subtract)
                link(tt(tq(5), tq(2), tq(3), ALU.add))
                tt(hv[:, 0, :, :, t], tq(4), buv[:, 0, :, :, t], ALU.add)
                link(tt(hv[:, 1, :, :, t], tq(5), buv[:, 1, :, :, t], ALU.add))
            dve.tensor_copy(sf[:, :, :].rearrange("p r (b i) -> p r i b", b=NB), hv[:, :, :, :, NSEQ - 1]).then_inc(S["hs"], 1)
            dve.wait_ge(S["yps"], NI)
            stt(yS[:, 3, 0:SEQ], qkvu[:, 15, 0:SEQ], dsk[:, 3:4], ps[:, 3, 0:SEQ], ALU.mult, ALU.add).then_inc(S["yS_ready"], 1)
            dve.wait_ge(S["ysps"], 1)
            for blk in range(4):
                ins = stt(yS[:, blk, SEQ:], qkvu[:, 12 + blk, SEQ:], dsk[:, blk:blk + 1], ps[:, 4, NS * blk:NS * blk + NS], ALU.mult, ALU.add)
            ins.then_inc(S["ysv"], 1)
            for hh in range(H + 1):
                if hh < H:
                    b = hh % 2
                    dve.wait_ge(S["s_ps"], hh + 1)
                    link(stt(scb[:, b, :], ps[:, 6 + b, 0:3 * P], SCALE, con[:, C_BP:C_BP + 3 * P], ALU.mult, ALU.add))
                    dve.tensor_reduce(st[:, 10:11], scb[:, b, 0:P], AX, ALU.max)
                    link(dve.tensor_reduce(st[:, 11:12], scb[:, b, P:], AX, ALU.max))
                    ts(st[:, 12 + 2 * b:14 + 2 * b], st[:, 10:12], -1.0, None, ALU.mult).then_inc(S["nm"], 1)
                if hh >= 1:
                    b = (hh - 1) % 2
                    dve.wait_ge(S["ex"], hh)
                    link(dve.reciprocal(st[:, 20 + 2 * b:22 + 2 * b], st[:, 16 + 2 * b:18 + 2 * b]))
                    ts(prb[:, b, 0:P], prb[:, b, 0:P], st[:, 20 + 2 * b:21 + 2 * b], None, ALU.mult)
                    ts(prb[:, b, P:], prb[:, b, P:], st[:, 21 + 2 * b:22 + 2 * b], None, ALU.mult).then_inc(S["pn"], 1)
                    if (hh - 1) % 2 == 1:
                        hp = (hh - 1) // 2
                        dve.wait_ge(S["o_ps"], hh)
                        dve.tensor_copy(aT[:, hp, 0:SEQ], ps[:, 2 + hp % 2, 0:SEQ]).then_inc(S["aT"], 1)
            for half in range(2):
                for n in range(1, 20, 2):
                    dve.wait_ge(S["kt_ps"], 20 * half + n + 1)
                    dve.tensor_copy(kT_s[:, 1, :], ps[:, 5, :]).then_inc(S["ktD"], 1)
                dve.wait_ge(S["ts_ps"], half + 1)
                stt(s_s[:, 0:512], ps[:, 0, :], SCALE, con[:, C_BS:C_BS + 512], ALU.mult, ALU.add)
                at = C_BS + 512 + 160 * half
                link(stt(s_s[:, 512:672], ps[:, 1, 0:160], SCALE, con[:, at:at + 160], ALU.mult, ALU.add))
                link(dve.tensor_reduce(st[:, 23:24], s_s, AX, ALU.max))
                ts(st[:, 24:25], st[:, 23:24], -1.0, None, ALU.mult).then_inc(S["nms"], 1)
                dve.wait_ge(S["exs"], half + 1)
                link(dve.reciprocal(st[:, 26:27], st[:, 25:26]))
                ts(p_s, p_s, st[:, 26:27], None, ALU.mult).then_inc(S["pns"], 1)
            dve.wait_ge(S["pv"], 2)
            pv = ps[:, 3, 0:NB * 32].rearrange("p (b c g t) -> p c b g t", b=NB, c=4, g=2)
            for g in range(2):
                rows = slice(64 * g, 64 * g + 64)
                dst = aT[rows, :, SEQ:].rearrange("p c (b t) -> p c b t", t=NSEQ)
                dve.tensor_copy(dst, pv[rows, :, :, g, :]).then_inc(S["aTs"], 1)
            yf = yS[:, :, :].rearrange("p a t -> p (a t)")
            link(tt(kvg, yf, yf, ALU.mult))
            link(ts(kvg, kvg, G_B, 1.0, ALU.mult, ALU.add))
            tt(kvg, kvg, yf, ALU.mult).then_inc(S["gel1"], 1)
            dve.wait_ge(S["gel2"], 1)
            tt(yf, yf, kvg, ALU.mult).then_inc(S["gg"], 1)
            for b in range(4):
                dve.wait_ge(S["glu"], b + 1)
                if b == 0:
                    dve.wait_ge(S["glu_ps"], 4)
                ins = tt(yS[:, b, :], yS[:, b, :], kvg.rearrange("p (b t) -> p b t", b=4)[:, b, :], ALU.mult)
            link(ins)
            tt(sqs, yS[:, :, :], yS[:, :, :], ALU.mult).then_inc(S["sq"], 1)
            dve.wait_ge(S["sqA"], 1)
            dve.wait_ge(S["sq"], 1)
            tt(aT[:, :, :], aT[:, :, :], bc(gat.unsqueeze(2), [P, 4, NTOK]), ALU.mult)
            tt(yS[:, :, :], yS[:, :, :], bc(gss.unsqueeze(2), [P, 4, NTOK]), ALU.mult).then_inc(S["mix"], 1)
            dve.wait_ge(S["ssq"], 1)
            for t, (_, n) in enumerate(TILES):
                ins = ts(st[0:n, 36 + 2 * t:38 + 2 * t], ps[0:n, 0, 2 * t:2 * t + 2], 1.0 / 512, EPS, ALU.mult, ALU.add)
            ins.then_inc(S["ms2"], 1)
            dve.wait_ge(S["rt2"], 1)
            link(dve.reciprocal(st[:, 42:48], st[:, 36:42]))
            for t, (_, n) in enumerate(TILES):
                dve.wait_ge(S["wo_ps"], t + 1)
                b0 = 4 * (t % 2)
                xv = x[0:n, t, :].rearrange("p (a n) -> p a n", a=2)
                link(stt(xv, ps[0:n, b0:b0 + 2, :], st[0:n, 42 + 2 * t:43 + 2 * t], xv, ALU.mult, ALU.add))
                stt(xv, ps[0:n, b0 + 2:b0 + 4, :], st[0:n, 43 + 2 * t:44 + 2 * t], xv, ALU.mult, ALU.add).then_inc(S["x2"], 1)
            dve.wait_ge(S["ss3"], 1)
            ts(st[:, 51:54], st[:, 48:51], 1.0 / D, EPS, ALU.mult, ALU.add).then_inc(S["ms3"], 1)
            dve.wait_ge(S["rt3"], 1)
            dve.wait_ge(S["gff"], 16)
            link(dve.reciprocal(st[:, 54:57], st[:, 51:54]))
            for t, (_, n) in enumerate(TILES):
                stt(h[0:n, t, :], x[0:n, t, :], st[0:n, 54 + t:55 + t], g_row[0:n, :], ALU.mult, ALU.mult).then_inc(S["h"], 1)
            for j in range(0, J, 2):
                dve.wait_ge(S["hT_ps"], j + 1)
                dve.tensor_copy(accT[:, j, :], ps[:, j, 0:NTOK]).then_inc(S["xT_d"], 1)
            dve.memset(posm, -1.0)
            dve.memset(gate, 0.0)
            link(dve.memset(rt_s[:, :, :, :], 0.0))
            for t, (_, n) in enumerate(TILES):
                dve.wait_ge(S["lg"], 3)
                lg, msk, gt, t8 = rt_s[0:n, t, 0, :], rt_s[0:n, t, 1, :], rt_s[0:n, t, 2, :], top[0:n, t, 0:8]
                link(tt(lg, ps[0:n, 0, 32 * t:32 * t + 32], bro[0:n, :], ALU.add))
                link(dve.max(t8, lg))
                dve.max_index(tidx[0:n, t, :], t8, lg)
                link(ts(top[0:n, t, 8:12], t8[:, 0:4], t8[:, 0:1], None, ALU.subtract))
                dve.tensor_copy(top[0:n, t, 16:20], tidx[0:n, t, 0:4]).then_inc(S["rout"], 1)
            for t, (_, n) in enumerate(TILES):
                dve.wait_ge(S["gex"], t + 1)
                link(dve.reciprocal(top[0:n, t, 21:22], top[0:n, t, 20:21]))
                link(ts(top[0:n, t, 12:16], top[0:n, t, 12:16], top[0:n, t, 21:22], None, ALU.mult))
                o1, o2 = oh[0:n, t, 0], oh[0:n, t, 1]
                link(tt(o1, bc(iota[0:n, 0:NEXP].unsqueeze(1), [n, TOPK, NEXP]), bc(top[0:n, t, 16:20].unsqueeze(2), [n, TOPK, NEXP]), ALU.is_equal))
                link(tt(o2, o1, bc(top[0:n, t, 12:16].unsqueeze(2), [n, TOPK, NEXP]), ALU.mult))
                dve.tensor_reduce(rt_s[0:n, t, 1, :], o1.rearrange("p k e -> p e k"), AX, ALU.add)
                link(dve.tensor_reduce(rt_s[0:n, t, 2, :], o2.rearrange("p k e -> p e k"), AX, ALU.add))
                dve.tensor_copy(gate[0:n, :, t], rt_s[0:n, t, 2, :]).then_inc(S["posm"], 1)
            dve.wait_ge(S["posps"], 1)
            for t, (_, n) in enumerate(TILES):
                link(stt(rt_s[0:n, t, 3, :], ps[0:n, 1, 32 * t:32 * t + 32], 1.0, rt_s[0:n, t, 1, :], ALU.add, ALU.mult))
                link(ts(posm[0:n, :, t], rt_s[0:n, t, 3, :], -1.0, None, ALU.add))
            dve.memset(y, 0.0).then_inc(S["yr"], 1)
            dve.memset(selT, 0.0).then_inc(S["selT"], 1)
            dve.tensor_copy(cnt[:, :], ps[:, 1, 96:128]).then_inc(S["cntr"], 1)

            def add_back(n):
                for j in range(J):
                    dve.wait_ge(S["comb"], n * J + (j + 1))
                    tt(accT[:, j, :], accT[:, j, :], ps[:, 5 + j % 2, 0:NTOK], ALU.add).then_inc(S["acc"], 1)

            def chunk(n, e, first, last):
                dve.wait_ge(S["selT_ps"], n + 1)
                ib = bc(iota[:, bass.ds(first, CAP)].unsqueeze(1), [P, 3, CAP])
                pb = bc(posm[:, bass.ds(e, 1), :].rearrange("p e t -> p (e t)").unsqueeze(2), [P, 3, CAP])
                gb = bc(gate[:, bass.ds(e, 1), :].rearrange("p e t -> p (e t)").unsqueeze(2), [P, 3, CAP])
                tt(sel, ib, pb, ALU.is_equal).then_inc(S["sel"], 1)
                dve.wait_ge(S["sel"], n * 2 + 1)
                tt(selg, sel, gb, ALU.mult).then_inc(S["sel"], 1)
                add_back(n)
                for b in range(2):
                    dve.wait_ge(S["mm1"], n * 2 + (b + 1))
                    bb = bc(b1T[:, bass.ds(e, 1), 8 * b:8 * b + 8].rearrange("p e m -> p (e m)").unsqueeze(2), [P, 8, CAP])
                    av = act_in[:, b].rearrange("p g m s -> p (g m) s")
                    tt(av, ps[:, 1 + b, :].rearrange("p (m s) -> p m s", m=8), bb, ALU.add).then_inc(S["swc"], 1)
                    dve.wait_ge(S["swc"], n * 4 + (1 + 2 * b))
                    ts(act_in[:, b, 0], act_in[:, b, 0], LIMIT, None, ALU.min).then_inc(S["glin"], 1)
                    ts(act_in[:, b, 1], act_in[:, b, 1], LIMIT, -LIMIT, ALU.min, ALU.max)
                    dve.wait_ge(S["sgm"], n * 2 + (b + 1))
                    tt(sig[:, b], sig[:, b], act_in[:, b, 0], ALU.mult).then_inc(S["swc"], 1)
                    dve.wait_ge(S["swc"], n * 4 + (2 + 2 * b))
                    stt(mid[:, b], act_in[:, b, 1], 1.0, sig[:, b], ALU.add, ALU.mult).then_inc(S["midr"], 1)

            dve.wait_ge(S["cntr"], 1)
            dve.wait_ge(S["acc0"], J)
            dve.wait_ge(S["b1T"], 1)
            total = run_experts(dve, chunk)
            add_back(total)
            for t, (_, n) in enumerate(TILES):
                dve.wait_ge(S["fin_ps"], t + 1)
                xv = x[0:n, t, :].rearrange("p (a n) -> p a n", a=2)
                b0 = 2 * t
                tt(xv, xv, ps[0:n, b0:b0 + 2, :], ALU.add).then_inc(S["x3"], 1)
            dve.wait_ge(S["ss4"], 1)
            ts(st[:, 63:66], st[:, 60:63], 1.0 / D, EPS, ALU.mult, ALU.add).then_inc(S["ms4"], 1)
            dve.wait_ge(S["rt4"], 1)
            dve.wait_ge(S["gfi"], 16)
            dve.reciprocal(st[:, 66:69], st[:, 63:66]).then_inc(S["ms4"], 1)
            dve.wait_ge(S["ms4"], 2)
            for t, (_, n) in enumerate(TILES):
                stt(x[0:n, t, :], x[0:n, t, :], st[0:n, 66 + t:67 + t], g_row[0:n, :], ALU.mult, ALU.mult).then_inc(S["yfin"], 1)

        @block.tensor
        def _(pe):
            mm, tp = pe.matmul, pe.transpose

            pe.wait_ge(S["con"], 16)
            pe.wait_ge(S["prm"], 16 * NPRM)
            for r in range(2):
                for b in range(4):
                    tp(ps[:, 2 + r, P * b:P * b + P], cnat[:, r, b, :], ident)
                tp(ps[:, 1, P * r:P * r + P], h0row[:, r, :], ident)
            pe.wait_ge(S["rows"], 1)
            for a, src in enumerate((par[0:NI, 0:P], par[0:NI, P:2 * P], st_out[0:NI, 0, :], st_out[0:NI, 1, :])):
                ins = tp(ps[:, 0, NI * a:NI * a + NI], src, ident[0:NI, 0:NI])
            ins.then_inc(S["prmT"], 1)
            pe.wait_ge(S["xn"], 1)
            for j in range(J):
                if j >= 4:
                    pe.wait_ge(S["xT_a"] if j % 2 else S["xT_d"], j // 2 - 1)
                for t, (t0, n) in enumerate(TILES):
                    ins = tp(ps[:, 4 + j % 4, t0:t0 + n], xn[0:n, t, j::J], ident[0:n, 0:n])
                ins.then_inc(S["xT_ps"], 1)
            blocks = [12, 13, 14, 15] + list(range(12))

            def project(n):
                c = blocks[n]
                if n == 0:
                    pe.wait_ge(S["win0"], 16)
                    pe.wait_ge(S["xT_a"], 4)
                    pe.wait_ge(S["xT_d"], 4)
                if n == 4:
                    pe.wait_ge(S["win1"], 48)
                if n >= 2:
                    pe.wait_ge(S["proj_ev"], n - 1)
                for j in range(J):
                    ins = mm(ps[:, 4 + n % 2, 0:NTOK], w_in[:, c // 4, j, P * (c % 4):P * (c % 4) + P], accT[:, j, :],
                             start=(j == 0), stop=(j == J - 1))
                ins.then_inc(S["proj"], 1)

            for n in range(4):
                project(n)
            pe.wait_ge(S["crev"], 1)
            pe.wait_ge(S["fdone"], 1)
            for r in range(2):
                for b in range(4):
                    ins = tp(ps[:, r, P * b:P * b + P], xb[:, r, P * b:P * b + P], ident)
            ins.then_inc(S["bT_ps"], 1)
            pe.wait_ge(S["bT"], 1)
            pe.wait_ge(S["proj_ev"], 4)

            def bu(i):
                rows = slice(32 * (i % 4), 32 * (i % 4) + 32)
                blk = i // 4
                if i >= 2:
                    pe.wait_ge(S["bu_used"], i - 1)
                for r in range(2):
                    w = bT[rows, r, P * blk:P * blk + P]
                    at = 64 * (i // 2) + NS * r
                    mm(ps[:, i % 2, at:at + NS], w, qkvu[rows, 12 + blk, SEQ:], start=True, stop=True)
                    ins = mm(ps[:, 6 + i % 2, SEQ * r:SEQ * r + SEQ], w, qkvu[rows, 12 + blk, 0:SEQ], start=True, stop=True)
                ins.then_inc(S["bu"], 1)

            def c_h(i):
                blk, q = i // 4, 32 * (i % 4)
                if blk >= 2 and i % 4 == 0:
                    pe.wait_ge(S["yS_ready"], blk - 1)
                pe.wait_ge(S["hlo"], i + 1)
                pe.wait_ge(S["hhi"], i + 1)
                for r in range(2):
                    ins = mm(ps[q:q + 32, 2 + blk % 2, 0:SEQ], cT[:, r, P * blk + q:P * blk + q + 32], ssm_h[:, i % 2, r, :],
                             start=(r == 0), stop=(r == 1), skip_group_check=True)
                ins.then_inc(S["yps"], 1)

            for i in range(NI):
                bu(i)
                if i < 12:
                    project(4 + i)
                if i >= 1:
                    c_h(i - 1)
            c_h(NI - 1)

            pe.wait_ge(S["proj_ev"], 16)
            for n in range(6):
                a, t = divmod(n, 3)
                t0, rows = TILES[t]
                if n >= 2:
                    pe.wait_ge(S["kvr"], n - 1)
                for b in range(4):
                    ins = tp(ps[0:rows, 4 + n % 2, P * b:P * b + P], qkvu[:, 4 + 4 * a + b, t0:t0 + rows], ident)
                ins.then_inc(S["kvr_ps"], 1)
            pe.wait_ge(S["kvr"], 6)

            pe.wait_ge(S["hs"], 1)
            pe.wait_ge(S["hfin"], 1)
            for i in range(NI):
                blk, q = i // 4, 32 * (i % 4)
                for r in range(2):
                    ins = mm(ps[q:q + 32, 4, NS * blk:NS * blk + NS], cT[:, r, P * blk + q:P * blk + q + 32], hs[:, r, i, :],
                             start=(r == 0), stop=(r == 1), skip_group_check=True)
            ins.then_inc(S["ysps"], 1)
            for r in range(2):
                tp(ps[0:NI, 5, P * r:P * r + P], hf[:, r, :], ident)
                ins = tp(ps[:, 5, SEQ + P * r:SEQ + P * r + P], sf[:, r, :], ident)
            ins.then_inc(S["sto_ps"], 1)

            pe.wait_ge(S["bu_used"], NI)
            pe.wait_ge(S["bus"], 1)
            for hh in range(H + 1):
                if hh < H:
                    b, hp, rows = hh % 2, hh // 2, slice(64 * (hh % 2), 64 * (hh % 2) + 64)
                    if hh >= 2:
                        pe.wait_ge(S["nm"], hh - 1)
                    mm(ps[:, 6 + b, 0:P], qkvu[rows, hp, 0:P], qkvu[rows, 4 + hp, 0:P], start=True, stop=True)
                    mm(ps[:, 6 + b, P:3 * P], qkvu[rows, hp, P:SEQ], qkvu[rows, 4 + hp, 0:SEQ], start=True, stop=True).then_inc(S["s_ps"], 1)
                if hh >= 1:
                    g = hh - 1
                    b, hp, rows = g % 2, g // 2, slice(64 * (g % 2), 64 * (g % 2) + 64)
                    pe.wait_ge(S["pn"], g + 1)
                    tp(ps[:, b, 0:P], prb[:, b, 0:P], ident)
                    tp(ps[:, b, P:2 * P], prb[:, b, P:2 * P], ident)
                    tp(ps[:, b, 2 * P:3 * P], prb[:, b, 2 * P:3 * P], ident).then_inc(S["pt_ps"], 1)
                    pe.wait_ge(S["pt"], g + 1)
                    if g == 0:
                        pe.wait_ge(S["yS_ready"], 4)
                    if g >= 4 and g % 2 == 0:
                        pe.wait_ge(S["aT"], hp - 1)
                    mm(ps[rows, 2 + hp % 2, 0:SEQ], kv_rows[:, 1, 0, 64 * g:64 * g + 64], ptb[:, b, 0:SEQ], start=True, stop=False, skip_group_check=True)
                    mm(ps[rows, 2 + hp % 2, P:SEQ], kv_rows[:, 1, 1, 64 * g:64 * g + 64], ptb[:, b, SEQ:], start=False, stop=True, skip_group_check=True).then_inc(S["o_ps"], 1)
            pe.wait_ge(S["aT"], 4)
            pe.wait_ge(S["qbd"], 1)
            pe.wait_ge(S["ysv"], 1)
            pe.wait_ge(S["sto"], 1)

            for half in range(2):
                def keys(n):
                    b4, rt = divmod(n, 5)
                    m = 20 * half + n
                    b = 4 * half + b4
                    if rt == 0:
                        pe.wait_ge(S[f"kload{b % 2}"], 80 * (b // 2 + 1))
                    if m >= 2:
                        pe.wait_ge(S["ktD"] if n % 2 else S["ktA"], m // 2)
                    for hp in range(4):
                        ins = tp(ps[:, 4 + n % 2, P * hp:P * hp + P], k_cache[:, b % 2, 512 * rt + P * hp:512 * rt + P * hp + P], ident)
                    ins.then_inc(S["kt_ps"], 1)

                keys(0)
                for n in range(20):
                    if n + 1 < 20:
                        keys(n + 1)
                    b4, rt = divmod(n, 5)
                    pe.wait_ge(S["ktD"] if n % 2 else S["ktA"], 10 * half + n // 2 + 1)
                    if n == 0 and half == 1:
                        pe.wait_ge(S["pts"], 1)
                    for hp in range(4):
                        at = P * (rt % 4) + 32 * b4 + 8 * hp
                        mm(ps[:, 6 + rt // 4, at:at + 8], kT_s[:, n % 2, P * hp:P * hp + P], qbd[:, hp, 4 * half + b4, :], start=True, stop=True)
                for hp in range(4):
                    dst = ps[0:NS, 7, P:2 * P].rearrange("p (b c n) -> p b c n", b=4, c=4)[:, :, hp, :]
                    ins = mm(dst, qkvu[:, 4 + hp, SEQ:], qbd[:, hp, 4 * half:4 * half + 4, :], start=True, stop=True)
                ins.then_inc(S["st_ps"], 1)
                pe.wait_ge(S["stE"], half + 1)
                for rt in range(5):
                    tp(ps[:, rt // 4, P * (rt % 4):P * (rt % 4) + P], sT[:, P * rt:P * rt + P], ident)
                tp(ps[:, 1, P:P + NS], sT[0:NS, 640:768], ident[0:NS, 0:NS]).then_inc(S["ts_ps"], 1)
                pe.wait_ge(S["pns"], half + 1)
                for rt in range(5):
                    tp(ps[:, 6 + rt // 4, P * (rt % 4):P * (rt % 4) + P], p_s[:, P * rt:P * rt + P], ident)
                tp(ps[0:NS, 7, P:2 * P], p_s[:, 640:672], ident).then_inc(S["pts_ps"], 1)
                pe.wait_ge(S["pts"], half + 1)
                for b4 in range(4):
                    pe.wait_ge(S[f"vload{b4}"], 80 * (half + 1))
                    for hp in range(4):
                        c0 = 32 * b4 + 8 * hp
                        dst = ps[:, 3, 128 * half + c0:128 * half + c0 + 8]
                        for rt in range(5):
                            mm(dst, v_cache[:, b4, 512 * rt + P * hp:512 * rt + P * hp + P], p_T[:, P * rt + c0:P * rt + c0 + 8],
                               start=(rt == 0), stop=False)
                        ins = mm(dst, kv_rows[0:NS, 1, 2, P * hp:P * hp + P], p_T[0:NS, 640 + c0:640 + c0 + 8], start=False, stop=True)
                ins.then_inc(S["pv"], 1)
            pe.wait_ge(S["wglu"], 32)
            pe.wait_ge(S["gg"], 1)
            for ob in range(4):
                for kb in range(4):
                    ins = mm(ps[:, 4 + ob, 0:NTOK], w_glu[:, kb, P * ob:P * ob + P], yS[:, kb, :], start=(kb == 0), stop=(kb == 3))
                ins.then_inc(S["glu_ps"], 1)
            pe.wait_ge(S["sto"], 1)
            pe.wait_ge(S["sqA"], 1)
            for t, (t0, n) in enumerate(TILES):
                for a, sq in enumerate((sqa, sqs)):
                    for kb in range(4):
                        ins = mm(ps[0:n, 0, 2 * t + a:2 * t + a + 1], sq[:, kb, t0:t0 + n], ones[:, 0:1], start=(kb == 0), stop=(kb == 3))
            ins.then_inc(S["ssq"], 1)
            pe.wait_ge(S["wout"], 16)
            pe.wait_ge(S["mix"], 1)
            pe.wait_ge(S["ms2"], 1)
            for t, (t0, n) in enumerate(TILES):
                b0 = 4 * (t % 2)
                if t == 2:
                    pe.wait_ge(S["x2"], 1)
                for a, src in enumerate((aT, yS)):
                    for kb in range(4):
                        for c in range(2):
                            ins = mm(ps[0:n, b0 + 2 * a + c, :], src[:, kb, t0:t0 + n], w_out[:, 4 * a + kb, 512 * c:512 * c + 512],
                                     start=(kb == 0), stop=(kb == 3))
                ins.then_inc(S["wo_ps"], 1)
            pe.wait_ge(S["h"], 3)
            for j in range(J):
                for t, (t0, n) in enumerate(TILES):
                    ins = tp(ps[:, j, t0:t0 + n], h[0:n, t, j::J], ident[0:n, 0:n])
                ins.then_inc(S["hT_ps"], 1)
            pe.wait_ge(S["xT_a"], 8)
            pe.wait_ge(S["xT_d"], 8)
            for t, (t0, n) in enumerate(TILES):
                for j in range(J):
                    ins = mm(ps[0:n, 0, 32 * t:32 * t + 32], accT[:, j, t0:t0 + n], wr[:, j, :], start=(j == 0), stop=(j == J - 1))
                ins.then_inc(S["lg"], 1)
            pe.wait_ge(S["b1"], 32)
            for m in range(16):
                ins = tp(ps[:, 5, 32 * m:32 * m + 32], b1_rows[:, P * m:P * m + P], ident[0:NEXP, 0:NEXP])
            ins.then_inc(S["b1T_ps"], 1)
            pe.wait_ge(S["posm"], 3)
            for t, (t0, n) in enumerate(TILES):
                for u in range(t + 1):
                    m = TILES[u][1]
                    w = tri[0:m, 0:n] if u == t else ones[0:m, 0:n]
                    mm(ps[0:n, 1, 32 * t:32 * t + 32], w, rt_s[0:m, u, 1, :], start=(u == 0), stop=(u == t))
            for u in range(3):
                m = TILES[u][1]
                ins = mm(ps[:, 1, 96:128], ones[0:m, :], rt_s[0:m, u, 1, :], start=(u == 0), stop=(u == 2))
                if u == 0:
                    ins.then_inc(S["selT_ps"], 1)
            ins.then_inc(S["posps"], 1)
            for t, (t0, n) in enumerate(TILES):
                ins = tp(ps[0:NEXP, 4, t0:t0 + n], rt_s[0:n, t, 2, :], ident[0:n, 0:n])
            ins.then_inc(S["gT_ps"], 1)
            pe.wait_ge(S["gT"], 1)
            for j in range(J):
                if j >= 2:
                    pe.wait_ge(S["acc0"], j - 1)
                mm(ps[:, 6 + j % 2, 0:NTOK], b2_rows[:, P * j:P * j + P], gT[:, :], start=True, stop=True).then_inc(S["b2ps"], 1)
            pe.wait_ge(S["cntr"], 1)
            pe.wait_ge(S["acc0"], J)
            pe.wait_ge(S["b1T"], 1)

            def scatter(n):
                for j in range(J):
                    if j >= 2:
                        pe.wait_ge(S["acc"], n * J + (j - 1))
                    mm(ps[:, 5 + j % 2, 0:NTOK], y[:, P * j:P * j + P], selT, start=True, stop=True).then_inc(S["comb"], 1)

            def chunk(n, e, first, last):
                pe.wait_ge(S["sel"], n * 2 + 2)
                for j in range(J):
                    for t, (t0, k) in enumerate(TILES):
                        ins = mm(ps[:, 0, CAP * j:CAP * j + CAP], h[0:k, t, j::J], sel[0:k, t, :], start=(t == 0), stop=(t == 2))
                ins.then_inc(S["gath"], 1)
                pe.wait_ge(S["yr"], n + 1)
                pe.wait_ge(S["selT"], n + 1)
                scatter(n)
                for t, (t0, k) in enumerate(TILES):
                    ins = tp(ps[0:CAP, 4, t0:t0 + k], selg[0:k, t, :], ident[0:k, 0:k])
                ins.then_inc(S["selT_ps"], 1)
                pe.wait_ge(S["xe"], n + 1)
                def up(k, b):
                    for j in (2 * k, 2 * k + 1):
                        for g in range(2):
                            for m in range(4):
                                col = (j % 2) * 2048 + DFF * g + P * (4 * b + m)
                                at = CAP * (4 * g + m)
                                ins = mm(ps[:, 1 + b, at:at + CAP], ring[:, k, col:col + P], xe[:, j, :],
                                         start=(j == 0 and g == 0 and m == 0), stop=(j == J - 1), skip_group_check=True)
                    return ins
                for k in range(3):
                    pe.wait_ge(s_w[k], e * 16 + 16)
                    up(k, 0)
                    ins = up(k, 1)
                    if last:
                        ins.then_inc(S["wfree"], 1)
                pe.wait_ge(s_w[3], e * 16 + 16)
                up(3, 0).then_inc(S["mm1"], 1)
                up(3, 1).then_inc(S["mm1"], 1)
                for b in range(2):
                    pe.wait_ge(s_w[4 + b], e * 16 + 16)
                    pe.wait_ge(S["midr"], n * 2 + (b + 1))
                    for m in range(4):
                        for j in range(J):
                            ins = mm(ps[:, 3, CAP * j:CAP * j + CAP], ring[:, 4 + b, D * m + P * j:D * m + P * j + P], mid[:, b, m, :],
                                     start=(b == 0 and m == 0 and j == 0), stop=(b == 1 and m == 3), skip_group_check=True)
                        if last and b == 0 and m == 0:
                            ins.then_inc(S["wfree"], 1)
                    if last and b == 0:
                        ins.then_inc(S["wfree"], 1)
                ins.then_inc(S["mm2"], 1)
                pe.wait_ge(S["yTr"], n + 1)
                pe.wait_ge(S["acc"], n * J + J)
                for j in range(J):
                    op = mm if j == 0 else tp
                    ins = op(ps[0:CAP, 5 + j // 4, P * (j % 4):P * (j % 4) + P], yT[:, CAP * j:CAP * j + CAP], ident)
                    if last and j == 0:
                        ins.then_inc(S["wfree"], 1)
                ins.then_inc(S["y_ps"], 1)

            total = run_experts(pe, chunk)
            pe.wait_ge(S["yr"], total + 1)
            pe.wait_ge(S["selT"], total + 1)
            scatter(total)
            pe.wait_ge(S["acc"], total * J + J)
            for t, (t0, n) in enumerate(TILES):
                for j in range(J):
                    ins = tp(ps[0:n, 2 * t + j // 4, P * (j % 4):P * (j % 4) + P], accT[:, j, t0:t0 + n], ident)
                ins.then_inc(S["fin_ps"], 1)


_INS = """x_prompt x_sample cache_k cache_v state_ssm_re state_ssm_im norm_mix_g w_in attn_out_norm_g
    ssm_a_re ssm_a_im ssm_log_dt ssm_b_re ssm_b_im ssm_c_re ssm_c_im ssm_d w_glu b_glu ssm_out_norm_g
    w_out norm_ffn_g w_router b_router w_moe1 b_moe1 w_moe2 b_moe2 norm_final_g""".split()
_OUTS = [("y_p", (1, SEQ, D)), ("y_s", (NB, NSEQ, D)), ("k_p", (1, 1, SEQ, H, HD)), ("v_p", (1, 1, SEQ, H, HD)),
         ("re_p", (1, 1, 32, 64)), ("im_p", (1, 1, 32, 64)), ("k_s", (1, NB, NSEQ, H, HD)), ("v_s", (1, NB, NSEQ, H, HD)),
         ("re_s", (1, NB, 32, 64)), ("im_s", (1, NB, 32, 64))]


def kernel(**inputs):
    import numpy as _np
    import concourse.bacc as _bacc
    from concourse import mybir as _mybir
    from concourse.bass_utils import run_bass_kernel_spmd as _run

    nc = _bacc.Bacc("TRN2", target_bir_lowering=False, num_devices=1, dynamic_dma_scratch_size=1024)
    arrays, ins, outs = {}, {}, {}
    for name in _INS + ["con"]:
        a = constants() if name == "con" else _np.ascontiguousarray(inputs[name])
        arrays[f"in_{name}_dram"] = a
        ins[name] = nc.dram_tensor(f"in_{name}_dram", a.shape, _mybir.dt.from_np(a.dtype), kind="ExternalInput").ap()
    for name, shape in _OUTS:
        outs[name] = nc.dram_tensor(f"out_{name}_dram", shape, _mybir.dt.float32, kind="ExternalOutput").ap()
    decoder_step(nc, ins, outs)
    r = _run(nc, [arrays], core_ids=[0])
    return tuple(r.results[0][f"out_{name}_dram"] for name, _ in _OUTS)
```

```python
from contextlib import ExitStack

import numpy as np

import concourse.bass as bass
from concourse import mybir

F32 = mybir.dt.float32
I32 = mybir.dt.int32
U32 = mybir.dt.uint32
FR = mybir.dt.float32r
ALU = mybir.AluOpType
ACT = mybir.ActivationFunctionType
AX = mybir.AxisListType.X

P = 128
D = 1024
J = D // P
SEQ, NB, NSEQ = 256, 8, 4
NS = NB * NSEQ
NTOK = SEQ + NS
TILES = [(0, P), (P, P), (SEQ, NS)]
H, HD = 8, 64
SCALE = HD ** -0.5
PAST = 1024
NEXP, TOPK, DFF = 32, 4, 1024
CAP = 128
CHUNKS = -(-NTOK // CAP)
NI = 16
HALF = SEQ // 2
EPS = 1e-5
ALPHA, LIMIT = 1.702, 7.0
NEG = -1e30
TWO_PI = 6.283185307179586
TP_HI = 6.28125
TP_LO = TWO_PI - TP_HI
ROUND = 1.5 * 2.0 ** 23
PI_IN = 3.1415925
G_A = 0.7978845608028654 * 2.0
G_B = 0.044715
NPIECE = 12

C_ID, C_TRI, C_BP, C_BS, C_IOTA, C_GM = 0, 128, 256, 640, 1472, 1856
C_ALL = 1984


def window_bias(delta):
    n = (((delta >= 0) & (delta <= 128)).astype(int)
         + ((delta >= 0) & (delta <= 512) & (delta % 4 == 0))
         + ((delta >= 0) & (delta <= 2048) & (delta % 16 == 0)))
    return np.where(n > 0, np.log(np.maximum(n, 1)), NEG)


def constants():
    c = np.zeros((P, C_ALL), np.float32)
    p = np.arange(P)[:, None]
    f = np.arange(P)[None, :]
    c[:, C_ID:C_ID + P] = p == f
    c[:, C_TRI:C_TRI + P] = p < f
    c[:, C_BP:C_BP + P] = window_bias(p - f)
    c[:, C_BP + P:C_BP + 3 * P] = window_bias(P + p - np.arange(SEQ)[None, :])
    qpos = PAST + p % NSEQ
    r = np.arange(P)
    for rt in range(4):
        c[:, C_BS + rt * P:C_BS + (rt + 1) * P] = window_bias(qpos - (512 + 4 * r + rt)[None, :])
    for half in range(2):
        at = C_BS + 512 + 160 * half
        c[:, at:at + P] = window_bias(qpos - (16 * (r % 32) + r // 32)[None, :])
        s = np.arange(NS)[None, :]
        same = (half * 4 + p // 32) == s // NSEQ
        c[:, at + P:at + 160] = np.where(same, window_bias(qpos - (PAST + s % NSEQ)), NEG)
    c[:, C_IOTA:C_IOTA + 384] = np.arange(384)
    c[:, C_GM:C_GM + P] = (f // 16) % 2 == p // 64
    return c


def decoder_step(nc, I, O):
    with ExitStack() as ctx:
        def sb(name, shape, dt=F32):
            return ctx.enter_context(nc.sbuf_tensor(name, shape, dt))

        def sem(name):
            return ctx.enter_context(nc.semaphore(name))

        ring = sb("ring", [P, 6, 4096])
        ring_at = nc.sbuf_base - 6 * 4096 * 4
        tmp = sb("tmp", [P, 4096])
        ring_w = ring[:, 0:3, :].rearrange("p s n -> p (s n)").rearrange("p (s n) -> p s n", s=6)
        w_in = ring[:, 0:4, :].rearrange("p s n -> p (s n)").rearrange("p (g j n) -> p g j n", g=4, j=J)
        kv = ring[:, 0:4, :].rearrange("p s n -> p (s n)")
        k_cache = kv[:, 0:2 * 2560].rearrange("p (s n) -> p s n", s=2)
        v_cache = kv[:, 2 * 2560:6 * 2560].rearrange("p (s n) -> p s n", s=4)
        w_out = ring[:, 4:6, :].rearrange("p s n -> p (s n)").rearrange("p (j n) -> p j n", j=J)

        con = sb("con", [P, C_ALL])
        ident = con[:, C_ID:C_ID + P]
        tri = con[:, C_TRI:C_TRI + P]
        iota = con[:, C_IOTA:C_IOTA + 384]
        gmask = con[:, C_GM:C_GM + P]
        x = sb("x", [P, 3, D])
        accT = sb("accT", [P, J, NTOK])
        uni = sb("uni", [P, 8704])
        qkvu = uni[:, 0:16 * NTOK].rearrange("p (c t) -> p c t", c=16)
        xn = uni[:, 0:3 * D].rearrange("p (t d) -> p t d", t=3)
        e_tab = uni[:, 4608:8704].rearrange("p (r i t) -> p r i t", r=2, i=NI)
        h = uni[:, 0:3072].rearrange("p (t d) -> p t d", t=3)
        o = 3072
        sel = uni[:, o:o + 384].rearrange("p (t s) -> p t s", t=3)
        selg = uni[:, o + 384:o + 768].rearrange("p (t s) -> p t s", t=3)
        selT = uni[:, o + 768:o + 1056]
        glu_b = uni[:, o + 1056:o + 1568]
        sig = uni[:, o + 1568:o + 2080]
        lin = uni[:, o + 2080:o + 3104].rearrange("p (b n) -> p b n", b=2)
        mid = uni[:, o + 3104:o + 4128].rearrange("p (b n) -> p b n", b=2)
        posm = uni[:, o + 4128:o + 4224].rearrange("p (e t) -> p e t", e=NEXP)
        gate = uni[:, o + 4224:o + 4320].rearrange("p (e t) -> p e t", e=NEXP)
        y = uni[:, o + 4320:o + 5344]
        b2_rows = uni[0:NEXP, o + 4320:o + 5344]
        g_row = con[:, C_BP:C_BP + D]

        e_tmp = tmp[:, 0:2048].rearrange("p (a i t) -> p a i t", a=2, i=NI)
        scb = tmp[:, 0:768].rearrange("p (b n) -> p b n", b=2)
        prb = tmp[:, 768:1536].rearrange("p (b n) -> p b n", b=2)
        ptb = tmp[:, 1536:2304].rearrange("p (b n) -> p b n", b=2)
        sT = tmp[:, 0:768]
        s_s = tmp[:, 768:1440]
        p_s = tmp[:, 1440:2112]
        p_T = tmp[:, 2112:2880]
        kT_s = tmp[:, 2880:3904].rearrange("p (b n) -> p b n", b=2)
        kv_rows = sb("kv_rows", [P, 2, 3, 512])
        b1b = kv_rows[:, :, :, :].rearrange("p a t n -> p (a t n)")[:, 0:2 * DFF]
        yS = sb("yS", [P, 4, NTOK])
        y_at = nc.sbuf_base - 4 * NTOK * 4
        aT = sb("aT", [P, 4, NTOK])
        w_glu = sb("w_glu", [P, 4, 512])
        KB = 1024
        w_hi = nc.alloc_sbuf_tensor_at("w_hi", [P, 4, 2048], FR, offset=ring_at + 48 * KB)
        w_lo = nc.alloc_sbuf_tensor_at("w_lo", [P, 4, 2048], FR, offset=ring_at + 80 * KB)
        xe_hi = nc.alloc_sbuf_tensor_at("xe_hi", [P, J, CAP], FR, offset=y_at)
        xe_lo = nc.alloc_sbuf_tensor_at("xe_lo", [P, J, CAP], FR, offset=y_at + 4 * KB)
        mt_hi = nc.alloc_sbuf_tensor_at("mt_hi", [P, J, CAP], FR, offset=y_at + 8 * KB)
        mt_lo = nc.alloc_sbuf_tensor_at("mt_lo", [P, J, CAP], FR, offset=y_at + 12 * KB)
        par = sb("par", [P, 256])
        ld = sb("ld", [P, 4])
        prm = sb("prm", [P, 24, NI])
        PA_LR, PA_LI, PA_RD, PA_TH, PA_R, PA_C, PA_S, PA_AR, PA_AI, PA_FR, PA_FI = range(11)
        s5 = ring[:, 4:6, :].rearrange("p s n -> p (s n)")
        s5_at = [0]

        def s5_buf(n):
            s5_at[0] += n
            return s5[:, s5_at[0] - n:s5_at[0]]

        bnat = s5_buf(512).rearrange("p (r n) -> p r n", r=2)
        xb = tmp[:, 2048:3072].rearrange("p (r n) -> p r n", r=2)
        cnat = tmp[:, 3072:4096].rearrange("p (r b n) -> p r b n", r=2, b=4)
        bT = s5_buf(1024).rearrange("p (r n) -> p r n", r=2)
        cT = s5_buf(1024).rearrange("p (r n) -> p r n", r=2)
        h0row = sb("h0row", [P, 2, P])
        h0 = s5_buf(256).rearrange("p (r n) -> p r n", r=2)
        hs = s5_buf(1024).rearrange("p (r i n) -> p r i n", r=2, i=NI)
        bus = aT[:, :, :].rearrange("p a t -> p (a t)")[:, 0:1024]
        ssm_a = s5_buf(512).rearrange("p (a t) -> p a t", a=4)
        ssm_b = s5_buf(512).rearrange("p (a t) -> p a t", a=4)
        ssm_g = s5_buf(1024).rearrange("p (b r a t) -> p b r a t", b=2, r=2, a=2)
        ssm_h = s5_buf(1024).rearrange("p (b r t) -> p b r t", b=2, r=2)
        ssm_p = s5_buf(512).rearrange("p (a t) -> p a t", a=4)
        hf = sb("hf", [P, 2, NI])
        sf = h0row
        st_out = sb("st_out", [P, 4, P])
        qbd = sb("qbd", [P, 4, NB, 8])
        wr = sb("wr", [P, J, NEXP])
        vec = sb("vec", [P, 64])
        gmx, dsk, bgl, gat, gss = (vec[:, 0:8], vec[:, 8:12], vec[:, 12:16], vec[:, 16:20], vec[:, 20:24])
        bro = sb("bro", [P, NEXP])
        ones = sb("ones", [P, P])
        kvg = uni[:, 4608:5760]
        sqa = uni[:, 5760:6912].rearrange("p (b t) -> p b t", b=4)
        sqs = uni[:, 6912:8064].rearrange("p (b t) -> p b t", b=4)
        st = sb("st", [P, 96])
        mark = sb("mark", [P, 8])
        gT = sb("gT", [NEXP, NTOK])
        rt_s = sb("rt_s", [P, 3, 6, NEXP])
        top = sb("top", [P, 3, 32])
        tidx = sb("tidx", [P, 3, 8], U32)
        oh = sb("oh", [P, 3, 2, TOPK, NEXP])
        cnt = sb("cnt", [P, NEXP], I32)
        ps = ctx.enter_context(nc.psum_tensor("ps", [P, 8, 512], F32))

        names = """x con prm win0 win1 wglu wout late gff gfi b1 kload0 kload1 vload0 vload1 vload2 vload3
            out ss ms rt xn rows dt prmT exps sin red crev xT_ps xT_d xT_a proj proj_ev etab fdone bT_ps bT
            bu bu_used hlo g1 hhi yps yblk bus_ps bus hs ysps yS_ready kvr_ps kvr qbd s_ps nm ex pn pt_ps pt o_ps aT
            kt_ps ktA ktD st_ps stE ts_ps nms exs pns pts_ps pts pv aTs sto_ps sto hfin sfin
            gel1 gel2 gg glu_ps glu sq sqA ssq ms2 rt2 mix wo_ps x2 ss3 ms3 rt3 h hT_ps hT lg rout posps posm cntr gT_ps gT b2ps acc0
            init sel gath xe_hi xe_lo selT_ps selT glin sgm midr mt_ps mt_hi mt_lo yr comb acc chain_a chain_v chain_p swc gex ysv
            w_hi w_lo_v w_lo_p w_used b1b b2 zero
            fin_ps x3 ss4 ms4 rt4 yfin""".split()
        S = {n: sem("s_" + n) for n in names}
        s_w = [sem(f"s_w{k}") for k in range(6)]
        NPRM = 17

        def bc(ap, shape):
            return ap.broadcast_to(shape)

        block = ctx.enter_context(nc.Block())

        def piece(e, k):
            if k < 8:
                src = I["w_moe1"][0, bass.ds(e, 1), :, :].rearrange("a (p j) (g b n) -> (a p) j b g n", j=J, g=2, b=2)
                j, b = 2 * (k % 4), 1 - k // 4
                return ring_w[:, k % 6, :].rearrange("p (j g n) -> p j g n", j=2, g=2), src[:, j:j + 2, b]
            src = I["w_moe2"][0, bass.ds(e, 1), :, :].rearrange("a (m q) n -> q (a m) n", q=P)
            return ring_w[:, k % 6, :].rearrange("p (m n) -> p m n", m=2), src[:, (2 * k - 12) % J:(2 * k - 12) % J + 2, :]

        LO_P = [1, 4, 7, 10]
        LO_V = [k for k in range(NPIECE) if k not in LO_P]

        def wait_low(eng, n, k, back=0):
            if k in LO_P:
                eng.wait_ge(S["w_lo_p"], n * 4 + (2 + LO_P.index(k) + 1 - back // 3))
            else:
                eng.wait_ge(S["w_lo_v"], n * 8 + (4 + LO_V.index(k) + 1 - 2 * back // 3))

        def run_experts(eng, chunk):
            done = eng.alloc_register()
            eng.reg_mov(done, 0)
            with eng.Fori(0, NEXP) as e:
                count = eng.value_load(cnt[0:1, bass.ds(e, 1)], min_val=0, max_val=NTOK)
                with eng.If(count > CAP):
                    with eng.Fori(1, CHUNKS) as c:
                        with eng.If(count > c * CAP):
                            chunk(eng.snap(done, min_val=0, max_val=NEXP * CHUNKS), e, c * CAP, False)
                            eng.reg_add(done, done, 1)
                chunk(eng.snap(done, min_val=0, max_val=NEXP * CHUNKS), e, 0, True)
                eng.reg_add(done, done, 1)
            return eng.snap(done, min_val=0, max_val=NEXP * CHUNKS)

        @block.sync
        def _(sp):
            sp.dma_start(x[:, 0:2, :], I["x_prompt"][0].rearrange("(t p) d -> p t d", p=P)).then_inc(S["x"], 16)
            sp.dma_start(x[0:NS, 2, :], I["x_sample"].rearrange("b t d -> (b t) d")).then_inc(S["x"], 16)
            wv = I["w_in"][0].rearrange("(p j) (g n) -> p g j n", j=J, g=4)
            sp.dma_start(w_in[:, 3, :, :], wv[:, 3]).then_inc(S["win0"], 16)
            sp.dma_start(con[:, :], I["con"]).then_inc(S["con"], 16)
            for g in range(3):
                sp.dma_start(w_in[:, g, :, :], wv[:, g]).then_inc(S["win1"], 16)
            sp.dma_start(w_glu[:, :, :], I["w_glu"][0].rearrange("(j p) n -> p j n", p=P)).then_inc(S["wglu"], 16)
            sp.dma_start(wr[:, :, :], I["w_router"][0].rearrange("(p j) n -> p j n", j=J)).then_inc(S["wglu"], 16)

            def load_cache(name, dst, b, sm):
                c = I[name][0, b].rearrange("r h e -> r (h e)")
                sp.dma_start(dst[:, 0:2048], c[512:1024].rearrange("(p j) n -> p (j n)", j=4)).then_inc(sm, 16)
                lo = c[0:512].rearrange("(i s) n -> s i n", s=16)
                for s in range(4):
                    sp.dma_start(dst[32 * s:32 * s + 32, 2048:2560], lo[s]).then_inc(sm, 16)

            sp.wait_ge(S["proj"], 16)
            for b in range(NB):
                if b >= 2:
                    sp.wait_ge(S["kt_ps"], 5 * (b - 1))
                load_cache("cache_k", k_cache[:, b % 2, :], b, S[f"kload{b % 2}"])
                if b >= 4:
                    sp.wait_ge(S["pv"], 1)
                load_cache("cache_v", v_cache[:, b % 4, :], b, S[f"vload{b % 4}"])
                if b == 1:
                    sp.wait_ge(S["sto_ps"], 1)
                    sp.dma_start(w_out, I["w_out"][0].rearrange("(j p) n -> p j n", p=P)).then_inc(S["wout"], 16)
            sp.wait_ge(S["kvr"], 6)
            for a, nm in enumerate("kv"):
                sp.dma_start(O[nm + "_p"].rearrange("a b (t p) h e -> p (a b t) (h e)", p=P), kv_rows[:, a, 0:2, :]).then_inc(S["out"], 16)
                sp.dma_start(O[nm + "_s"].rearrange("a b t h e -> (a b t) (h e)"), kv_rows[0:NS, a, 2, :]).then_inc(S["out"], 16)
            sp.wait_ge(S["sto"], 1)
            for r, nm in enumerate(("re_p", "im_p")):
                sp.dma_start(O[nm].rearrange("a b (i g) n -> (a b i) (g n)", g=2), st_out[0:NI, r, :]).then_inc(S["out"], 16)
            for r, nm in enumerate(("re_s", "im_s")):
                sp.dma_start(O[nm].rearrange("a b (i g) n -> (a b i) (g n)", g=2), st_out[:, 2 + r, :]).then_inc(S["out"], 16)
            sp.wait_ge(S["pv"], 2)
            sp.dma_start(g_row, I["norm_ffn_g"].broadcast_to([P, D])).then_inc(S["gff"], 16)
            for k in range(6):
                sp.dma_start(*piece(0, k)).then_inc(s_w[k], 16)
            sp.wait_ge(S["ssq"], 1)
            sp.dma_start(b2_rows, I["b_moe2"][0]).then_inc(S["b2"], 16)
            sp.wait_ge(S["h"], 3)
            sp.dma_start(g_row, I["norm_final_g"].rearrange("(a d) -> a d", a=1).broadcast_to([P, D])).then_inc(S["gfi"], 16)
            sp.wait_ge(S["cntr"], 1)
            sp.wait_ge(S["out"], 16 * 8)

            following = sp.alloc_register()
            sp.reg_mov(following, 0)
            own_reg = sp.alloc_register()

            def load(n, e, own, k):
                wait_low(sp, n, k, back=6)
                sp.dma_start(*piece(own if k in (4, 10) else e, k)).then_inc(s_w[k % 6], 16)

            def weights(n, e, first, last):
                sp.wait_ge(S["midr"], n * 2 + 1)
                sp.dma_start(b1b, I["b_moe1"][0, bass.ds(e, 1), :].broadcast_to([P, 2 * DFF])).then_inc(S["b1b"], 16)
                sp.reg_mov(own_reg, e)
                own = sp.snap(own_reg, min_val=0, max_val=NEXP - 1)
                for k in range(6, 12):
                    load(n, e, own, k)

                def ahead(e):
                    sp.reg_mov(own_reg, e)
                    own = sp.snap(own_reg, min_val=0, max_val=NEXP - 1)
                    for k in range(6):
                        load(n + 1, e, own, k)
                if last:
                    sp.reg_add(following, following, 1)
                    with sp.If(e < NEXP - 1):
                        ahead(sp.snap(following, min_val=0, max_val=NEXP - 1))
                else:
                    ahead(e)

            run_experts(sp, weights)
            sp.wait_ge(S["yfin"], 3)
            sp.dma_start(O["y_p"][0].rearrange("(t p) d -> p t d", p=P), x[:, 0:2, :]).then_inc(S["out"], 16)
            sp.dma_start(O["y_s"].rearrange("b t d -> (b t) d"), x[0:NS, 2, :]).then_inc(S["out"], 16)
            sp.wait_ge(S["out"], 16 * 10)

        @block.gpsimd
        def _(pool):
            chain = [0]

            def link(ins):
                chain[0] += 1
                ins.then_inc(S["chain_p"], 1)
                pool.wait_ge(S["chain_p"], chain[0])

            tt = pool.tensor_tensor
            pool.wait_ge(S["exps"], 1)
            link(pool.tensor_copy(e_tab[:, 0, :, 0:1], prm[:, PA_C, :].unsqueeze(2)))
            link(pool.tensor_copy(e_tab[:, 1, :, 0:1], prm[:, PA_S, :].unsqueeze(2)))
            m = 1
            while m < HALF:
                re, im = e_tab[:, 0, :, 0:m], e_tab[:, 1, :, 0:m]
                cr = bc(e_tab[:, 0, :, m - 1:m], [P, NI, m])
                ci = bc(e_tab[:, 1, :, m - 1:m], [P, NI, m])
                t1, t2 = e_tmp[:, 0, :, 0:m], e_tmp[:, 1, :, 0:m]
                link(tt(t1, re, cr, ALU.mult))
                link(tt(t2, im, ci, ALU.mult))
                link(tt(e_tab[:, 0, :, m:2 * m], t1, t2, ALU.subtract))
                link(tt(t1, re, ci, ALU.mult))
                link(tt(t2, im, cr, ALU.mult))
                ins = tt(e_tab[:, 1, :, m:2 * m], t1, t2, ALU.add)
                m *= 2
                if m < HALF:
                    link(ins)
            ins.then_inc(S["etab"], 1)
            pool.wait_ge(S["etab"], 1)
            for i in range(NI):
                b = i % 2
                er, ei = e_tab[:, 0, i, :], e_tab[:, 1, i, :]
                pool.wait_ge(S["g1"], i + 1)
                if i >= 1:
                    pool.wait_ge(S["hhi"], i)
                if i >= 2:
                    pool.wait_ge(S["yps"], i - 1)
                gr, gi = ssm_g[:, b, 0, 1, :], ssm_g[:, b, 1, 1, :]
                tt(ssm_p[:, 0, :], gr, er, ALU.mult)
                tt(ssm_p[:, 1, :], gi, er, ALU.mult)
                tt(ssm_p[:, 2, :], gi, ei, ALU.mult)
                link(tt(ssm_p[:, 3, :], gr, ei, ALU.mult))
                tt(ssm_h[:, b, 0, HALF:], ssm_p[:, 0, :], ssm_p[:, 2, :], ALU.subtract)
                tt(ssm_h[:, b, 1, HALF:], ssm_p[:, 1, :], ssm_p[:, 3, :], ALU.add).then_inc(S["hhi"], 1)
                pool.wait_ge(S["hhi"], i + 1)
                ins = pool.tensor_copy(hf[:, :, i:i + 1], ssm_h[:, b, :, SEQ - 1:SEQ])
            ins.then_inc(S["hfin"], 1)

            def low_parts(n, e, first, last):
                for k in LO_P:
                    pool.wait_ge(S["w_hi"], n * NPIECE + (k + 1))
                    tt(w_lo[:, k % 4, :], ring_w[:, k % 6, :], w_hi[:, k % 4, :].bitcast(F32), ALU.subtract).then_inc(S["w_lo_p"], 1)

            pool.wait_ge(S["cntr"], 1)
            run_experts(pool, low_parts)

        @block.scalar
        def _(act):
            chain = [0]

            def link(ins):
                chain[0] += 1
                ins.then_inc(S["chain_a"], 1)
                act.wait_ge(S["chain_a"], chain[0])

            def small(dst, src):
                act.dma_start(dst, src).then_inc(S["prm"], 16)

            A = act.activation
            with nc.allow_non_contiguous_dma(reason="parameters of a few hundred words"):
                small(ld[0:NI, 0:2], I["ssm_log_dt"][0].rearrange("(i g) -> i g", g=2))
                small(par[0:NI, 0:P], I["ssm_a_re"][0].rearrange("(i g) n -> i (g n)", g=2))
                small(par[0:NI, P:2 * P], I["ssm_a_im"][0].rearrange("(i g) n -> i (g n)", g=2))
                small(gmx, I["norm_mix_g"][0].rearrange("(p j) -> p j", j=J))
                for r, nm in enumerate(("state_ssm_re", "state_ssm_im")):
                    small(h0row[:, r, :], I[nm][0].rearrange("b (i g) n -> (b i) (g n)", g=2))
                for r, nm in enumerate(("ssm_b_re", "ssm_b_im")):
                    small(bnat[:, r, :].rearrange("p (i c) -> p i c", i=NI), I[nm][0].rearrange("(i g) n c -> (g n) i c", g=2))
                for r, nm in enumerate(("ssm_c_re", "ssm_c_im")):
                    for dup in range(2):
                        small(cnat[:, r, :, 64 * dup:64 * dup + 64], I[nm][0].rearrange("g c n -> (g c) n").rearrange("(b p) n -> p b n", p=P))
                small(dsk, I["ssm_d"][0].rearrange("(b g) c -> (g c) b", g=8))
                small(bgl, I["b_glu"][0].rearrange("(b p) -> p b", p=P))
                small(gat, I["attn_out_norm_g"][0].rearrange("(b p) -> p b", p=P))
                small(gss, I["ssm_out_norm_g"][0].rearrange("(b p) -> p b", p=P))
                small(bro[:, :], I["b_router"].broadcast_to([P, NEXP]))
            act.wait_ge(S["prm"], 16 * NPRM)
            A(ld[0:NI, 0:2], ld[0:NI, 0:2], ACT.Exp).then_inc(S["dt"], 1)
            act.wait_ge(S["x"], 32)
            act.wait_ge(S["init"], 1)
            for t, (_, n) in enumerate(TILES):
                ins = A(xn[0:n, t, :], x[0:n, t, :], ACT.Square, accum_out=st[0:n, t:t + 1])
            ins.then_inc(S["ss"], 1)
            act.wait_ge(S["ms"], 1)
            A(st[:, 3:6], st[:, 3:6], ACT.Sqrt).then_inc(S["rt"], 1)
            act.wait_ge(S["red"], 1)
            A(prm[:, PA_R, :], prm[:, PA_RD, :], ACT.Exp)
            A(prm[:, PA_C, :], prm[:, 11, :], ACT.Sin)
            A(prm[:, PA_S, :], prm[:, 12, :], ACT.Sin).then_inc(S["exps"], 1)
            for n, j in enumerate(range(1, J, 2)):
                act.wait_ge(S["xT_ps"], j + 1)
                A(accT[:, j, :], ps[:, 4 + j % 4, 0:NTOK], ACT.Copy, scale=gmx[:, j:j + 1]).then_inc(S["xT_a"], 1)
            for n, c in enumerate([12, 13, 14, 15] + list(range(12))):
                act.wait_ge(S["proj"], n + 1)
                A(qkvu[:, c, :], ps[:, 4 + n % 2, 0:NTOK], ACT.Copy).then_inc(S["proj_ev"], 1)
            act.wait_ge(S["proj_ev"], 16)
            for g in range(2):
                rows = slice(64 * g, 64 * g + 64)
                ins = A(qbd[rows, :, :, 4 * g:4 * g + 4], qkvu[rows, 0:4, SEQ:].rearrange("p c (b t) -> p c b t", t=NSEQ), ACT.Copy)
            ins.then_inc(S["qbd"], 1)
            act.wait_ge(S["bu"], NI)
            for n in range(2):
                ins = A(bus.rearrange("p (k n c) -> p n k c", k=8, n=2)[:, n], ps[:, n, :].rearrange("p (k c) -> p k c", k=8), ACT.Copy)
            ins.then_inc(S["bus"], 1)
            for n in range(6):
                a, t = divmod(n, 3)
                rows = TILES[t][1]
                act.wait_ge(S["kvr_ps"], n + 1)
                A(kv_rows[0:rows, a, t, :], ps[0:rows, 4 + n % 2, :], ACT.Copy).then_inc(S["kvr"], 1)
            act.wait_ge(S["sto_ps"], 1)
            A(st_out[0:NI, 0:2, :], ps[0:NI, 5, 0:2 * P].rearrange("p (r n) -> p r n", r=2), ACT.Copy)
            A(st_out[:, 2:4, :], ps[:, 5, 2 * P:4 * P].rearrange("p (r n) -> p r n", r=2), ACT.Copy).then_inc(S["sto"], 1)
            for hh in range(H + 1):
                if hh < H:
                    b = hh % 2
                    act.wait_ge(S["nm"], hh + 1)
                    A(prb[:, b, 0:P], scb[:, b, 0:P], ACT.Exp, bias=st[:, 12 + 2 * b:13 + 2 * b], accum_out=st[:, 16 + 2 * b:17 + 2 * b])
                    A(prb[:, b, P:], scb[:, b, P:], ACT.Exp, bias=st[:, 13 + 2 * b:14 + 2 * b], accum_out=st[:, 17 + 2 * b:18 + 2 * b]).then_inc(S["ex"], 1)
                if hh >= 1:
                    b = (hh - 1) % 2
                    act.wait_ge(S["pt_ps"], hh)
                    A(ptb[:, b, :], ps[:, b, 0:3 * P], ACT.Copy).then_inc(S["pt"], 1)
            for half in range(2):
                for n in range(0, 20, 2):
                    act.wait_ge(S["kt_ps"], 20 * half + n + 1)
                    if half == 0 and n == 0:
                        act.wait_ge(S["o_ps"], H)
                    A(kT_s[:, 0, :], ps[:, 4, :], ACT.Copy).then_inc(S["ktA"], 1)
                act.wait_ge(S["st_ps"], half + 1)
                A(sT[:, 0:512], ps[:, 6, :], ACT.Copy)
                A(sT[:, 512:640], ps[:, 7, 0:P], ACT.Copy)
                A(sT[0:NS, 640:768], ps[0:NS, 7, P:2 * P], ACT.Copy).then_inc(S["stE"], 1)
                act.wait_ge(S["nms"], half + 1)
                A(p_s, s_s, ACT.Exp, bias=st[:, 24:25], accum_out=st[:, 25:26]).then_inc(S["exs"], 1)
                act.wait_ge(S["pts_ps"], half + 1)
                A(p_T[:, 0:512], ps[:, 6, :], ACT.Copy)
                A(p_T[:, 512:640], ps[:, 7, 0:P], ACT.Copy)
                A(p_T[0:NS, 640:768], ps[0:NS, 7, P:2 * P], ACT.Copy).then_inc(S["pts"], 1)
            act.wait_ge(S["gel1"], 1)
            A(kvg, kvg, ACT.Sigmoid, scale=G_A).then_inc(S["gel2"], 1)
            for b in range(4):
                act.wait_ge(S["glu_ps"], b + 1)
                A(kvg.rearrange("p (b t) -> p b t", b=4)[:, b, :], ps[:, 4 + b, 0:NTOK], ACT.Sigmoid, bias=bgl[:, b:b + 1]).then_inc(S["glu"], 1)
            act.wait_ge(S["aTs"], 2)
            act.wait_ge(S["sq"], 1)
            A(sqa, aT[:, :, :], ACT.Square).then_inc(S["sqA"], 1)
            act.wait_ge(S["ms2"], 1)
            A(st[:, 36:42], st[:, 36:42], ACT.Sqrt).then_inc(S["rt2"], 1)
            for t, (_, n) in enumerate(TILES):
                act.wait_ge(S["x2"], t + 1)
                ins = A(h[0:n, t, :], x[0:n, t, :], ACT.Square, accum_out=st[0:n, 48 + t:49 + t])
            ins.then_inc(S["ss3"], 1)
            act.wait_ge(S["ms3"], 1)
            A(st[:, 51:54], st[:, 51:54], ACT.Sqrt).then_inc(S["rt3"], 1)
            for j in range(1, J, 2):
                act.wait_ge(S["hT_ps"], j + 1)
                A(accT[:, j, :], ps[:, j, 0:NTOK], ACT.Copy).then_inc(S["xT_a"], 1)
            for t, (_, n) in enumerate(TILES):
                act.wait_ge(S["rout"], t + 1)
                A(top[0:n, t, 12:16], top[0:n, t, 8:12], ACT.Exp, accum_out=top[0:n, t, 20:21]).then_inc(S["gex"], 1)
            act.wait_ge(S["gT_ps"], 1)
            A(gT[:, :], ps[0:NEXP, 4, 0:NTOK], ACT.Copy).then_inc(S["gT"], 1)
            for j in range(J):
                act.wait_ge(S["b2ps"], j + 1)
                A(accT[:, j, :], ps[:, 6 + j % 2, 0:NTOK], ACT.Copy).then_inc(S["acc0"], 1)

            def rows_out(n):
                act.wait_ge(S["w_used"], n * NPIECE + 4)
                A(y.rearrange("p (a n) -> p a n", a=2), ps[:, 6:8, :], ACT.Copy).then_inc(S["yr"], 1)

            def act_pass(n, e, first, last):
                def high(*ks):
                    for k in ks:
                        act.wait_ge(s_w[k % 6], n * 32 + 16 * (k // 6 + 1))
                        act.wait_ge(S["w_used"], n * NPIECE + (k + 1))
                        A(w_hi[:, k % 4, :], ring_w[:, k % 6, :], ACT.Copy).then_inc(S["w_hi"], 1)

                def mid_high(b):
                    act.wait_ge(S["mt_ps"], n * 2 + (b + 1))
                    A(mt_hi[:, 4 * b:4 * b + 4, :], ps[:, 4 + b, :].rearrange("p (m s) -> p m s", m=4), ACT.Copy).then_inc(S["mt_hi"], 1)

                def sigmoid(b):
                    act.wait_ge(S["glin"], n * 2 + (b + 1))
                    A(sig, glu_b, ACT.Sigmoid, scale=ALPHA).then_inc(S["sgm"], 1)

                high(0, 1)
                rows_out(n)
                for a in range(2):
                    act.wait_ge(S["gath"], n * 2 + (a + 1))
                    A(xe_hi[:, 4 * a:4 * a + 4, :], ps[:, 4 + a, :].rearrange("p (j s) -> p j s", j=4), ACT.Copy).then_inc(S["xe_hi"], 1)
                high(2, 3, 4, 5, 6, 7)
                sigmoid(0)
                high(8, 9)
                mid_high(0)
                high(10, 11)
                sigmoid(1)
                mid_high(1)
                act.wait_ge(S["selT_ps"], n + 2)
                A(selT, ps[:, 4, 0:NTOK], ACT.Copy).then_inc(S["selT"], 1)

            act.wait_ge(S["cntr"], 1)
            act.wait_ge(S["zero"], 1)
            total = run_experts(act, act_pass)
            rows_out(total)

            for t, (_, n) in enumerate(TILES):
                act.wait_ge(S["x3"], t + 1)
                ins = A(h[0:n, t, :], x[0:n, t, :], ACT.Square, accum_out=st[0:n, 60 + t:61 + t])
            ins.then_inc(S["ss4"], 1)
            act.wait_ge(S["ms4"], 1)
            A(st[:, 63:66], st[:, 63:66], ACT.Sqrt).then_inc(S["rt4"], 1)

        @block.vector
        def _(dve):
            chain = [0]

            def link(ins):
                chain[0] += 1
                ins.then_inc(S["chain_v"], 1)
                dve.wait_ge(S["chain_v"], chain[0])

            tt, ts, stt = dve.tensor_tensor, dve.tensor_scalar, dve.scalar_tensor_tensor
            dve.memset(ones[:, :], 1.0)
            dve.memset(xb[:, :, :], 0.0)
            dve.memset(st[:, :], 1.0)
            dve.memset(qbd[:, :, :, :], 0.0).then_inc(S["init"], 1)
            for c, (what, count) in enumerate((("w_lo_v", 4), ("w_lo_p", 2), ("w_used", 4), ("midr", 1), ("acc", 1))):
                dve.memset(mark[:, c:c + 1], 1.0).then_inc(S[what], count)
            dve.wait_ge(S["prm"], 16 * NPRM)
            dve.wait_ge(S["dt"], 1)
            dtb = bc(ld[0:NI, 0:2].unsqueeze(2), [NI, 2, 64])
            tt(st_out[0:NI, 0, :].rearrange("p (g n) -> p g n", g=2), par[0:NI, 0:P].rearrange("p (g n) -> p g n", g=2), dtb, ALU.mult)
            tt(st_out[0:NI, 1, :].rearrange("p (g n) -> p g n", g=2), par[0:NI, P:2 * P].rearrange("p (g n) -> p g n", g=2), dtb, ALU.mult).then_inc(S["rows"], 1)
            dve.wait_ge(S["ss"], 1)
            ts(st[:, 3:6], st[:, 0:3], 1.0 / D, EPS, ALU.mult, ALU.add).then_inc(S["ms"], 1)
            dve.wait_ge(S["rt"], 1)
            link(dve.reciprocal(st[:, 6:9], st[:, 3:6]))
            for t, (_, n) in enumerate(TILES):
                ins = ts(xn[0:n, t, :], x[0:n, t, :], st[0:n, 6 + t:7 + t], None, ALU.mult)
            ins.then_inc(S["xn"], 1)
            dve.wait_ge(S["prmT"], 1)
            link(dve.tensor_copy(prm[:, 0:4, :], ps[:, 0, 0:64].rearrange("p (a i) -> p a i", a=4)))
            link(ts(prm[:, 11, :], prm[:, PA_TH, :], TWO_PI / 4, None, ALU.add))
            link(dve.tensor_copy(prm[:, 12, :], prm[:, PA_TH, :]))
            two = prm[:, 11:13, :]
            kk = prm[:, 13:15, :]
            link(ts(kk, two, 1.0 / TWO_PI, ROUND, ALU.mult, ALU.add))
            link(ts(kk, kk, -ROUND, None, ALU.add))
            link(stt(two, kk, -TP_HI, two, ALU.mult, ALU.add))
            link(stt(two, kk, -TP_LO, two, ALU.mult, ALU.add))
            ts(two, two, PI_IN, -PI_IN, ALU.min, ALU.max).then_inc(S["red"], 1)
            link(dve.tensor_copy(h0[:, :, :], ps[:, 1, 0:2 * P].rearrange("p (r n) -> p r n", r=2)))
            gm4 = bc(gmask.unsqueeze(1), [P, 4, P])
            tt(cT[:, 0, :].rearrange("p (b n) -> p b n", b=4), ps[:, 2, :].rearrange("p (b n) -> p b n", b=4), gm4, ALU.mult)
            stt(cT[:, 1, :].rearrange("p (b n) -> p b n", b=4), ps[:, 3, :].rearrange("p (b n) -> p b n", b=4), -1.0, gm4, ALU.mult, ALU.mult).then_inc(S["crev"], 1)
            for j in range(0, J, 2):
                dve.wait_ge(S["xT_ps"], j + 1)
                ts(accT[:, j, :], ps[:, 4 + j % 4, 0:NTOK], gmx[:, j:j + 1], None, ALU.mult).then_inc(S["xT_d"], 1)
            dve.wait_ge(S["exps"], 1)
            q = lambda n: prm[:, n, :]
            tt(q(PA_AR), q(PA_R), q(PA_C), ALU.mult)
            link(tt(q(PA_AI), q(PA_R), q(PA_S), ALU.mult))
            ts(q(15), q(PA_AR), -1.0, None, ALU.add)
            tt(q(16), q(PA_LR), q(PA_LR), ALU.mult)
            link(tt(q(17), q(PA_LI), q(PA_LI), ALU.mult))
            link(tt(q(16), q(16), q(17), ALU.add))
            dve.reciprocal(q(16), q(16))
            tt(q(18), q(15), q(PA_LR), ALU.mult)
            tt(q(19), q(PA_AI), q(PA_LI), ALU.mult)
            tt(q(20), q(PA_AI), q(PA_LR), ALU.mult)
            link(tt(q(21), q(15), q(PA_LI), ALU.mult))
            tt(q(18), q(18), q(19), ALU.add)
            link(tt(q(20), q(20), q(21), ALU.subtract))
            tt(q(PA_FR), q(18), q(16), ALU.mult)
            link(tt(q(PA_FI), q(20), q(16), ALU.mult))
            v3 = lambda r: bnat[:, r, :].rearrange("p (i c) -> p i c", i=NI)
            fr, fi = (bc(q(n).unsqueeze(2), [P, NI, 16]) for n in (PA_FR, PA_FI))
            s3 = lambda n: ssm_a[:, 2 * n:2 * n + 2, :].rearrange("p a t -> p (a t)").rearrange("p (i c) -> p i c", i=NI)
            s4 = lambda n: ssm_b[:, 2 * n:2 * n + 2, :].rearrange("p a t -> p (a t)").rearrange("p (i c) -> p i c", i=NI)
            tt(s3(0), v3(0), fr, ALU.mult)
            tt(s3(1), v3(1), fi, ALU.mult)
            tt(s4(0), v3(1), fr, ALU.mult)
            link(tt(s4(1), v3(0), fi, ALU.mult))
            for g in range(2):
                rows = slice(64 * g, 64 * g + 64)
                dst = lambda r: xb[rows, r, :].rearrange("p (i g c) -> p i g c", i=NI, g=2)[:, :, g, :]
                tt(dst(0), s3(0)[rows], s3(1)[rows], ALU.subtract)
                ins = tt(dst(1), s4(0)[rows], s4(1)[rows], ALU.add)
            ins.then_inc(S["fdone"], 1)
            dve.wait_ge(S["bT_ps"], 1)
            dve.tensor_copy(bT[:, 0, :], ps[:, 0, :])
            dve.tensor_copy(bT[:, 1, :], ps[:, 1, :]).then_inc(S["bT"], 1)
            dve.wait_ge(S["etab"], 1)
            for i in range(NI):
                b = i % 2
                er, ei = e_tab[:, 0, i, :], e_tab[:, 1, i, :]
                buf = ps[:, 6 + b, :].rearrange("p (r t) -> p r t", r=4)
                dve.wait_ge(S["bu"], i + 1)
                if i >= 1:
                    dve.wait_ge(S["g1"], i)
                tt(ssm_a[:, :, :], buf, bc(er.unsqueeze(1), [P, 4, HALF]), ALU.mult)
                tt(ssm_b[:, 0:2, :], buf[:, 2:4, :], bc(ei.unsqueeze(1), [P, 2, HALF]), ALU.mult)
                tt(ssm_b[:, 2:4, :], buf[:, 0:2, :], bc(ei.unsqueeze(1), [P, 2, HALF]), ALU.mult).then_inc(S["bu_used"], 1)
                dve.wait_ge(S["bu_used"], i + 1)
                tt(ssm_a[:, 0:2, :], ssm_a[:, 0:2, :], ssm_b[:, 0:2, :], ALU.add)
                link(tt(ssm_a[:, 2:4, :], ssm_a[:, 2:4, :], ssm_b[:, 2:4, :], ALU.subtract))
                decay = bc(prm[:, PA_R, i:i + 1], [P, HALF])
                if i >= 2:
                    dve.wait_ge(S["hhi"], i - 1)
                    dve.wait_ge(S["yps"], i - 1)
                dve.tensor_tensor_scan(ssm_g[:, b, 0, 0, :], decay, ssm_a[:, 0, :], 0.0, ALU.mult, ALU.add)
                link(dve.tensor_tensor_scan(ssm_g[:, b, 1, 0, :], decay, ssm_a[:, 2, :], 0.0, ALU.mult, ALU.add))
                gr, gi = ssm_g[:, b, 0, 0, :], ssm_g[:, b, 1, 0, :]
                tt(ssm_b[:, 0, :], gr, er, ALU.mult)
                tt(ssm_b[:, 1, :], gi, er, ALU.mult)
                tt(ssm_b[:, 2, :], gi, ei, ALU.mult)
                link(tt(ssm_b[:, 3, :], gr, ei, ALU.mult))
                tt(ssm_h[:, b, 0, 0:HALF], ssm_b[:, 0, :], ssm_b[:, 2, :], ALU.subtract)
                tt(ssm_h[:, b, 1, 0:HALF], ssm_b[:, 1, :], ssm_b[:, 3, :], ALU.add).then_inc(S["hlo"], 1)
                dve.wait_ge(S["hlo"], i + 1)
                dve.tensor_tensor_scan(ssm_g[:, b, 0, 1, :], decay, ssm_a[:, 1, :], ssm_h[:, b, 0, HALF - 1:HALF], ALU.mult, ALU.add)
                dve.tensor_tensor_scan(ssm_g[:, b, 1, 1, :], decay, ssm_a[:, 3, :], ssm_h[:, b, 1, HALF - 1:HALF], ALU.mult, ALU.add).then_inc(S["g1"], 1)
                if i % 4 == 1 and i >= 4:
                    blk = i // 4 - 1
                    dve.wait_ge(S["yps"], 4 * (blk + 1))
                    stt(yS[:, blk, 0:SEQ], qkvu[:, 12 + blk, 0:SEQ], dsk[:, blk:blk + 1], ps[:, 2 + blk % 2, 0:SEQ], ALU.mult, ALU.add).then_inc(S["yS_ready"], 1)
            dve.wait_ge(S["bus"], 1)
            dve.wait_ge(S["g1"], NI)
            ar, ai = (bc(prm[:, n, :].unsqueeze(2), [P, NI, NB]) for n in (PA_AR, PA_AI))
            hv = hs[:, :, :, :].rearrange("p r i (b t) -> p r i b t", t=NSEQ)
            buv = bus.rearrange("p (i r b t) -> p r i b t", i=NI, r=2, t=NSEQ)
            h0v = h0[:, :, :].rearrange("p r (b i) -> p r i b", b=NB)
            tq = lambda n: (ssm_a, ssm_b)[n // 4][:, n % 4, :].rearrange("p (i b) -> p i b", i=NI)
            for t in range(NSEQ):
                pr, pi = (h0v[:, 0], h0v[:, 1]) if t == 0 else (hv[:, 0, :, :, t - 1], hv[:, 1, :, :, t - 1])
                tt(tq(0), pr, ar, ALU.mult)
                tt(tq(1), pi, ai, ALU.mult)
                tt(tq(2), pi, ar, ALU.mult)
                link(tt(tq(3), pr, ai, ALU.mult))
                tt(tq(4), tq(0), tq(1), ALU.subtract)
                link(tt(tq(5), tq(2), tq(3), ALU.add))
                tt(hv[:, 0, :, :, t], tq(4), buv[:, 0, :, :, t], ALU.add)
                link(tt(hv[:, 1, :, :, t], tq(5), buv[:, 1, :, :, t], ALU.add))
            dve.tensor_copy(sf[:, :, :].rearrange("p r (b i) -> p r i b", b=NB), hv[:, :, :, :, NSEQ - 1]).then_inc(S["hs"], 1)
            dve.wait_ge(S["yps"], NI)
            stt(yS[:, 3, 0:SEQ], qkvu[:, 15, 0:SEQ], dsk[:, 3:4], ps[:, 3, 0:SEQ], ALU.mult, ALU.add).then_inc(S["yS_ready"], 1)
            dve.wait_ge(S["ysps"], 1)
            for blk in range(4):
                ins = stt(yS[:, blk, SEQ:], qkvu[:, 12 + blk, SEQ:], dsk[:, blk:blk + 1], ps[:, 4, NS * blk:NS * blk + NS], ALU.mult, ALU.add)
            ins.then_inc(S["ysv"], 1)
            for hh in range(H + 1):
                if hh < H:
                    b = hh % 2
                    dve.wait_ge(S["s_ps"], hh + 1)
                    link(stt(scb[:, b, :], ps[:, 6 + b, 0:3 * P], SCALE, con[:, C_BP:C_BP + 3 * P], ALU.mult, ALU.add))
                    dve.tensor_reduce(st[:, 10:11], scb[:, b, 0:P], AX, ALU.max)
                    link(dve.tensor_reduce(st[:, 11:12], scb[:, b, P:], AX, ALU.max))
                    ts(st[:, 12 + 2 * b:14 + 2 * b], st[:, 10:12], -1.0, None, ALU.mult).then_inc(S["nm"], 1)
                if hh >= 1:
                    b = (hh - 1) % 2
                    dve.wait_ge(S["ex"], hh)
                    link(dve.reciprocal(st[:, 20 + 2 * b:22 + 2 * b], st[:, 16 + 2 * b:18 + 2 * b]))
                    ts(prb[:, b, 0:P], prb[:, b, 0:P], st[:, 20 + 2 * b:21 + 2 * b], None, ALU.mult)
                    ts(prb[:, b, P:], prb[:, b, P:], st[:, 21 + 2 * b:22 + 2 * b], None, ALU.mult).then_inc(S["pn"], 1)
                    if (hh - 1) % 2 == 1:
                        hp = (hh - 1) // 2
                        dve.wait_ge(S["o_ps"], hh)
                        dve.tensor_copy(aT[:, hp, 0:SEQ], ps[:, 2 + hp % 2, 0:SEQ]).then_inc(S["aT"], 1)
            for half in range(2):
                for n in range(1, 20, 2):
                    dve.wait_ge(S["kt_ps"], 20 * half + n + 1)
                    dve.tensor_copy(kT_s[:, 1, :], ps[:, 5, :]).then_inc(S["ktD"], 1)
                dve.wait_ge(S["ts_ps"], half + 1)
                stt(s_s[:, 0:512], ps[:, 0, :], SCALE, con[:, C_BS:C_BS + 512], ALU.mult, ALU.add)
                at = C_BS + 512 + 160 * half
                link(stt(s_s[:, 512:672], ps[:, 1, 0:160], SCALE, con[:, at:at + 160], ALU.mult, ALU.add))
                link(dve.tensor_reduce(st[:, 23:24], s_s, AX, ALU.max))
                ts(st[:, 24:25], st[:, 23:24], -1.0, None, ALU.mult).then_inc(S["nms"], 1)
                dve.wait_ge(S["exs"], half + 1)
                link(dve.reciprocal(st[:, 26:27], st[:, 25:26]))
                ts(p_s, p_s, st[:, 26:27], None, ALU.mult).then_inc(S["pns"], 1)
            dve.wait_ge(S["pv"], 2)
            pv = ps[:, 3, 0:NB * 32].rearrange("p (b c g t) -> p c b g t", b=NB, c=4, g=2)
            for g in range(2):
                rows = slice(64 * g, 64 * g + 64)
                dst = aT[rows, :, SEQ:].rearrange("p c (b t) -> p c b t", t=NSEQ)
                dve.tensor_copy(dst, pv[rows, :, :, g, :]).then_inc(S["aTs"], 1)
            yf = yS[:, :, :].rearrange("p a t -> p (a t)")
            link(tt(kvg, yf, yf, ALU.mult))
            link(ts(kvg, kvg, G_B, 1.0, ALU.mult, ALU.add))
            tt(kvg, kvg, yf, ALU.mult).then_inc(S["gel1"], 1)
            dve.wait_ge(S["gel2"], 1)
            tt(yf, yf, kvg, ALU.mult).then_inc(S["gg"], 1)
            for b in range(4):
                dve.wait_ge(S["glu"], b + 1)
                if b == 0:
                    dve.wait_ge(S["glu_ps"], 4)
                ins = tt(yS[:, b, :], yS[:, b, :], kvg.rearrange("p (b t) -> p b t", b=4)[:, b, :], ALU.mult)
            link(ins)
            tt(sqs, yS[:, :, :], yS[:, :, :], ALU.mult).then_inc(S["sq"], 1)
            dve.wait_ge(S["sqA"], 1)
            dve.wait_ge(S["sq"], 1)
            tt(aT[:, :, :], aT[:, :, :], bc(gat.unsqueeze(2), [P, 4, NTOK]), ALU.mult)
            tt(yS[:, :, :], yS[:, :, :], bc(gss.unsqueeze(2), [P, 4, NTOK]), ALU.mult).then_inc(S["mix"], 1)
            dve.wait_ge(S["ssq"], 1)
            for t, (_, n) in enumerate(TILES):
                ins = ts(st[0:n, 36 + 2 * t:38 + 2 * t], ps[0:n, 0, 2 * t:2 * t + 2], 1.0 / 512, EPS, ALU.mult, ALU.add)
            ins.then_inc(S["ms2"], 1)
            dve.wait_ge(S["rt2"], 1)
            link(dve.reciprocal(st[:, 42:48], st[:, 36:42]))
            for t, (_, n) in enumerate(TILES):
                dve.wait_ge(S["wo_ps"], t + 1)
                b0 = 4 * (t % 2)
                xv = x[0:n, t, :].rearrange("p (a n) -> p a n", a=2)
                link(stt(xv, ps[0:n, b0:b0 + 2, :], st[0:n, 42 + 2 * t:43 + 2 * t], xv, ALU.mult, ALU.add))
                stt(xv, ps[0:n, b0 + 2:b0 + 4, :], st[0:n, 43 + 2 * t:44 + 2 * t], xv, ALU.mult, ALU.add).then_inc(S["x2"], 1)
            dve.wait_ge(S["ss3"], 1)
            ts(st[:, 51:54], st[:, 48:51], 1.0 / D, EPS, ALU.mult, ALU.add).then_inc(S["ms3"], 1)
            dve.wait_ge(S["rt3"], 1)
            dve.wait_ge(S["gff"], 16)
            link(dve.reciprocal(st[:, 54:57], st[:, 51:54]))
            for t, (_, n) in enumerate(TILES):
                stt(h[0:n, t, :], x[0:n, t, :], st[0:n, 54 + t:55 + t], g_row[0:n, :], ALU.mult, ALU.mult).then_inc(S["h"], 1)
            for j in range(0, J, 2):
                dve.wait_ge(S["hT_ps"], j + 1)
                dve.tensor_copy(accT[:, j, :], ps[:, j, 0:NTOK]).then_inc(S["xT_d"], 1)
            dve.memset(posm, -1.0)
            dve.memset(gate, 0.0)
            link(dve.memset(rt_s[:, :, :, :], 0.0))
            for t, (_, n) in enumerate(TILES):
                dve.wait_ge(S["lg"], 3)
                lg, msk, gt, t8 = rt_s[0:n, t, 0, :], rt_s[0:n, t, 1, :], rt_s[0:n, t, 2, :], top[0:n, t, 0:8]
                link(tt(lg, ps[0:n, 0, 32 * t:32 * t + 32], bro[0:n, :], ALU.add))
                link(dve.max(t8, lg))
                dve.max_index(tidx[0:n, t, :], t8, lg)
                link(ts(top[0:n, t, 8:12], t8[:, 0:4], t8[:, 0:1], None, ALU.subtract))
                dve.tensor_copy(top[0:n, t, 16:20], tidx[0:n, t, 0:4]).then_inc(S["rout"], 1)
            for t, (_, n) in enumerate(TILES):
                dve.wait_ge(S["gex"], t + 1)
                link(dve.reciprocal(top[0:n, t, 21:22], top[0:n, t, 20:21]))
                link(ts(top[0:n, t, 12:16], top[0:n, t, 12:16], top[0:n, t, 21:22], None, ALU.mult))
                o1, o2 = oh[0:n, t, 0], oh[0:n, t, 1]
                link(tt(o1, bc(iota[0:n, 0:NEXP].unsqueeze(1), [n, TOPK, NEXP]), bc(top[0:n, t, 16:20].unsqueeze(2), [n, TOPK, NEXP]), ALU.is_equal))
                link(tt(o2, o1, bc(top[0:n, t, 12:16].unsqueeze(2), [n, TOPK, NEXP]), ALU.mult))
                dve.tensor_reduce(rt_s[0:n, t, 1, :], o1.rearrange("p k e -> p e k"), AX, ALU.add)
                link(dve.tensor_reduce(rt_s[0:n, t, 2, :], o2.rearrange("p k e -> p e k"), AX, ALU.add))
                dve.tensor_copy(gate[0:n, :, t], rt_s[0:n, t, 2, :]).then_inc(S["posm"], 1)
            dve.wait_ge(S["posps"], 1)
            for t, (_, n) in enumerate(TILES):
                link(stt(rt_s[0:n, t, 3, :], ps[0:n, 1, 32 * t:32 * t + 32], 1.0, rt_s[0:n, t, 1, :], ALU.add, ALU.mult))
                link(ts(posm[0:n, :, t], rt_s[0:n, t, 3, :], -1.0, None, ALU.add))
            dve.memset(selT, 0.0).then_inc(S["selT"], 1)
            dve.tensor_copy(cnt[:, :], ps[:, 1, 96:128]).then_inc(S["cntr"], 1)

            def add_back(n):
                for q in range(J // 2):
                    dve.wait_ge(S["comb"], n * (J // 2) + (q + 1))
                    b, pair = 2 * (q % 2), accT[:, 2 * q:2 * q + 2, :]
                    tt(pair, pair, ps[:, b:b + 2, 0:NTOK], ALU.add).then_inc(S["acc"], 1)

            def dve_pass(n, e, first, last):
                def low(*ks):
                    for k in ks:
                        dve.wait_ge(S["w_hi"], n * NPIECE + (k + 1))
                        tt(w_lo[:, k % 4, :], ring_w[:, k % 6, :], w_hi[:, k % 4, :].bitcast(F32), ALU.subtract).then_inc(S["w_lo_v"], 1)

                def mid_low(b):
                    dve.wait_ge(S["mt_hi"], n * 2 + (b + 1))
                    tt(mt_lo[:, 4 * b:4 * b + 4, :], ps[:, 4 + b, :].rearrange("p (m s) -> p m s", m=4), mt_hi[:, 4 * b:4 * b + 4, :].bitcast(F32),
                       ALU.subtract).then_inc(S["mt_lo"], 1)

                def swiglu(b):
                    dve.wait_ge(S["w_used"], n * NPIECE + (4 + 4 * (b + 1)))
                    tt(glu_b, ps[:, 2 * b, :], b1b[:, 512 - 512 * b:1024 - 512 * b], ALU.add)
                    tt(lin[:, b], ps[:, 2 * b + 1, :], b1b[:, DFF + 512 - 512 * b:DFF + 1024 - 512 * b], ALU.add).then_inc(S["swc"], 1)
                    dve.wait_ge(S["swc"], n * 4 + (1 + 2 * b))
                    ts(glu_b, glu_b, LIMIT, None, ALU.min).then_inc(S["glin"], 1)
                    ts(lin[:, b], lin[:, b], LIMIT, -LIMIT, ALU.min, ALU.max)
                    dve.wait_ge(S["sgm"], n * 2 + (b + 1))
                    tt(sig, sig, glu_b, ALU.mult).then_inc(S["swc"], 1)
                    dve.wait_ge(S["swc"], n * 4 + (2 + 2 * b))
                    stt(mid[:, b], lin[:, b], 1.0, sig, ALU.add, ALU.mult).then_inc(S["midr"], 1)

                dve.wait_ge(S["selT_ps"], n + 1)
                ib = bc(iota[:, bass.ds(first, CAP)].unsqueeze(1), [P, 3, CAP])
                pb = bc(posm[:, bass.ds(e, 1), :].rearrange("p e t -> p (e t)").unsqueeze(2), [P, 3, CAP])
                gb = bc(gate[:, bass.ds(e, 1), :].rearrange("p e t -> p (e t)").unsqueeze(2), [P, 3, CAP])
                tt(sel, ib, pb, ALU.is_equal).then_inc(S["sel"], 1)
                low(0)
                for a in range(2):
                    dve.wait_ge(S["xe_hi"], n * 2 + (a + 1))
                    tt(xe_lo[:, 4 * a:4 * a + 4, :], ps[:, 4 + a, :].rearrange("p (j s) -> p j s", j=4), xe_hi[:, 4 * a:4 * a + 4, :].bitcast(F32),
                       ALU.subtract).then_inc(S["xe_lo"], 1)
                dve.wait_ge(S["sel"], n * 2 + 1)
                tt(selg, sel, gb, ALU.mult).then_inc(S["sel"], 1)
                low(2, 3, 5, 6)
                dve.wait_ge(S["b1b"], n * 16 + 16)
                swiglu(0)
                low(8)
                low(9)
                mid_low(0)
                swiglu(1)
                low(11)
                mid_low(1)
                add_back(n)

            dve.wait_ge(S["cntr"], 1)
            dve.wait_ge(S["acc0"], J)
            dve.memset(ps[:, 6:8, :], 0.0).then_inc(S["zero"], 1)
            total = run_experts(dve, dve_pass)
            add_back(total)
            for t, (_, n) in enumerate(TILES):
                dve.wait_ge(S["fin_ps"], t + 1)
                xv = x[0:n, t, :].rearrange("p (a n) -> p a n", a=2)
                b0 = 2 * t
                tt(xv, xv, ps[0:n, b0:b0 + 2, :], ALU.add).then_inc(S["x3"], 1)
            dve.wait_ge(S["ss4"], 1)
            ts(st[:, 63:66], st[:, 60:63], 1.0 / D, EPS, ALU.mult, ALU.add).then_inc(S["ms4"], 1)
            dve.wait_ge(S["rt4"], 1)
            dve.wait_ge(S["gfi"], 16)
            dve.reciprocal(st[:, 66:69], st[:, 63:66]).then_inc(S["ms4"], 1)
            dve.wait_ge(S["ms4"], 2)
            for t, (_, n) in enumerate(TILES):
                stt(x[0:n, t, :], x[0:n, t, :], st[0:n, 66 + t:67 + t], g_row[0:n, :], ALU.mult, ALU.mult).then_inc(S["yfin"], 1)

        @block.tensor
        def _(pe):
            mm, tp = pe.matmul, pe.transpose

            pe.wait_ge(S["con"], 16)
            pe.wait_ge(S["prm"], 16 * NPRM)
            for r in range(2):
                for b in range(4):
                    tp(ps[:, 2 + r, P * b:P * b + P], cnat[:, r, b, :], ident)
                tp(ps[:, 1, P * r:P * r + P], h0row[:, r, :], ident)
            pe.wait_ge(S["rows"], 1)
            for a, src in enumerate((par[0:NI, 0:P], par[0:NI, P:2 * P], st_out[0:NI, 0, :], st_out[0:NI, 1, :])):
                ins = tp(ps[:, 0, NI * a:NI * a + NI], src, ident[0:NI, 0:NI])
            ins.then_inc(S["prmT"], 1)
            pe.wait_ge(S["xn"], 1)
            for j in range(J):
                if j >= 4:
                    pe.wait_ge(S["xT_a"] if j % 2 else S["xT_d"], j // 2 - 1)
                for t, (t0, n) in enumerate(TILES):
                    ins = tp(ps[:, 4 + j % 4, t0:t0 + n], xn[0:n, t, j::J], ident[0:n, 0:n])
                ins.then_inc(S["xT_ps"], 1)
            blocks = [12, 13, 14, 15] + list(range(12))

            def project(n):
                c = blocks[n]
                if n == 0:
                    pe.wait_ge(S["win0"], 16)
                    pe.wait_ge(S["xT_a"], 4)
                    pe.wait_ge(S["xT_d"], 4)
                if n == 4:
                    pe.wait_ge(S["win1"], 48)
                if n >= 2:
                    pe.wait_ge(S["proj_ev"], n - 1)
                for j in range(J):
                    ins = mm(ps[:, 4 + n % 2, 0:NTOK], w_in[:, c // 4, j, P * (c % 4):P * (c % 4) + P], accT[:, j, :],
                             start=(j == 0), stop=(j == J - 1))
                ins.then_inc(S["proj"], 1)

            for n in range(4):
                project(n)
            pe.wait_ge(S["crev"], 1)
            pe.wait_ge(S["fdone"], 1)
            for r in range(2):
                for b in range(4):
                    ins = tp(ps[:, r, P * b:P * b + P], xb[:, r, P * b:P * b + P], ident)
            ins.then_inc(S["bT_ps"], 1)
            pe.wait_ge(S["bT"], 1)
            pe.wait_ge(S["proj_ev"], 4)

            def bu(i):
                rows = slice(32 * (i % 4), 32 * (i % 4) + 32)
                blk = i // 4
                if i >= 2:
                    pe.wait_ge(S["bu_used"], i - 1)
                for r in range(2):
                    w = bT[rows, r, P * blk:P * blk + P]
                    at = 64 * (i // 2) + NS * r
                    mm(ps[:, i % 2, at:at + NS], w, qkvu[rows, 12 + blk, SEQ:], start=True, stop=True)
                    ins = mm(ps[:, 6 + i % 2, SEQ * r:SEQ * r + SEQ], w, qkvu[rows, 12 + blk, 0:SEQ], start=True, stop=True)
                ins.then_inc(S["bu"], 1)

            def c_h(i):
                blk, q = i // 4, 32 * (i % 4)
                if blk >= 2 and i % 4 == 0:
                    pe.wait_ge(S["yS_ready"], blk - 1)
                pe.wait_ge(S["hlo"], i + 1)
                pe.wait_ge(S["hhi"], i + 1)
                for r in range(2):
                    ins = mm(ps[q:q + 32, 2 + blk % 2, 0:SEQ], cT[:, r, P * blk + q:P * blk + q + 32], ssm_h[:, i % 2, r, :],
                             start=(r == 0), stop=(r == 1), skip_group_check=True)
                ins.then_inc(S["yps"], 1)

            for i in range(NI):
                bu(i)
                if i < 12:
                    project(4 + i)
                if i >= 1:
                    c_h(i - 1)
            c_h(NI - 1)

            pe.wait_ge(S["proj_ev"], 16)
            for n in range(6):
                a, t = divmod(n, 3)
                t0, rows = TILES[t]
                if n >= 2:
                    pe.wait_ge(S["kvr"], n - 1)
                for b in range(4):
                    ins = tp(ps[0:rows, 4 + n % 2, P * b:P * b + P], qkvu[:, 4 + 4 * a + b, t0:t0 + rows], ident)
                ins.then_inc(S["kvr_ps"], 1)
            pe.wait_ge(S["kvr"], 6)

            pe.wait_ge(S["hs"], 1)
            pe.wait_ge(S["hfin"], 1)
            for i in range(NI):
                blk, q = i // 4, 32 * (i % 4)
                for r in range(2):
                    ins = mm(ps[q:q + 32, 4, NS * blk:NS * blk + NS], cT[:, r, P * blk + q:P * blk + q + 32], hs[:, r, i, :],
                             start=(r == 0), stop=(r == 1), skip_group_check=True)
            ins.then_inc(S["ysps"], 1)
            for r in range(2):
                tp(ps[0:NI, 5, P * r:P * r + P], hf[:, r, :], ident)
                ins = tp(ps[:, 5, SEQ + P * r:SEQ + P * r + P], sf[:, r, :], ident)
            ins.then_inc(S["sto_ps"], 1)

            pe.wait_ge(S["bu_used"], NI)
            pe.wait_ge(S["bus"], 1)
            for hh in range(H + 1):
                if hh < H:
                    b, hp, rows = hh % 2, hh // 2, slice(64 * (hh % 2), 64 * (hh % 2) + 64)
                    if hh >= 2:
                        pe.wait_ge(S["nm"], hh - 1)
                    mm(ps[:, 6 + b, 0:P], qkvu[rows, hp, 0:P], qkvu[rows, 4 + hp, 0:P], start=True, stop=True)
                    mm(ps[:, 6 + b, P:3 * P], qkvu[rows, hp, P:SEQ], qkvu[rows, 4 + hp, 0:SEQ], start=True, stop=True).then_inc(S["s_ps"], 1)
                if hh >= 1:
                    g = hh - 1
                    b, hp, rows = g % 2, g // 2, slice(64 * (g % 2), 64 * (g % 2) + 64)
                    pe.wait_ge(S["pn"], g + 1)
                    tp(ps[:, b, 0:P], prb[:, b, 0:P], ident)
                    tp(ps[:, b, P:2 * P], prb[:, b, P:2 * P], ident)
                    tp(ps[:, b, 2 * P:3 * P], prb[:, b, 2 * P:3 * P], ident).then_inc(S["pt_ps"], 1)
                    pe.wait_ge(S["pt"], g + 1)
                    if g == 0:
                        pe.wait_ge(S["yS_ready"], 4)
                    if g >= 4 and g % 2 == 0:
                        pe.wait_ge(S["aT"], hp - 1)
                    mm(ps[rows, 2 + hp % 2, 0:SEQ], kv_rows[:, 1, 0, 64 * g:64 * g + 64], ptb[:, b, 0:SEQ], start=True, stop=False, skip_group_check=True)
                    mm(ps[rows, 2 + hp % 2, P:SEQ], kv_rows[:, 1, 1, 64 * g:64 * g + 64], ptb[:, b, SEQ:], start=False, stop=True, skip_group_check=True).then_inc(S["o_ps"], 1)
            pe.wait_ge(S["aT"], 4)
            pe.wait_ge(S["qbd"], 1)
            pe.wait_ge(S["ysv"], 1)
            pe.wait_ge(S["sto"], 1)

            for half in range(2):
                def keys(n):
                    b4, rt = divmod(n, 5)
                    m = 20 * half + n
                    b = 4 * half + b4
                    if rt == 0:
                        pe.wait_ge(S[f"kload{b % 2}"], 80 * (b // 2 + 1))
                    if m >= 2:
                        pe.wait_ge(S["ktD"] if n % 2 else S["ktA"], m // 2)
                    for hp in range(4):
                        ins = tp(ps[:, 4 + n % 2, P * hp:P * hp + P], k_cache[:, b % 2, 512 * rt + P * hp:512 * rt + P * hp + P], ident)
                    ins.then_inc(S["kt_ps"], 1)

                keys(0)
                for n in range(20):
                    if n + 1 < 20:
                        keys(n + 1)
                    b4, rt = divmod(n, 5)
                    pe.wait_ge(S["ktD"] if n % 2 else S["ktA"], 10 * half + n // 2 + 1)
                    if n == 0 and half == 1:
                        pe.wait_ge(S["pts"], 1)
                    for hp in range(4):
                        at = P * (rt % 4) + 32 * b4 + 8 * hp
                        mm(ps[:, 6 + rt // 4, at:at + 8], kT_s[:, n % 2, P * hp:P * hp + P], qbd[:, hp, 4 * half + b4, :], start=True, stop=True)
                for hp in range(4):
                    dst = ps[0:NS, 7, P:2 * P].rearrange("p (b c n) -> p b c n", b=4, c=4)[:, :, hp, :]
                    ins = mm(dst, qkvu[:, 4 + hp, SEQ:], qbd[:, hp, 4 * half:4 * half + 4, :], start=True, stop=True)
                ins.then_inc(S["st_ps"], 1)
                pe.wait_ge(S["stE"], half + 1)
                for rt in range(5):
                    tp(ps[:, rt // 4, P * (rt % 4):P * (rt % 4) + P], sT[:, P * rt:P * rt + P], ident)
                tp(ps[:, 1, P:P + NS], sT[0:NS, 640:768], ident[0:NS, 0:NS]).then_inc(S["ts_ps"], 1)
                pe.wait_ge(S["pns"], half + 1)
                for rt in range(5):
                    tp(ps[:, 6 + rt // 4, P * (rt % 4):P * (rt % 4) + P], p_s[:, P * rt:P * rt + P], ident)
                tp(ps[0:NS, 7, P:2 * P], p_s[:, 640:672], ident).then_inc(S["pts_ps"], 1)
                pe.wait_ge(S["pts"], half + 1)
                for b4 in range(4):
                    pe.wait_ge(S[f"vload{b4}"], 80 * (half + 1))
                    for hp in range(4):
                        c0 = 32 * b4 + 8 * hp
                        dst = ps[:, 3, 128 * half + c0:128 * half + c0 + 8]
                        for rt in range(5):
                            mm(dst, v_cache[:, b4, 512 * rt + P * hp:512 * rt + P * hp + P], p_T[:, P * rt + c0:P * rt + c0 + 8],
                               start=(rt == 0), stop=False)
                        ins = mm(dst, kv_rows[0:NS, 1, 2, P * hp:P * hp + P], p_T[0:NS, 640 + c0:640 + c0 + 8], start=False, stop=True)
                ins.then_inc(S["pv"], 1)
            pe.wait_ge(S["wglu"], 32)
            pe.wait_ge(S["gg"], 1)
            for ob in range(4):
                for kb in range(4):
                    ins = mm(ps[:, 4 + ob, 0:NTOK], w_glu[:, kb, P * ob:P * ob + P], yS[:, kb, :], start=(kb == 0), stop=(kb == 3))
                ins.then_inc(S["glu_ps"], 1)
            pe.wait_ge(S["sto"], 1)
            pe.wait_ge(S["sqA"], 1)
            for t, (t0, n) in enumerate(TILES):
                for a, sq in enumerate((sqa, sqs)):
                    for kb in range(4):
                        ins = mm(ps[0:n, 0, 2 * t + a:2 * t + a + 1], sq[:, kb, t0:t0 + n], ones[:, 0:1], start=(kb == 0), stop=(kb == 3))
            ins.then_inc(S["ssq"], 1)
            pe.wait_ge(S["wout"], 16)
            pe.wait_ge(S["mix"], 1)
            pe.wait_ge(S["ms2"], 1)
            for t, (t0, n) in enumerate(TILES):
                b0 = 4 * (t % 2)
                if t == 2:
                    pe.wait_ge(S["x2"], 1)
                for a, src in enumerate((aT, yS)):
                    for kb in range(4):
                        for c in range(2):
                            ins = mm(ps[0:n, b0 + 2 * a + c, :], src[:, kb, t0:t0 + n], w_out[:, 4 * a + kb, 512 * c:512 * c + 512],
                                     start=(kb == 0), stop=(kb == 3))
                ins.then_inc(S["wo_ps"], 1)
            pe.wait_ge(S["h"], 3)
            for j in range(J):
                for t, (t0, n) in enumerate(TILES):
                    ins = tp(ps[:, j, t0:t0 + n], h[0:n, t, j::J], ident[0:n, 0:n])
                ins.then_inc(S["hT_ps"], 1)
            pe.wait_ge(S["xT_a"], 8)
            pe.wait_ge(S["xT_d"], 8)
            for t, (t0, n) in enumerate(TILES):
                for j in range(J):
                    ins = mm(ps[0:n, 0, 32 * t:32 * t + 32], accT[:, j, t0:t0 + n], wr[:, j, :], start=(j == 0), stop=(j == J - 1))
                ins.then_inc(S["lg"], 1)
            pe.wait_ge(S["posm"], 3)
            for t, (t0, n) in enumerate(TILES):
                for u in range(t + 1):
                    m = TILES[u][1]
                    w = tri[0:m, 0:n] if u == t else ones[0:m, 0:n]
                    mm(ps[0:n, 1, 32 * t:32 * t + 32], w, rt_s[0:m, u, 1, :], start=(u == 0), stop=(u == t))
            for u in range(3):
                m = TILES[u][1]
                ins = mm(ps[:, 1, 96:128], ones[0:m, :], rt_s[0:m, u, 1, :], start=(u == 0), stop=(u == 2))
                if u == 0:
                    ins.then_inc(S["selT_ps"], 1)
            ins.then_inc(S["posps"], 1)
            for t, (t0, n) in enumerate(TILES):
                ins = tp(ps[0:NEXP, 4, t0:t0 + n], rt_s[0:n, t, 2, :], ident[0:n, 0:n])
            ins.then_inc(S["gT_ps"], 1)
            pe.wait_ge(S["gT"], 1)
            pe.wait_ge(S["b2"], 16)
            for j in range(J):
                if j >= 2:
                    pe.wait_ge(S["acc0"], j - 1)
                mm(ps[:, 6 + j % 2, 0:NTOK], b2_rows[:, P * j:P * j + P], gT[:, :], start=True, stop=True).then_inc(S["b2ps"], 1)
            pe.wait_ge(S["cntr"], 1)
            pe.wait_ge(S["acc0"], J)

            def sum_back(n):
                pe.wait_ge(S["yr"], n + 1)
                pe.wait_ge(S["selT"], n + 1)
                for j in range(J):
                    if j % 2 == 0 and j >= 4:
                        pe.wait_ge(S["acc"], n * (J // 2) + j // 2)
                    ins = mm(ps[:, j % 4, 0:NTOK], y[:, P * j:P * j + P], selT, start=True, stop=True)
                    if j % 2:
                        ins.then_inc(S["comb"], 1)

            def pe_pass(n, e, first, last):
                def three(out, x_hi, x_lo, w, start, stop):
                    for c, o in enumerate(out):
                        mm(o, x_hi, w[0][c], start=start, stop=False)
                    for c, o in enumerate(out):
                        mm(o, x_hi, w[1][c], start=False, stop=False)
                    for c, o in enumerate(out):
                        ins = mm(o, x_lo, w[0][c], start=False, stop=stop)
                    return ins

                def first_product(k):
                    wait_low(pe, n, k)
                    b = k // 4
                    for jj in range(2):
                        j = 2 * (k % 4) + jj
                        w = [[t[:, k % 4, 1024 * jj + 512 * g:1024 * jj + 512 * g + 512] for g in range(2)] for t in (w_hi, w_lo)]
                        ins = three([ps[:, 2 * b + g, :] for g in range(2)], xe_hi[:, j, :], xe_lo[:, j, :], w, j == 0, j == J - 1)
                    ins.then_inc(S["w_used"], 1)

                def mid_transposed(b):
                    pe.wait_ge(S["midr"], n * 2 + (b + 2))
                    for m in range(4):
                        op = mm if m == 0 else tp
                        ins = op(ps[:, 4 + b, CAP * m:CAP * m + CAP], mid[:, b, P * m:P * m + P], ident)
                    ins.then_inc(S["mt_ps"], 1)

                def second_product(k):
                    wait_low(pe, n, k)
                    for mm_ in range(2):
                        m = 2 * (k - 8) + mm_
                        w = [[t[:, k % 4, 1024 * mm_ + 512 * c:1024 * mm_ + 512 * c + 512] for c in range(2)] for t in (w_hi, w_lo)]
                        ins = three([ps[:, 6 + c, :] for c in range(2)], mt_hi[:, m, :], mt_lo[:, m, :], w, m == 0, m == J - 1)
                    ins.then_inc(S["w_used"], 1)

                pe.wait_ge(S["selT"], n + 1)
                pe.wait_ge(S["sel"], n * 2 + 1)
                for a in range(2):
                    for j in range(4 * a, 4 * a + 4):
                        for t, (t0, k) in enumerate(TILES):
                            ins = mm(ps[:, 4 + a, CAP * (j % 4):CAP * (j % 4) + CAP], h[0:k, t, j::J], sel[0:k, t, :], start=(t == 0), stop=(t == 2))
                    ins.then_inc(S["gath"], 1)
                pe.wait_ge(S["xe_lo"], n * 2 + 1)
                pe.wait_ge(S["acc"], n * (J // 2) + 1)
                first_product(0)
                first_product(1)
                pe.wait_ge(S["xe_lo"], n * 2 + 2)
                first_product(2)
                first_product(3)
                first_product(4)
                first_product(5)
                first_product(6)
                mid_transposed(0)
                first_product(7)
                pe.wait_ge(S["mt_lo"], n * 2 + 1)
                pe.wait_ge(S["yr"], n + 1)
                second_product(8)
                second_product(9)
                mid_transposed(1)
                sum_back(n)
                pe.wait_ge(S["sel"], n * 2 + 2)
                for t, (t0, k) in enumerate(TILES):
                    op = mm if t == 0 else tp
                    ins = op(ps[:, 4, t0:t0 + k], selg[0:k, t, :], ident[0:k, 0:k])
                ins.then_inc(S["selT_ps"], 1)
                pe.wait_ge(S["mt_lo"], n * 2 + 2)
                second_product(10)
                second_product(11)

            pe.wait_ge(S["zero"], 1)
            total = run_experts(pe, pe_pass)
            pe.wait_ge(S["acc"], total * (J // 2) + 1)
            sum_back(total)
            pe.wait_ge(S["acc"], total * (J // 2) + (J // 2 + 1))
            for t, (t0, n) in enumerate(TILES):
                for j in range(J):
                    ins = tp(ps[0:n, 2 * t + j // 4, P * (j % 4):P * (j % 4) + P], accT[:, j, t0:t0 + n], ident)
                ins.then_inc(S["fin_ps"], 1)


_INS = """x_prompt x_sample cache_k cache_v state_ssm_re state_ssm_im norm_mix_g w_in attn_out_norm_g
    ssm_a_re ssm_a_im ssm_log_dt ssm_b_re ssm_b_im ssm_c_re ssm_c_im ssm_d w_glu b_glu ssm_out_norm_g
    w_out norm_ffn_g w_router b_router w_moe1 b_moe1 w_moe2 b_moe2 norm_final_g""".split()
_OUTS = [("y_p", (1, SEQ, D)), ("y_s", (NB, NSEQ, D)), ("k_p", (1, 1, SEQ, H, HD)), ("v_p", (1, 1, SEQ, H, HD)),
         ("re_p", (1, 1, 32, 64)), ("im_p", (1, 1, 32, 64)), ("k_s", (1, NB, NSEQ, H, HD)), ("v_s", (1, NB, NSEQ, H, HD)),
         ("re_s", (1, NB, 32, 64)), ("im_s", (1, NB, 32, 64))]


def kernel(**inputs):
    import numpy as _np
    import concourse.bacc as _bacc
    from concourse import mybir as _mybir
    from concourse.bass_utils import run_bass_kernel_spmd as _run

    nc = _bacc.Bacc("TRN2", target_bir_lowering=False, num_devices=1, dynamic_dma_scratch_size=1024)
    arrays, ins, outs = {}, {}, {}
    for name in _INS + ["con"]:
        a = constants() if name == "con" else _np.ascontiguousarray(inputs[name])
        arrays[f"in_{name}_dram"] = a
        ins[name] = nc.dram_tensor(f"in_{name}_dram", a.shape, _mybir.dt.from_np(a.dtype), kind="ExternalInput").ap()
    for name, shape in _OUTS:
        outs[name] = nc.dram_tensor(f"out_{name}_dram", shape, _mybir.dt.float32, kind="ExternalOutput").ap()
    decoder_step(nc, ins, outs)
    r = _run(nc, [arrays], core_ids=[0])
    return tuple(r.results[0][f"out_{name}_dram"] for name, _ in _OUTS)
```

```python
from contextlib import ExitStack

import numpy as np

import concourse.bass as bass
from concourse import mybir

F32 = mybir.dt.float32
I32 = mybir.dt.int32
U32 = mybir.dt.uint32
FR = mybir.dt.float32r
ALU = mybir.AluOpType
ACT = mybir.ActivationFunctionType
AX = mybir.AxisListType.X

P = 128
D = 1024
J = D // P
SEQ, NB, NSEQ = 256, 8, 4
NS = NB * NSEQ
NTOK = SEQ + NS
TILES = [(0, P), (P, P), (SEQ, NS)]
H, HD = 8, 64
SCALE = HD ** -0.5
PAST = 1024
NEXP, TOPK, DFF = 32, 4, 1024
CAP = 128
CHUNKS = -(-NTOK // CAP)
NI = 16
HALF = SEQ // 2
EPS = 1e-5
ALPHA, LIMIT = 1.702, 7.0
NEG = -1e30
TWO_PI = 6.283185307179586
TP_HI = 6.28125
TP_LO = TWO_PI - TP_HI
ROUND = 1.5 * 2.0 ** 23
PI_IN = 3.1415925
G_A = 0.7978845608028654 * 2.0
G_B = 0.044715
NPIECE = 12

C_ID, C_TRI, C_BP, C_BS, C_IOTA, C_GM = 0, 128, 256, 640, 1472, 1856
C_ALL = 1984


def window_bias(delta):
    n = (((delta >= 0) & (delta <= 128)).astype(int)
         + ((delta >= 0) & (delta <= 512) & (delta % 4 == 0))
         + ((delta >= 0) & (delta <= 2048) & (delta % 16 == 0)))
    return np.where(n > 0, np.log(np.maximum(n, 1)), NEG)


def constants():
    c = np.zeros((P, C_ALL), np.float32)
    p = np.arange(P)[:, None]
    f = np.arange(P)[None, :]
    c[:, C_ID:C_ID + P] = p == f
    c[:, C_TRI:C_TRI + P] = p < f
    c[:, C_BP:C_BP + P] = window_bias(p - f)
    c[:, C_BP + P:C_BP + 3 * P] = window_bias(P + p - np.arange(SEQ)[None, :])
    qpos = PAST + p % NSEQ
    r = np.arange(P)
    for rt in range(4):
        c[:, C_BS + rt * P:C_BS + (rt + 1) * P] = window_bias(qpos - (512 + 4 * r + rt)[None, :])
    for half in range(2):
        at = C_BS + 512 + 160 * half
        c[:, at:at + P] = window_bias(qpos - (16 * (r % 32) + r // 32)[None, :])
        s = np.arange(NS)[None, :]
        same = (half * 4 + p // 32) == s // NSEQ
        c[:, at + P:at + 160] = np.where(same, window_bias(qpos - (PAST + s % NSEQ)), NEG)
    c[:, C_IOTA:C_IOTA + 384] = np.arange(384)
    c[:, C_GM:C_GM + P] = (f // 16) % 2 == p // 64
    return c


def decoder_step(nc, I, O):
    with ExitStack() as ctx:
        def sb(name, shape, dt=F32):
            return ctx.enter_context(nc.sbuf_tensor(name, shape, dt))

        def sem(name):
            return ctx.enter_context(nc.semaphore(name))

        ring = sb("ring", [P, 6, 4096])
        ring_at = nc.sbuf_base - 6 * 4096 * 4
        tmp = sb("tmp", [P, 4096])
        ring_w = ring[:, 0:3, :].rearrange("p s n -> p (s n)").rearrange("p (s n) -> p s n", s=6)
        w_in = ring[:, 0:4, :].rearrange("p s n -> p (s n)").rearrange("p (g j n) -> p g j n", g=4, j=J)
        kv = ring[:, 0:4, :].rearrange("p s n -> p (s n)")
        k_cache = kv[:, 0:2 * 2560].rearrange("p (s n) -> p s n", s=2)
        v_cache = kv[:, 2 * 2560:6 * 2560].rearrange("p (s n) -> p s n", s=4)
        w_out = ring[:, 4:6, :].rearrange("p s n -> p (s n)").rearrange("p (j n) -> p j n", j=J)

        con = sb("con", [P, C_ALL])
        ident = con[:, C_ID:C_ID + P]
        tri = con[:, C_TRI:C_TRI + P]
        iota = con[:, C_IOTA:C_IOTA + 384]
        gmask = con[:, C_GM:C_GM + P]
        x = sb("x", [P, 3, D])
        accT = sb("accT", [P, J, NTOK])
        uni = sb("uni", [P, 9440])
        uni_at = nc.sbuf_base - 9440 * 4
        qkvu = uni[:, 0:16 * NTOK].rearrange("p (c t) -> p c t", c=16)
        kT4 = uni[:, 4608:8704].rearrange("p (b c n) -> p b c n", b=2, c=4)
        kT1 = kv[:, 6 * 2560:6 * 2560 + 1024].rearrange("p (b c n) -> p b c n", b=2, c=4)
        xn = uni[:, 0:3 * D].rearrange("p (t d) -> p t d", t=3)
        e_tab = uni[:, 4608:8704].rearrange("p (r i t) -> p r i t", r=2, i=NI)
        h = uni[:, 0:3072].rearrange("p (t d) -> p t d", t=3)
        o = 3072
        sel = uni[:, o:o + 384].rearrange("p (t s) -> p t s", t=3)
        selg = uni[:, o + 384:o + 768].rearrange("p (t s) -> p t s", t=3)
        glu_b = uni[:, o + 768:o + 1280]
        sig = uni[:, o + 1280:o + 1792]
        lin = uni[:, o + 1792:o + 2816].rearrange("p (b n) -> p b n", b=2)
        mid = uni[:, o + 2816:o + 3840].rearrange("p (b n) -> p b n", b=2)
        posm = uni[:, o + 3840:o + 3936].rearrange("p (e t) -> p e t", e=NEXP)
        gate = uni[:, o + 3936:o + 4032].rearrange("p (e t) -> p e t", e=NEXP)
        o += 4032
        b2_rows = uni[0:NEXP, o:o + D]
        g_row = con[:, C_BP:C_BP + D]

        e_tmp = tmp[:, 0:2048].rearrange("p (a i t) -> p a i t", a=2, i=NI)
        scb = tmp[:, 0:768].rearrange("p (b n) -> p b n", b=2)
        prb = tmp[:, 768:1536].rearrange("p (b n) -> p b n", b=2)
        ptb = tmp[:, 1536:2304].rearrange("p (b n) -> p b n", b=2)
        s_s = tmp[:, 768:1440]
        p_s = tmp[:, 1440:2112]
        p_T = tmp[:, 2112:2880]
        qz = tmp[:, 2880:3904].rearrange("p (c b n) -> p c b n", c=4, b=NB)
        o_s = [tmp[:, 0:512], tmp[:, 768:1280]]
        kv_rows = sb("kv_rows", [P, 2, 3, 512])
        b1b = kv_rows[:, :, :, :].rearrange("p a t n -> p (a t n)")[:, 0:2 * DFF]
        yS = sb("yS", [P, 4, NTOK])
        y_at = nc.sbuf_base - 4 * NTOK * 4
        aT = sb("aT", [P, 4, NTOK])
        w_glu = sb("w_glu", [P, 4, 512])
        KB = 1024
        w_hi = nc.alloc_sbuf_tensor_at("w_hi", [P, 4, 2048], FR, offset=ring_at + 48 * KB)
        w_lo = nc.alloc_sbuf_tensor_at("w_lo", [P, 4, 2048], FR, offset=ring_at + 80 * KB)
        xe_hi = nc.alloc_sbuf_tensor_at("xe_hi", [P, J, CAP], FR, offset=y_at)
        xe_lo = nc.alloc_sbuf_tensor_at("xe_lo", [P, J, CAP], FR, offset=y_at + 4 * KB)
        y_hi = nc.alloc_sbuf_tensor_at("y_hi", [P, D], FR, offset=uni_at + 4 * o)
        y_lo = nc.alloc_sbuf_tensor_at("y_lo", [P, D], FR, offset=uni_at + 4 * (o + D))
        selT = nc.alloc_sbuf_tensor_at("selT", [P, NTOK], FR, offset=uni_at + 4 * (o + 2 * D))
        mt_hi = nc.alloc_sbuf_tensor_at("mt_hi", [P, J, CAP], FR, offset=y_at + 8 * KB)
        mt_lo = nc.alloc_sbuf_tensor_at("mt_lo", [P, J, CAP], FR, offset=y_at + 12 * KB)
        par = sb("par", [P, 256])
        ld = sb("ld", [P, 4])
        prm = sb("prm", [P, 24, NI])
        PA_LR, PA_LI, PA_RD, PA_TH, PA_R, PA_C, PA_S, PA_AR, PA_AI, PA_FR, PA_FI = range(11)
        s5 = ring[:, 4:6, :].rearrange("p s n -> p (s n)")
        s5_at = [0]

        def s5_buf(n):
            s5_at[0] += n
            return s5[:, s5_at[0] - n:s5_at[0]]

        bnat = s5_buf(512).rearrange("p (r n) -> p r n", r=2)
        xb = tmp[:, 2048:3072].rearrange("p (r n) -> p r n", r=2)
        cnat = tmp[:, 3072:4096].rearrange("p (r b n) -> p r b n", r=2, b=4)
        bT = s5_buf(1024).rearrange("p (r n) -> p r n", r=2)
        cT = s5_buf(1024).rearrange("p (r n) -> p r n", r=2)
        h0row = sb("h0row", [P, 2, P])
        h0 = s5_buf(256).rearrange("p (r n) -> p r n", r=2)
        hs = s5_buf(1024).rearrange("p (r i n) -> p r i n", r=2, i=NI)
        bus = bT.rearrange("p r n -> p (r n)")
        e_tmp_v = s5[:, s5_at[0]:s5_at[0] + 2048].rearrange("p (a n) -> p a n", a=2)
        ssm_a = s5_buf(512).rearrange("p (a t) -> p a t", a=4)
        ssm_b = s5_buf(512).rearrange("p (a t) -> p a t", a=4)
        ssm_g = s5_buf(1024).rearrange("p (b r a t) -> p b r a t", b=2, r=2, a=2)
        ssm_h = s5_buf(1024).rearrange("p (b r t) -> p b r t", b=2, r=2)
        ssm_p = s5_buf(512).rearrange("p (a t) -> p a t", a=4)
        hf = sb("hf", [P, 2, NI])
        sf = h0row
        st_out = sb("st_out", [P, 4, P])
        wr = sb("wr", [P, J, NEXP])
        vec = sb("vec", [P, 64])
        gmx, dsk, bgl, gat, gss = (vec[:, 0:8], vec[:, 8:12], vec[:, 12:16], vec[:, 16:20], vec[:, 20:24])
        bro = sb("bro", [P, NEXP])
        ones = sb("ones", [P, P])
        kvg = uni[:, 4608:5760]
        sqa = uni[:, 5760:6912].rearrange("p (b t) -> p b t", b=4)
        sqs = uni[:, 6912:8064].rearrange("p (b t) -> p b t", b=4)
        st = sb("st", [P, 96])
        mark = sb("mark", [P, 8])
        gslot = mark[:, 7:8]
        gT = sb("gT", [NEXP, NTOK])
        rt_s = sb("rt_s", [P, 3, 6, NEXP])
        top = sb("top", [P, 3, 32])
        tidx = sb("tidx", [P, 3, 8], U32)
        oh = sb("oh", [P, 3, 2, TOPK, NEXP])
        cnt = sb("cnt", [P, NEXP], I32)
        ps = ctx.enter_context(nc.psum_tensor("ps", [P, 8, 512], F32))

        names = """x con prm win0 win1 wglu wout late gff gfi kload0 kload1 vload0 vload1 vload2 vload3 out ss ms
            rt xn rows dt prmT exps red crev xT_ps xT_d xT_a proj proj_ev etab fdone bT_ps bT bu bu_used
            hlo g1 hhi yps bus hs ysps yS_ready kvr_ps kvr qbd s_ps nm ex pn pt_ps pt o_ps aT kt_ps ktA ktD
            nms exs pns pts_ps pts pv aTs sto_ps sto hfin gel1 gel2 gg glu_ps glu sq sqA ssq ms2 rt2 mix
            wo_ps x2 ss3 ms3 rt3 h hT_ps lg rout posps posm cntr gT_ps gT b2ps acc0 init sel gath xe_hi
            xe_lo selT_ps selT glin sgm midr mt_ps mt_hi mt_lo y_hi y_lo comb acc chain_a chain_v chain_p
            swc gex ysv w_hi w_lo_v w_lo_p w_used b1b b2 zero etab_half etab_v qzero gmx con_rest sc osel
            o_ev fin_ps x3 ss4 ms4 rt4 yfin""".split()
        S = {n: sem("s_" + n) for n in names}
        s_w = [sem(f"s_w{k}") for k in range(6)]
        NPRM = 11

        def bc(ap, shape):
            return ap.broadcast_to(shape)

        def keys_to(n):
            b, rt = divmod(n, 5)
            return kT4[:, b % 2, :, P * rt:P * rt + P] if rt < 4 else kT1[:, b % 2]

        block = ctx.enter_context(nc.Block())

        def piece(e, k):
            if k < 8:
                src = I["w_moe1"][0, bass.ds(e, 1), :, :].rearrange("a (p j) (g b n) -> (a p) j b g n", j=J, g=2, b=2)
                j, b = 2 * (k % 4), 1 - k // 4
                return ring_w[:, k % 6, :].rearrange("p (j g n) -> p j g n", j=2, g=2), src[:, j:j + 2, b]
            src = I["w_moe2"][0, bass.ds(e, 1), :, :].rearrange("a (m q) n -> q (a m) n", q=P)
            return ring_w[:, k % 6, :].rearrange("p (m n) -> p m n", m=2), src[:, (2 * k - 12) % J:(2 * k - 12) % J + 2, :]

        LO_P = [1, 4, 7, 10]
        LO_V = [k for k in range(NPIECE) if k not in LO_P]

        def wait_low(eng, n, k):
            name, own = ("w_lo_p", LO_P) if k in LO_P else ("w_lo_v", LO_V)
            eng.wait_ge(S[name], n * len(own) + (len(own) + own.index(k) + 1))

        def wait_low_before(eng, n, k):
            if k >= 6:
                wait_low(eng, n, k - 6)
            else:
                name, own = ("w_lo_p", LO_P) if k + 6 in LO_P else ("w_lo_v", LO_V)
                eng.wait_ge(S[name], n * len(own) + (own.index(k + 6) + 1))

        def run_experts(eng, chunk):
            done = eng.alloc_register()
            eng.reg_mov(done, 0)
            with eng.Fori(0, NEXP) as e:
                count = eng.value_load(cnt[0:1, bass.ds(e, 1)], min_val=0, max_val=NTOK)
                with eng.If(count > CAP):
                    with eng.Fori(1, CHUNKS) as c:
                        with eng.If(count > c * CAP):
                            chunk(eng.snap(done, min_val=0, max_val=NEXP * CHUNKS), e, c * CAP, False)
                            eng.reg_add(done, done, 1)
                chunk(eng.snap(done, min_val=0, max_val=NEXP * CHUNKS), e, 0, True)
                eng.reg_add(done, done, 1)
            return eng.snap(done, min_val=0, max_val=NEXP * CHUNKS)

        @block.sync
        def _(sp):
            sp.dma_start(x[:, 0:2, :], I["x_prompt"][0].rearrange("(t p) d -> p t d", p=P)).then_inc(S["x"], 16)
            sp.dma_start(x[0:NS, 2, :], I["x_sample"].rearrange("b t d -> (b t) d")).then_inc(S["x"], 16)
            sp.dma_start(con[:, 0:P], I["con"][:, 0:P]).then_inc(S["con"], 16)
            wv = I["w_in"][0].rearrange("(p j) (g n) -> p g j n", j=J, g=4)
            sp.dma_start(w_in[:, 3, :, :], wv[:, 3]).then_inc(S["win0"], 16)
            sp.wait_ge(S["prm"], 16 * NPRM)

            def late(dst, src):
                sp.dma_start(dst, src).then_inc(S["late"], 16)

            with nc.allow_non_contiguous_dma(reason="parameters of a few hundred words"):
                late(dsk, I["ssm_d"][0].rearrange("(b g) c -> (g c) b", g=8))
                late(bgl, I["b_glu"][0].rearrange("(b p) -> p b", p=P))
                late(gat, I["attn_out_norm_g"][0].rearrange("(b p) -> p b", p=P))
                late(gss, I["ssm_out_norm_g"][0].rearrange("(b p) -> p b", p=P))
                late(bro[:, :], I["b_router"].broadcast_to([P, NEXP]))
            sp.dma_start(con[:, P:], I["con"][:, P:]).then_inc(S["con_rest"], 16)
            for g in range(3):
                sp.dma_start(w_in[:, g, :, :], wv[:, g]).then_inc(S["win1"], 16)
            sp.dma_start(w_glu[:, :, :], I["w_glu"][0].rearrange("(j p) n -> p j n", p=P)).then_inc(S["wglu"], 16)
            sp.dma_start(wr[:, :, :], I["w_router"][0].rearrange("(p j) n -> p j n", j=J)).then_inc(S["wglu"], 16)

            def load_cache(name, dst, b, sm):
                c = I[name][0, b].rearrange("r h e -> r (h e)")
                sp.dma_start(dst[:, 0:2048], c[512:1024].rearrange("(p j) n -> p (j n)", j=4)).then_inc(sm, 16)
                lo = c[0:512].rearrange("(i s) n -> s i n", s=16)
                for s in range(4):
                    sp.dma_start(dst[32 * s:32 * s + 32, 2048:2560], lo[s]).then_inc(sm, 16)

            sp.wait_ge(S["proj"], 16)
            def load_keys(b):
                if b >= 2:
                    sp.wait_ge(S["kt_ps"], 5 * (b - 1))
                load_cache("cache_k", k_cache[:, b % 2, :], b, S[f"kload{b % 2}"])

            def load_values(b):
                if b >= 4:
                    sp.wait_ge(S["pv"], b - 3)
                load_cache("cache_v", v_cache[:, b % 4, :], b, S[f"vload{b % 4}"])

            load_keys(0)
            load_keys(1)
            for b in range(4):
                load_values(b)
            for b in range(2, 7):
                load_keys(b)
            load_values(4)
            load_keys(7)
            load_values(5)
            sp.wait_ge(S["sto_ps"], 1)
            sp.dma_start(w_out, I["w_out"][0].rearrange("(j p) n -> p j n", p=P)).then_inc(S["wout"], 16)
            load_values(6)
            load_values(7)
            sp.wait_ge(S["kvr"], 6)
            for a, nm in enumerate("kv"):
                sp.dma_start(O[nm + "_p"].rearrange("a b (t p) h e -> p (a b t) (h e)", p=P), kv_rows[:, a, 0:2, :]).then_inc(S["out"], 16)
                sp.dma_start(O[nm + "_s"].rearrange("a b t h e -> (a b t) (h e)"), kv_rows[0:NS, a, 2, :]).then_inc(S["out"], 16)
            sp.wait_ge(S["sto"], 1)
            for r, nm in enumerate(("re_p", "im_p")):
                sp.dma_start(O[nm].rearrange("a b (i g) n -> (a b i) (g n)", g=2), st_out[0:NI, r, :]).then_inc(S["out"], 16)
            for r, nm in enumerate(("re_s", "im_s")):
                sp.dma_start(O[nm].rearrange("a b (i g) n -> (a b i) (g n)", g=2), st_out[:, 2 + r, :]).then_inc(S["out"], 16)
            sp.wait_ge(S["pv"], NB)
            sp.dma_start(g_row, I["norm_ffn_g"].broadcast_to([P, D])).then_inc(S["gff"], 16)
            for k in range(6):
                sp.dma_start(*piece(0, k)).then_inc(s_w[k], 16)
            sp.wait_ge(S["ssq"], 1)
            sp.dma_start(b2_rows, I["b_moe2"][0]).then_inc(S["b2"], 16)
            sp.wait_ge(S["h"], 3)
            sp.dma_start(g_row, I["norm_final_g"].rearrange("(a d) -> a d", a=1).broadcast_to([P, D])).then_inc(S["gfi"], 16)
            sp.wait_ge(S["cntr"], 1)
            sp.wait_ge(S["out"], 16 * 8)

            following = sp.alloc_register()
            sp.reg_mov(following, 0)
            own_reg = sp.alloc_register()

            def load(n, e, own, k):
                wait_low_before(sp, n, k)
                sp.dma_start(*piece(own if k in (4, 10) else e, k)).then_inc(s_w[k % 6], 16)

            def weights(n, e, first, last):
                sp.wait_ge(S["midr"], n * 2 + 1)
                sp.dma_start(b1b, I["b_moe1"][0, bass.ds(e, 1), :].broadcast_to([P, 2 * DFF])).then_inc(S["b1b"], 16)
                sp.reg_mov(own_reg, e)
                own = sp.snap(own_reg, min_val=0, max_val=NEXP - 1)
                for k in range(6, 12):
                    load(n, e, own, k)

                def ahead(e):
                    sp.reg_mov(own_reg, e)
                    own = sp.snap(own_reg, min_val=0, max_val=NEXP - 1)
                    for k in range(6):
                        load(n + 1, e, own, k)
                if last:
                    sp.reg_add(following, following, 1)
                    with sp.If(e < NEXP - 1):
                        ahead(sp.snap(following, min_val=0, max_val=NEXP - 1))
                else:
                    ahead(e)

            run_experts(sp, weights)
            sp.wait_ge(S["yfin"], 3)
            sp.dma_start(O["y_p"][0].rearrange("(t p) d -> p t d", p=P), x[:, 0:2, :]).then_inc(S["out"], 16)
            sp.dma_start(O["y_s"].rearrange("b t d -> (b t) d"), x[0:NS, 2, :]).then_inc(S["out"], 16)
            sp.wait_ge(S["out"], 16 * 10)

        @block.gpsimd
        def _(pool):
            chain = [0]

            def link(ins):
                chain[0] += 1
                ins.then_inc(S["chain_p"], 1)
                pool.wait_ge(S["chain_p"], chain[0])

            tt = pool.tensor_tensor
            pool.wait_ge(S["exps"], 1)
            link(pool.tensor_copy(e_tab[:, 0, :, 0:1], prm[:, PA_C, :].unsqueeze(2)))
            link(pool.tensor_copy(e_tab[:, 1, :, 0:1], prm[:, PA_S, :].unsqueeze(2)))
            m = 1
            while m < HALF:
                re, im = e_tab[:, 0, :, 0:m], e_tab[:, 1, :, 0:m]
                cr = bc(e_tab[:, 0, :, m - 1:m], [P, NI, m])
                ci = bc(e_tab[:, 1, :, m - 1:m], [P, NI, m])
                t1, t2 = e_tmp[:, 0, :, 0:m], e_tmp[:, 1, :, 0:m]
                link(tt(t1, re, cr, ALU.mult))
                link(tt(t2, im, ci, ALU.mult))
                ins = tt(e_tab[:, 0, :, m:2 * m], t1, t2, ALU.subtract)
                if 2 * m == HALF:
                    break
                link(ins)
                link(tt(t1, re, ci, ALU.mult))
                link(tt(t2, im, cr, ALU.mult))
                ins = tt(e_tab[:, 1, :, m:2 * m], t1, t2, ALU.add)
                m *= 2
                if 2 * m == HALF:
                    ins.then_inc(S["etab_half"], 1)
                    pool.wait_ge(S["etab_half"], 1)
                else:
                    link(ins)
            ins.then_inc(S["etab"], 1)
            pool.wait_ge(S["etab"], 1)
            pool.wait_ge(S["etab_v"], 1)
            for i in range(NI):
                b = i % 2
                er, ei = e_tab[:, 0, i, :], e_tab[:, 1, i, :]
                pool.wait_ge(S["g1"], i + 1)
                if i >= 1:
                    pool.wait_ge(S["hhi"], i)
                if i >= 2:
                    pool.wait_ge(S["yps"], i - 1)
                gr, gi = ssm_g[:, b, 0, 1, :], ssm_g[:, b, 1, 1, :]
                tt(ssm_p[:, 0, :], gr, er, ALU.mult)
                tt(ssm_p[:, 1, :], gi, er, ALU.mult)
                tt(ssm_p[:, 2, :], gi, ei, ALU.mult)
                link(tt(ssm_p[:, 3, :], gr, ei, ALU.mult))
                tt(ssm_h[:, b, 0, HALF:], ssm_p[:, 0, :], ssm_p[:, 2, :], ALU.subtract)
                tt(ssm_h[:, b, 1, HALF:], ssm_p[:, 1, :], ssm_p[:, 3, :], ALU.add).then_inc(S["hhi"], 1)
                pool.wait_ge(S["hhi"], i + 1)
                ins = pool.tensor_copy(hf[:, :, i:i + 1], ssm_h[:, b, :, SEQ - 1:SEQ])
            ins.then_inc(S["hfin"], 1)
            pool.wait_ge(S["bus"], 1)
            pool.wait_ge(S["g1"], NI)
            ar, ai = (bc(prm[:, n, :].unsqueeze(2), [P, NI, NB]) for n in (PA_AR, PA_AI))
            hv = hs[:, :, :, :].rearrange("p r i (b t) -> p r i b t", t=NSEQ)
            buv = bus.rearrange("p (i r b t) -> p r i b t", i=NI, r=2, t=NSEQ)
            h0v = h0[:, :, :].rearrange("p r (b i) -> p r i b", b=NB)
            tq = lambda n: (ssm_a, ssm_b)[n // 4][:, n % 4, :].rearrange("p (i b) -> p i b", i=NI)
            for t in range(NSEQ):
                pr, pi = (h0v[:, 0], h0v[:, 1]) if t == 0 else (hv[:, 0, :, :, t - 1], hv[:, 1, :, :, t - 1])
                tt(tq(0), pr, ar, ALU.mult)
                tt(tq(1), pi, ai, ALU.mult)
                tt(tq(2), pi, ar, ALU.mult)
                link(tt(tq(3), pr, ai, ALU.mult))
                tt(tq(4), tq(0), tq(1), ALU.subtract)
                link(tt(tq(5), tq(2), tq(3), ALU.add))
                tt(hv[:, 0, :, :, t], tq(4), buv[:, 0, :, :, t], ALU.add)
                link(tt(hv[:, 1, :, :, t], tq(5), buv[:, 1, :, :, t], ALU.add))
            pool.tensor_copy(sf[:, :, :].rearrange("p r (b i) -> p r i b", b=NB), hv[:, :, :, :, NSEQ - 1]).then_inc(S["hs"], 1)

            def low_parts(n, e, first, last):
                for k in LO_P:
                    pool.wait_ge(S["w_hi"], n * NPIECE + (k + 1))
                    tt(w_lo[:, k % 4, :], ring_w[:, k % 6, :], w_hi[:, k % 4, :].bitcast(F32), ALU.subtract).then_inc(S["w_lo_p"], 1)

            pool.wait_ge(S["cntr"], 1)
            run_experts(pool, low_parts)

        @block.scalar
        def _(act):
            chain = [0]

            def link(ins):
                chain[0] += 1
                ins.then_inc(S["chain_a"], 1)
                act.wait_ge(S["chain_a"], chain[0])

            def small(dst, src):
                act.dma_start(dst, src).then_inc(S["prm"], 16)

            A = act.activation
            with nc.allow_non_contiguous_dma(reason="parameters of a few hundred words"):
                act.dma_start(gmx, I["norm_mix_g"][0].rearrange("(p j) -> p j", j=J)).then_inc(S["gmx"], 16)
                small(ld[0:NI, 0:2], I["ssm_log_dt"][0].rearrange("(i g) -> i g", g=2))
                small(par[0:NI, 0:P], I["ssm_a_re"][0].rearrange("(i g) n -> i (g n)", g=2))
                small(par[0:NI, P:2 * P], I["ssm_a_im"][0].rearrange("(i g) n -> i (g n)", g=2))
                for r, nm in enumerate(("state_ssm_re", "state_ssm_im")):
                    small(h0row[:, r, :], I[nm][0].rearrange("b (i g) n -> (b i) (g n)", g=2))
                for r, nm in enumerate(("ssm_b_re", "ssm_b_im")):
                    small(bnat[:, r, :].rearrange("p (i c) -> p i c", i=NI), I[nm][0].rearrange("(i g) n c -> (g n) i c", g=2))
                for r, nm in enumerate(("ssm_c_re", "ssm_c_im")):
                    for dup in range(2):
                        small(cnat[:, r, :, 64 * dup:64 * dup + 64], I[nm][0].rearrange("g c n -> (g c) n").rearrange("(b p) n -> p b n", p=P))
            act.wait_ge(S["x"], 32)
            act.wait_ge(S["init"], 1)
            for t, (_, n) in enumerate(TILES):
                ins = A(xn[0:n, t, :], x[0:n, t, :], ACT.Square, accum_out=st[0:n, t:t + 1])
            ins.then_inc(S["ss"], 1)
            act.wait_ge(S["ms"], 1)
            A(st[:, 3:6], st[:, 3:6], ACT.Sqrt).then_inc(S["rt"], 1)
            act.wait_ge(S["gmx"], 16)
            for n, j in enumerate(range(1, J, 2)):
                act.wait_ge(S["xT_ps"], j + 1)
                A(accT[:, j, :], ps[:, 4 + j % 4, 0:NTOK], ACT.Copy, scale=gmx[:, j:j + 1]).then_inc(S["xT_a"], 1)
            act.wait_ge(S["prm"], 16 * NPRM)
            A(ld[0:NI, 0:2], ld[0:NI, 0:2], ACT.Exp).then_inc(S["dt"], 1)
            act.wait_ge(S["red"], 1)
            A(prm[:, PA_R, :], prm[:, PA_RD, :], ACT.Exp)
            A(prm[:, PA_C, :], prm[:, 11, :], ACT.Sin)
            A(prm[:, PA_S, :], prm[:, 12, :], ACT.Sin).then_inc(S["exps"], 1)
            for n, c in enumerate([12, 13, 14, 15] + list(range(12))):
                act.wait_ge(S["proj"], n + 1)
                A(qkvu[:, c, :], ps[:, 4 + n % 2, 0:NTOK], ACT.Copy).then_inc(S["proj_ev"], 1)
            act.wait_ge(S["proj_ev"], 16)
            act.wait_ge(S["qzero"], 1)
            for c in range(4):
                for g in range(2):
                    rows, at = slice(64 * g, 64 * g + 64), 8 * c + 4 * g
                    ins = A(qz[rows, c, :, at:at + 4], qkvu[rows, c, SEQ:].rearrange("p (b t) -> p b t", t=NSEQ), ACT.Copy)
            ins.then_inc(S["qbd"], 1)
            for n in range(6):
                a, t = divmod(n, 3)
                rows = TILES[t][1]
                act.wait_ge(S["kvr_ps"], n + 1)
                A(kv_rows[0:rows, a, t, :], ps[0:rows, 4 + n % 2, :], ACT.Copy).then_inc(S["kvr"], 1)
            act.wait_ge(S["bu"], NI)
            for n in range(2):
                ins = A(bus.rearrange("p (k n c) -> p n k c", k=8, n=2)[:, n], ps[:, n, :].rearrange("p (k c) -> p k c", k=8), ACT.Copy)
            ins.then_inc(S["bus"], 1)
            def key_tile_out(n):
                act.wait_ge(S["kt_ps"], n + 1)
                if n == 0:
                    act.wait_ge(S["hfin"], 1)
                if n >= 10:
                    act.wait_ge(S["sc"], n // 5 - 1)
                A(keys_to(n), ps[:, 4, :].rearrange("p (c n) -> p c n", c=4), ACT.Copy).then_inc(S["ktA"], 1)

            for hh in range(H + 1):
                if hh < H:
                    b = hh % 2
                    act.wait_ge(S["nm"], hh + 1)
                    A(prb[:, b, 0:P], scb[:, b, 0:P], ACT.Exp, bias=st[:, 12 + 2 * b:13 + 2 * b], accum_out=st[:, 16 + 2 * b:17 + 2 * b])
                    A(prb[:, b, P:], scb[:, b, P:], ACT.Exp, bias=st[:, 13 + 2 * b:14 + 2 * b], accum_out=st[:, 17 + 2 * b:18 + 2 * b]).then_inc(S["ex"], 1)
                if hh % 2 == 0:
                    key_tile_out(hh)
                if hh >= 1:
                    b = (hh - 1) % 2
                    act.wait_ge(S["pt_ps"], hh)
                    A(ptb[:, b, :], ps[:, b, 0:3 * P], ACT.Copy).then_inc(S["pt"], 1)
            act.wait_ge(S["sto_ps"], 1)
            A(st_out[0:NI, 0:2, :], ps[0:NI, 1, 0:2 * P].rearrange("p (r n) -> p r n", r=2), ACT.Copy)
            A(st_out[:, 2:4, :], ps[:, 1, 2 * P:4 * P].rearrange("p (r n) -> p r n", r=2), ACT.Copy).then_inc(S["sto"], 1)
            def keys_out(b):
                for n in range(5 * b, 5 * b + 5):
                    if n % 2 == 0:
                        key_tile_out(n)

            def exponentials(half):
                act.wait_ge(S["nms"], half + 1)
                A(p_s, s_s, ACT.Exp, bias=st[:, 24:25], accum_out=st[:, 25:26]).then_inc(S["exs"], 1)

            def probs_out(half):
                act.wait_ge(S["pts_ps"], half + 1)
                A(p_T[:, 0:512], ps[:, 0, :], ACT.Copy)
                A(p_T[:, 512:640], ps[:, 1, 0:P], ACT.Copy)
                A(p_T[0:NS, 640:768], ps[0:NS, 1, P:2 * P], ACT.Copy).then_inc(S["pts"], 1)

            def rows_of(half):
                act.wait_ge(S["pv"], 4 * half + 4)
                A(o_s[half], ps[:, 2 + half, :], ACT.Copy).then_inc(S["o_ev"], 1)

            for b in range(2, 5):
                keys_out(b)
            exponentials(0)
            keys_out(5)
            probs_out(0)
            keys_out(6)
            keys_out(7)
            exponentials(1)
            rows_of(0)
            probs_out(1)
            rows_of(1)
            act.wait_ge(S["late"], 16 * 5)
            act.wait_ge(S["gel1"], 1)
            A(kvg, kvg, ACT.Sigmoid, scale=G_A).then_inc(S["gel2"], 1)
            for b in range(4):
                act.wait_ge(S["glu_ps"], b + 1)
                A(kvg.rearrange("p (b t) -> p b t", b=4)[:, b, :], ps[:, 4 + b, 0:NTOK], ACT.Sigmoid, bias=bgl[:, b:b + 1]).then_inc(S["glu"], 1)
            act.wait_ge(S["aTs"], 4)
            act.wait_ge(S["sq"], 1)
            A(sqa, aT[:, :, :], ACT.Square).then_inc(S["sqA"], 1)
            act.wait_ge(S["ms2"], 1)
            A(st[:, 36:42], st[:, 36:42], ACT.Sqrt).then_inc(S["rt2"], 1)
            for t, (_, n) in enumerate(TILES):
                act.wait_ge(S["x2"], t + 1)
                A(h[0:n, t, :], x[0:n, t, :], ACT.Square, accum_out=st[0:n, 48 + t:49 + t]).then_inc(S["ss3"], 1)
                act.wait_ge(S["ms3"], t + 1)
                A(st[:, 51 + t:52 + t], st[:, 51 + t:52 + t], ACT.Sqrt).then_inc(S["rt3"], 1)
            for j in range(1, J, 2):
                act.wait_ge(S["hT_ps"], j + 1)
                A(accT[:, j, :], ps[:, j, 0:NTOK], ACT.Copy).then_inc(S["xT_a"], 1)
            for t, (_, n) in enumerate(TILES):
                act.wait_ge(S["rout"], t + 1)
                A(top[0:n, t, 12:16], top[0:n, t, 8:12], ACT.Exp, accum_out=top[0:n, t, 20:21]).then_inc(S["gex"], 1)
            act.wait_ge(S["gT_ps"], 1)
            A(gT[:, :], ps[0:NEXP, 4, 0:NTOK], ACT.Copy).then_inc(S["gT"], 1)
            for j in range(J):
                act.wait_ge(S["b2ps"], j + 1)
                A(accT[:, j, :], ps[:, 2 + j % 2, 0:NTOK], ACT.Copy).then_inc(S["acc0"], 1)

            def rows_out(n):
                act.wait_ge(S["w_used"], n * NPIECE + 4)
                act.wait_ge(S["selT"], n + 1)
                A(y_hi[:, :].rearrange("p (a n) -> p a n", a=2), ps[:, 6:8, :], ACT.Copy, scale=gslot).then_inc(S["y_hi"], 1)

            def act_pass(n, e, first, last):
                def high(*ks):
                    for k in ks:
                        act.wait_ge(s_w[k % 6], n * 32 + 16 * (k // 6 + 1))
                        act.wait_ge(S["w_used"], n * NPIECE + (k + 1))
                        A(w_hi[:, k % 4, :], ring_w[:, k % 6, :], ACT.Copy).then_inc(S["w_hi"], 1)

                def mid_high(b):
                    act.wait_ge(S["mt_ps"], n * 2 + (b + 1))
                    A(mt_hi[:, 4 * b:4 * b + 4, :], ps[:, 4 + b, :].rearrange("p (m s) -> p m s", m=4), ACT.Copy).then_inc(S["mt_hi"], 1)

                def sigmoid(b):
                    act.wait_ge(S["glin"], n * 2 + (b + 1))
                    A(sig, glu_b, ACT.Sigmoid, scale=ALPHA).then_inc(S["sgm"], 1)

                high(0, 1)
                rows_out(n)
                for a in range(2):
                    act.wait_ge(S["gath"], n * 2 + (a + 1))
                    A(xe_hi[:, 4 * a:4 * a + 4, :], ps[:, 4 + a, :].rearrange("p (j s) -> p j s", j=4), ACT.Copy).then_inc(S["xe_hi"], 1)
                high(2, 3, 4, 5, 6, 7)
                sigmoid(0)
                high(8, 9)
                mid_high(0)
                high(10, 11)
                sigmoid(1)
                mid_high(1)

            act.wait_ge(S["cntr"], 1)
            act.wait_ge(S["selT"], 1)
            total = run_experts(act, act_pass)
            rows_out(total)

            for t, (_, n) in enumerate(TILES):
                act.wait_ge(S["x3"], t + 1)
                ins = A(h[0:n, t, :], x[0:n, t, :], ACT.Square, accum_out=st[0:n, 60 + t:61 + t])
            ins.then_inc(S["ss4"], 1)
            act.wait_ge(S["ms4"], 1)
            A(st[:, 63:66], st[:, 63:66], ACT.Sqrt).then_inc(S["rt4"], 1)

        @block.vector
        def _(dve):
            chain = [0]

            def link(ins):
                chain[0] += 1
                ins.then_inc(S["chain_v"], 1)
                dve.wait_ge(S["chain_v"], chain[0])

            tt, ts, stt = dve.tensor_tensor, dve.tensor_scalar, dve.scalar_tensor_tensor
            dve.memset(ones[:, :], 1.0)
            dve.memset(xb[:, :, :], 0.0)
            dve.memset(st[:, :], 1.0).then_inc(S["init"], 1)
            for c, (what, count) in enumerate((("w_lo_v", len(LO_V)), ("w_lo_p", len(LO_P)), ("w_used", 4), ("midr", 1), ("acc", 1))):
                dve.memset(mark[:, c:c + 1], 1.0).then_inc(S[what], count)
            dve.wait_ge(S["ss"], 1)
            ts(st[:, 3:6], st[:, 0:3], 1.0 / D, EPS, ALU.mult, ALU.add).then_inc(S["ms"], 1)
            dve.wait_ge(S["rt"], 1)
            link(dve.reciprocal(st[:, 6:9], st[:, 3:6]))
            for t, (_, n) in enumerate(TILES):
                ins = ts(xn[0:n, t, :], x[0:n, t, :], st[0:n, 6 + t:7 + t], None, ALU.mult)
            ins.then_inc(S["xn"], 1)
            dve.wait_ge(S["gmx"], 16)
            for j in range(0, J, 2):
                dve.wait_ge(S["xT_ps"], j + 1)
                ts(accT[:, j, :], ps[:, 4 + j % 4, 0:NTOK], gmx[:, j:j + 1], None, ALU.mult).then_inc(S["xT_d"], 1)
            dve.wait_ge(S["prm"], 16 * NPRM)
            dve.wait_ge(S["dt"], 1)
            dtb = bc(ld[0:NI, 0:2].unsqueeze(2), [NI, 2, 64])
            tt(st_out[0:NI, 0, :].rearrange("p (g n) -> p g n", g=2), par[0:NI, 0:P].rearrange("p (g n) -> p g n", g=2), dtb, ALU.mult)
            tt(st_out[0:NI, 1, :].rearrange("p (g n) -> p g n", g=2), par[0:NI, P:2 * P].rearrange("p (g n) -> p g n", g=2), dtb, ALU.mult).then_inc(S["rows"], 1)
            dve.wait_ge(S["prmT"], 1)
            link(dve.tensor_copy(prm[:, 0:4, :], ps[:, 0, 0:64].rearrange("p (a i) -> p a i", a=4)))
            link(ts(prm[:, 11, :], prm[:, PA_TH, :], TWO_PI / 4, None, ALU.add))
            link(dve.tensor_copy(prm[:, 12, :], prm[:, PA_TH, :]))
            two = prm[:, 11:13, :]
            kk = prm[:, 13:15, :]
            link(ts(kk, two, 1.0 / TWO_PI, ROUND, ALU.mult, ALU.add))
            link(ts(kk, kk, -ROUND, None, ALU.add))
            link(stt(two, kk, -TP_HI, two, ALU.mult, ALU.add))
            link(stt(two, kk, -TP_LO, two, ALU.mult, ALU.add))
            ts(two, two, PI_IN, -PI_IN, ALU.min, ALU.max).then_inc(S["red"], 1)
            link(dve.tensor_copy(h0[:, :, :], ps[:, 1, 0:2 * P].rearrange("p (r n) -> p r n", r=2)))
            dve.wait_ge(S["con_rest"], 16)
            gm4 = bc(gmask.unsqueeze(1), [P, 4, P])
            tt(cT[:, 0, :].rearrange("p (b n) -> p b n", b=4), ps[:, 2, :].rearrange("p (b n) -> p b n", b=4), gm4, ALU.mult)
            stt(cT[:, 1, :].rearrange("p (b n) -> p b n", b=4), ps[:, 3, :].rearrange("p (b n) -> p b n", b=4), -1.0, gm4, ALU.mult, ALU.mult).then_inc(S["crev"], 1)
            dve.wait_ge(S["exps"], 1)
            q = lambda n: prm[:, n, :]
            tt(q(PA_AR), q(PA_R), q(PA_C), ALU.mult)
            link(tt(q(PA_AI), q(PA_R), q(PA_S), ALU.mult))
            ts(q(15), q(PA_AR), -1.0, None, ALU.add)
            tt(q(16), q(PA_LR), q(PA_LR), ALU.mult)
            link(tt(q(17), q(PA_LI), q(PA_LI), ALU.mult))
            link(tt(q(16), q(16), q(17), ALU.add))
            dve.reciprocal(q(16), q(16))
            tt(q(18), q(15), q(PA_LR), ALU.mult)
            tt(q(19), q(PA_AI), q(PA_LI), ALU.mult)
            tt(q(20), q(PA_AI), q(PA_LR), ALU.mult)
            link(tt(q(21), q(15), q(PA_LI), ALU.mult))
            tt(q(18), q(18), q(19), ALU.add)
            link(tt(q(20), q(20), q(21), ALU.subtract))
            tt(q(PA_FR), q(18), q(16), ALU.mult)
            link(tt(q(PA_FI), q(20), q(16), ALU.mult))
            v3 = lambda r: bnat[:, r, :].rearrange("p (i c) -> p i c", i=NI)
            fr, fi = (bc(q(n).unsqueeze(2), [P, NI, 16]) for n in (PA_FR, PA_FI))
            s3 = lambda n: ssm_a[:, 2 * n:2 * n + 2, :].rearrange("p a t -> p (a t)").rearrange("p (i c) -> p i c", i=NI)
            s4 = lambda n: ssm_b[:, 2 * n:2 * n + 2, :].rearrange("p a t -> p (a t)").rearrange("p (i c) -> p i c", i=NI)
            tt(s3(0), v3(0), fr, ALU.mult)
            tt(s3(1), v3(1), fi, ALU.mult)
            tt(s4(0), v3(1), fr, ALU.mult)
            link(tt(s4(1), v3(0), fi, ALU.mult))
            for g in range(2):
                rows = slice(64 * g, 64 * g + 64)
                dst = lambda r: xb[rows, r, :].rearrange("p (i g c) -> p i g c", i=NI, g=2)[:, :, g, :]
                tt(dst(0), s3(0)[rows], s3(1)[rows], ALU.subtract)
                ins = tt(dst(1), s4(0)[rows], s4(1)[rows], ALU.add)
            ins.then_inc(S["fdone"], 1)
            dve.wait_ge(S["bT_ps"], 1)
            dve.memset(qz, 0.0).then_inc(S["qzero"], 1)
            dve.tensor_copy(bT[:, 0, :], ps[:, 0, :])
            dve.tensor_copy(bT[:, 1, :], ps[:, 1, :]).then_inc(S["bT"], 1)
            dve.wait_ge(S["late"], 16 * 5)
            dve.wait_ge(S["etab_half"], 1)
            hh = HALF // 2
            re, im = e_tab[:, 0, :, 0:hh], e_tab[:, 1, :, 0:hh]
            t1, t2 = (e_tmp_v[:, a].rearrange("p (i t) -> p i t", i=NI) for a in range(2))
            tt(t1, re, bc(e_tab[:, 1, :, hh - 1:hh], [P, NI, hh]), ALU.mult)
            link(tt(t2, im, bc(e_tab[:, 0, :, hh - 1:hh], [P, NI, hh]), ALU.mult))
            tt(e_tab[:, 1, :, hh:HALF], t1, t2, ALU.add).then_inc(S["etab_v"], 1)
            dve.wait_ge(S["etab"], 1)
            dve.wait_ge(S["etab_v"], 1)
            for i in range(NI):
                b = i % 2
                er, ei = e_tab[:, 0, i, :], e_tab[:, 1, i, :]
                buf = ps[:, 6 + b, :].rearrange("p (r t) -> p r t", r=4)
                dve.wait_ge(S["bu"], i + 1)
                if i >= 1:
                    dve.wait_ge(S["g1"], i)
                tt(ssm_a[:, :, :], buf, bc(er.unsqueeze(1), [P, 4, HALF]), ALU.mult)
                tt(ssm_b[:, 0:2, :], buf[:, 2:4, :], bc(ei.unsqueeze(1), [P, 2, HALF]), ALU.mult)
                tt(ssm_b[:, 2:4, :], buf[:, 0:2, :], bc(ei.unsqueeze(1), [P, 2, HALF]), ALU.mult).then_inc(S["bu_used"], 1)
                dve.wait_ge(S["bu_used"], i + 1)
                tt(ssm_a[:, 0:2, :], ssm_a[:, 0:2, :], ssm_b[:, 0:2, :], ALU.add)
                link(tt(ssm_a[:, 2:4, :], ssm_a[:, 2:4, :], ssm_b[:, 2:4, :], ALU.subtract))
                decay = bc(prm[:, PA_R, i:i + 1], [P, HALF])
                if i >= 2:
                    dve.wait_ge(S["hhi"], i - 1)
                    dve.wait_ge(S["yps"], i - 1)
                dve.tensor_tensor_scan(ssm_g[:, b, 0, 0, :], decay, ssm_a[:, 0, :], 0.0, ALU.mult, ALU.add)
                link(dve.tensor_tensor_scan(ssm_g[:, b, 1, 0, :], decay, ssm_a[:, 2, :], 0.0, ALU.mult, ALU.add))
                gr, gi = ssm_g[:, b, 0, 0, :], ssm_g[:, b, 1, 0, :]
                tt(ssm_b[:, 0, :], gr, er, ALU.mult)
                tt(ssm_b[:, 1, :], gi, er, ALU.mult)
                tt(ssm_b[:, 2, :], gi, ei, ALU.mult)
                link(tt(ssm_b[:, 3, :], gr, ei, ALU.mult))
                tt(ssm_h[:, b, 0, 0:HALF], ssm_b[:, 0, :], ssm_b[:, 2, :], ALU.subtract)
                tt(ssm_h[:, b, 1, 0:HALF], ssm_b[:, 1, :], ssm_b[:, 3, :], ALU.add).then_inc(S["hlo"], 1)
                dve.wait_ge(S["hlo"], i + 1)
                dve.tensor_tensor_scan(ssm_g[:, b, 0, 1, :], decay, ssm_a[:, 1, :], ssm_h[:, b, 0, HALF - 1:HALF], ALU.mult, ALU.add)
                dve.tensor_tensor_scan(ssm_g[:, b, 1, 1, :], decay, ssm_a[:, 3, :], ssm_h[:, b, 1, HALF - 1:HALF], ALU.mult, ALU.add).then_inc(S["g1"], 1)
                if i % 4 == 1 and i >= 4:
                    blk = i // 4 - 1
                    dve.wait_ge(S["yps"], 4 * (blk + 1))
                    stt(yS[:, blk, 0:SEQ], qkvu[:, 12 + blk, 0:SEQ], dsk[:, blk:blk + 1], ps[:, 2 + blk % 2, 0:SEQ], ALU.mult, ALU.add).then_inc(S["yS_ready"], 1)
            dve.wait_ge(S["yps"], NI)
            stt(yS[:, 3, 0:SEQ], qkvu[:, 15, 0:SEQ], dsk[:, 3:4], ps[:, 3, 0:SEQ], ALU.mult, ALU.add).then_inc(S["yS_ready"], 1)
            def key_tile_out(n):
                dve.wait_ge(S["kt_ps"], n + 1)
                if n == 1:
                    dve.wait_ge(S["hfin"], 1)
                if n >= 10:
                    dve.wait_ge(S["sc"], n // 5 - 1)
                dve.tensor_copy(keys_to(n), ps[:, 5, :].rearrange("p (c n) -> p c n", c=4)).then_inc(S["ktD"], 1)

            def pair_out(hp):
                dve.wait_ge(S["o_ps"], 2 * hp + 2)
                dve.tensor_copy(aT[:, hp, 0:SEQ], ps[:, 2 + hp % 2, 0:SEQ]).then_inc(S["aT"], 1)

            for hh in range(H + 1):
                if hh < H:
                    b = hh % 2
                    dve.wait_ge(S["s_ps"], hh + 1)
                    link(stt(scb[:, b, :], ps[:, 6 + b, 0:3 * P], SCALE, con[:, C_BP:C_BP + 3 * P], ALU.mult, ALU.add))
                    dve.tensor_reduce(st[:, 10:11], scb[:, b, 0:P], AX, ALU.max)
                    link(dve.tensor_reduce(st[:, 11:12], scb[:, b, P:], AX, ALU.max))
                    ts(st[:, 12 + 2 * b:14 + 2 * b], st[:, 10:12], -1.0, None, ALU.mult).then_inc(S["nm"], 1)
                if hh % 2:
                    key_tile_out(hh)
                    if hh >= 3:
                        pair_out((hh - 3) // 2)
                if hh >= 1:
                    b = (hh - 1) % 2
                    dve.wait_ge(S["ex"], hh)
                    link(dve.reciprocal(st[:, 20 + 2 * b:22 + 2 * b], st[:, 16 + 2 * b:18 + 2 * b]))
                    ts(prb[:, b, 0:P], prb[:, b, 0:P], st[:, 20 + 2 * b:21 + 2 * b], None, ALU.mult)
                    ts(prb[:, b, P:], prb[:, b, P:], st[:, 21 + 2 * b:22 + 2 * b], None, ALU.mult).then_inc(S["pn"], 1)
            pair_out(3)
            dve.wait_ge(S["ysps"], 1)
            for blk in range(4):
                ins = stt(yS[:, blk, SEQ:], qkvu[:, 12 + blk, SEQ:], dsk[:, blk:blk + 1], ps[:, 0, NS * blk:NS * blk + NS], ALU.mult, ALU.add)
            ins.then_inc(S["ysv"], 1)
            def keys_out(b):
                for n in range(5 * b, 5 * b + 5):
                    if n % 2:
                        key_tile_out(n)

            def maxima(half):
                dve.wait_ge(S["sc"], 4 * half + 4)
                stt(s_s[:, 0:512], ps[:, 6, :], SCALE, con[:, C_BS:C_BS + 512], ALU.mult, ALU.add)
                at = C_BS + 512 + 160 * half
                link(stt(s_s[:, 512:672], ps[:, 7, 0:160], SCALE, con[:, at:at + 160], ALU.mult, ALU.add))
                link(dve.tensor_reduce(st[:, 23:24], s_s, AX, ALU.max))
                ts(st[:, 24:25], st[:, 23:24], -1.0, None, ALU.mult).then_inc(S["nms"], 1)

            def normalise(half):
                dve.wait_ge(S["exs"], half + 1)
                link(dve.reciprocal(st[:, 26:27], st[:, 25:26]))
                ts(p_s, p_s, st[:, 26:27], None, ALU.mult).then_inc(S["pns"], 1)

            key_tile_out(H + 1)
            for b in range(2, 5):
                keys_out(b)
            maxima(0)
            keys_out(5)
            normalise(0)
            keys_out(6)
            keys_out(7)
            maxima(1)
            normalise(1)
            dve.wait_ge(S["osel"], 1)
            sel_o = ps[:, 0, 0:2 * P].rearrange("p (a c b g t) -> p a c b g t", a=2, c=4, b=4, g=2)
            for half in range(2):
                for g in range(2):
                    rows = slice(64 * g, 64 * g + 64)
                    dst = aT[rows, :, SEQ + 16 * half:SEQ + 16 * half + 16].rearrange("p c (b t) -> p c b t", t=NSEQ)
                    dve.tensor_copy(dst, sel_o[rows, half, :, :, g, :]).then_inc(S["aTs"], 1)
            yf = yS[:, :, :].rearrange("p a t -> p (a t)")
            link(tt(kvg, yf, yf, ALU.mult))
            link(ts(kvg, kvg, G_B, 1.0, ALU.mult, ALU.add))
            tt(kvg, kvg, yf, ALU.mult).then_inc(S["gel1"], 1)
            dve.wait_ge(S["gel2"], 1)
            tt(yf, yf, kvg, ALU.mult).then_inc(S["gg"], 1)
            for b in range(4):
                dve.wait_ge(S["glu"], b + 1)
                if b == 0:
                    dve.wait_ge(S["glu_ps"], 4)
                ins = tt(yS[:, b, :], yS[:, b, :], kvg.rearrange("p (b t) -> p b t", b=4)[:, b, :], ALU.mult)
            link(ins)
            tt(sqs, yS[:, :, :], yS[:, :, :], ALU.mult).then_inc(S["sq"], 1)
            dve.wait_ge(S["sqA"], 1)
            dve.wait_ge(S["sq"], 1)
            tt(aT[:, :, :], aT[:, :, :], bc(gat.unsqueeze(2), [P, 4, NTOK]), ALU.mult)
            tt(yS[:, :, :], yS[:, :, :], bc(gss.unsqueeze(2), [P, 4, NTOK]), ALU.mult).then_inc(S["mix"], 1)
            dve.wait_ge(S["ssq"], 1)
            for t, (_, n) in enumerate(TILES):
                ins = ts(st[0:n, 36 + 2 * t:38 + 2 * t], ps[0:n, 0, 2 * t:2 * t + 2], 1.0 / 512, EPS, ALU.mult, ALU.add)
            ins.then_inc(S["ms2"], 1)
            dve.wait_ge(S["rt2"], 1)
            link(dve.reciprocal(st[:, 42:48], st[:, 36:42]))
            for t, (_, n) in enumerate(TILES):
                dve.wait_ge(S["wo_ps"], t + 1)
                b0 = 4 * (t % 2)
                xv = x[0:n, t, :].rearrange("p (a n) -> p a n", a=2)
                link(stt(xv, ps[0:n, b0:b0 + 2, :], st[0:n, 42 + 2 * t:43 + 2 * t], xv, ALU.mult, ALU.add))
                stt(xv, ps[0:n, b0 + 2:b0 + 4, :], st[0:n, 43 + 2 * t:44 + 2 * t], xv, ALU.mult, ALU.add).then_inc(S["x2"], 1)
                dve.wait_ge(S["ss3"], t + 1)
                ts(st[:, 51 + t:52 + t], st[:, 48 + t:49 + t], 1.0 / D, EPS, ALU.mult, ALU.add).then_inc(S["ms3"], 1)
                dve.wait_ge(S["rt3"], t + 1)
                link(dve.reciprocal(st[:, 54 + t:55 + t], st[:, 51 + t:52 + t]))
                if t == 0:
                    dve.wait_ge(S["gff"], 16)
                stt(h[0:n, t, :], x[0:n, t, :], st[0:n, 54 + t:55 + t], g_row[0:n, :], ALU.mult, ALU.mult).then_inc(S["h"], 1)
            for j in range(0, J, 2):
                dve.wait_ge(S["hT_ps"], j + 1)
                dve.tensor_copy(accT[:, j, :], ps[:, j, 0:NTOK]).then_inc(S["xT_d"], 1)
            dve.memset(posm, -1.0)
            dve.memset(gate, 0.0)
            link(dve.memset(rt_s[:, :, :, :], 0.0))
            for t, (_, n) in enumerate(TILES):
                dve.wait_ge(S["lg"], 3)
                lg, msk, gt, t8 = rt_s[0:n, t, 0, :], rt_s[0:n, t, 1, :], rt_s[0:n, t, 2, :], top[0:n, t, 0:8]
                link(tt(lg, ps[0:n, 0, 32 * t:32 * t + 32], bro[0:n, :], ALU.add))
                link(dve.max(t8, lg))
                dve.max_index(tidx[0:n, t, :], t8, lg)
                link(ts(top[0:n, t, 8:12], t8[:, 0:4], t8[:, 0:1], None, ALU.subtract))
                dve.tensor_copy(top[0:n, t, 16:20], tidx[0:n, t, 0:4]).then_inc(S["rout"], 1)
            for t, (_, n) in enumerate(TILES):
                dve.wait_ge(S["gex"], t + 1)
                link(dve.reciprocal(top[0:n, t, 21:22], top[0:n, t, 20:21]))
                link(ts(top[0:n, t, 12:16], top[0:n, t, 12:16], top[0:n, t, 21:22], None, ALU.mult))
                o1, o2 = oh[0:n, t, 0], oh[0:n, t, 1]
                link(tt(o1, bc(iota[0:n, 0:NEXP].unsqueeze(1), [n, TOPK, NEXP]), bc(top[0:n, t, 16:20].unsqueeze(2), [n, TOPK, NEXP]), ALU.is_equal))
                link(tt(o2, o1, bc(top[0:n, t, 12:16].unsqueeze(2), [n, TOPK, NEXP]), ALU.mult))
                dve.tensor_reduce(rt_s[0:n, t, 1, :], o1.rearrange("p k e -> p e k"), AX, ALU.add)
                link(dve.tensor_reduce(rt_s[0:n, t, 2, :], o2.rearrange("p k e -> p e k"), AX, ALU.add))
                dve.tensor_copy(gate[0:n, :, t], rt_s[0:n, t, 2, :]).then_inc(S["posm"], 1)
            dve.wait_ge(S["posps"], 1)
            for t, (_, n) in enumerate(TILES):
                link(stt(rt_s[0:n, t, 3, :], ps[0:n, 1, 32 * t:32 * t + 32], 1.0, rt_s[0:n, t, 1, :], ALU.add, ALU.mult))
                link(ts(posm[0:n, :, t], rt_s[0:n, t, 3, :], -1.0, None, ALU.add))
            dve.memset(gslot, 0.0)
            dve.tensor_copy(cnt[:, :], ps[:, 1, 96:128]).then_inc(S["cntr"], 1)

            def add_back(n):
                dve.wait_ge(S["acc0"], J)
                for q in range(J // 2):
                    dve.wait_ge(S["comb"], n * (J // 2) + (q + 1))
                    b, pair = 2 * (q % 2), accT[:, 2 * q:2 * q + 2, :]
                    tt(pair, pair, ps[:, b:b + 2, 0:NTOK], ALU.add).then_inc(S["acc"], 1)

            def rows_low(n):
                dve.wait_ge(S["y_hi"], n + 1)
                stt(y_lo[:, :].rearrange("p (a n) -> p a n", a=2), ps[:, 6:8, :], gslot, y_hi[:, :].bitcast(F32).rearrange("p (a n) -> p a n", a=2),
                    ALU.mult, ALU.subtract).then_inc(S["y_lo"], 1)

            def dve_pass(n, e, first, last):
                def low(*ks):
                    for k in ks:
                        dve.wait_ge(S["w_hi"], n * NPIECE + (k + 1))
                        tt(w_lo[:, k % 4, :], ring_w[:, k % 6, :], w_hi[:, k % 4, :].bitcast(F32), ALU.subtract).then_inc(S["w_lo_v"], 1)

                def mid_low(b):
                    dve.wait_ge(S["mt_hi"], n * 2 + (b + 1))
                    tt(mt_lo[:, 4 * b:4 * b + 4, :], ps[:, 4 + b, :].rearrange("p (m s) -> p m s", m=4), mt_hi[:, 4 * b:4 * b + 4, :].bitcast(F32),
                       ALU.subtract).then_inc(S["mt_lo"], 1)

                def swiglu(b):
                    dve.wait_ge(S["w_used"], n * NPIECE + (4 + 4 * (b + 1)))
                    tt(glu_b, ps[:, 2 * b, :], b1b[:, 512 - 512 * b:1024 - 512 * b], ALU.add)
                    tt(lin[:, b], ps[:, 2 * b + 1, :], b1b[:, DFF + 512 - 512 * b:DFF + 1024 - 512 * b], ALU.add).then_inc(S["swc"], 1)
                    dve.wait_ge(S["swc"], n * 4 + (1 + 2 * b))
                    ts(glu_b, glu_b, LIMIT, None, ALU.min).then_inc(S["glin"], 1)
                    ts(lin[:, b], lin[:, b], LIMIT, -LIMIT, ALU.min, ALU.max)
                    dve.wait_ge(S["sgm"], n * 2 + (b + 1))
                    tt(sig, sig, glu_b, ALU.mult).then_inc(S["swc"], 1)
                    dve.wait_ge(S["swc"], n * 4 + (2 + 2 * b))
                    stt(mid[:, b], lin[:, b], 1.0, sig, ALU.add, ALU.mult).then_inc(S["midr"], 1)

                dve.wait_ge(S["selT"], n + 1)
                ib = bc(iota[:, bass.ds(first, CAP)].unsqueeze(1), [P, 3, CAP])
                pb = bc(posm[:, bass.ds(e, 1), :].rearrange("p e t -> p (e t)").unsqueeze(2), [P, 3, CAP])
                gb = bc(gate[:, bass.ds(e, 1), :].rearrange("p e t -> p (e t)").unsqueeze(2), [P, 3, CAP])
                tt(sel, ib, pb, ALU.is_equal).then_inc(S["sel"], 1)
                low(0)
                rows_low(n)
                for a in range(2):
                    dve.wait_ge(S["xe_hi"], n * 2 + (a + 1))
                    tt(xe_lo[:, 4 * a:4 * a + 4, :], ps[:, 4 + a, :].rearrange("p (j s) -> p j s", j=4), xe_hi[:, 4 * a:4 * a + 4, :].bitcast(F32),
                       ALU.subtract).then_inc(S["xe_lo"], 1)
                dve.wait_ge(S["sel"], n * 2 + 1)
                tt(selg, sel, gb, ALU.mult).then_inc(S["sel"], 1)
                low(2, 3, 5, 6)
                dve.wait_ge(S["b1b"], n * 16 + 16)
                swiglu(0)
                low(8)
                low(9)
                mid_low(0)
                swiglu(1)
                low(11)
                mid_low(1)
                add_back(n)
                dve.wait_ge(S["selT_ps"], n + 2)
                dve.tensor_reduce(gslot, ps[:, 4, 0:NTOK], AX, ALU.add)
                ts(selT[:, :], ps[:, 4, 0:NTOK], 0.0, None, ALU.is_gt).then_inc(S["selT"], 1)

            dve.wait_ge(S["cntr"], 1)
            dve.memset(ps[:, 6:8, :], 0.0).then_inc(S["zero"], 1)
            dve.wait_ge(S["zero"], 1)
            dve.tensor_copy(selT[:, :], ps[:, 6, 0:NTOK]).then_inc(S["selT"], 1)
            total = run_experts(dve, dve_pass)
            rows_low(total)
            add_back(total)
            for t, (_, n) in enumerate(TILES):
                dve.wait_ge(S["fin_ps"], t + 1)
                xv = x[0:n, t, :].rearrange("p (a n) -> p a n", a=2)
                b0 = 2 * t
                tt(xv, xv, ps[0:n, b0:b0 + 2, :], ALU.add).then_inc(S["x3"], 1)
            dve.wait_ge(S["ss4"], 1)
            ts(st[:, 63:66], st[:, 60:63], 1.0 / D, EPS, ALU.mult, ALU.add).then_inc(S["ms4"], 1)
            dve.wait_ge(S["rt4"], 1)
            dve.wait_ge(S["gfi"], 16)
            dve.reciprocal(st[:, 66:69], st[:, 63:66]).then_inc(S["ms4"], 1)
            dve.wait_ge(S["ms4"], 2)
            for t, (_, n) in enumerate(TILES):
                stt(x[0:n, t, :], x[0:n, t, :], st[0:n, 66 + t:67 + t], g_row[0:n, :], ALU.mult, ALU.mult).then_inc(S["yfin"], 1)

        @block.tensor
        def _(pe):
            mm, tp = pe.matmul, pe.transpose

            pe.wait_ge(S["con"], 16)
            pe.wait_ge(S["xn"], 1)
            for j in range(J):
                if j >= 4:
                    pe.wait_ge(S["xT_a"] if j % 2 else S["xT_d"], j // 2 - 1)
                for t, (t0, n) in enumerate(TILES):
                    ins = tp(ps[:, 4 + j % 4, t0:t0 + n], xn[0:n, t, j::J], ident[0:n, 0:n])
                ins.then_inc(S["xT_ps"], 1)
            pe.wait_ge(S["prm"], 16 * NPRM)
            for r in range(2):
                for b in range(4):
                    tp(ps[:, 2 + r, P * b:P * b + P], cnat[:, r, b, :], ident)
                tp(ps[:, 1, P * r:P * r + P], h0row[:, r, :], ident)
            pe.wait_ge(S["rows"], 1)
            for a, src in enumerate((par[0:NI, 0:P], par[0:NI, P:2 * P], st_out[0:NI, 0, :], st_out[0:NI, 1, :])):
                ins = tp(ps[:, 0, NI * a:NI * a + NI], src, ident[0:NI, 0:NI])
            ins.then_inc(S["prmT"], 1)
            blocks = [12, 13, 14, 15] + list(range(12))

            def project(n):
                c = blocks[n]
                if n == 0:
                    pe.wait_ge(S["win0"], 16)
                    pe.wait_ge(S["xT_a"], 4)
                    pe.wait_ge(S["xT_d"], 4)
                if n == 4:
                    pe.wait_ge(S["win1"], 48)
                if n >= 2:
                    pe.wait_ge(S["proj_ev"], n - 1)
                for j in range(J):
                    ins = mm(ps[:, 4 + n % 2, 0:NTOK], w_in[:, c // 4, j, P * (c % 4):P * (c % 4) + P], accT[:, j, :],
                             start=(j == 0), stop=(j == J - 1))
                ins.then_inc(S["proj"], 1)

            for n in range(4):
                project(n)
            pe.wait_ge(S["crev"], 1)
            pe.wait_ge(S["fdone"], 1)
            for r in range(2):
                for b in range(4):
                    ins = tp(ps[:, r, P * b:P * b + P], xb[:, r, P * b:P * b + P], ident)
            ins.then_inc(S["bT_ps"], 1)
            pe.wait_ge(S["bT"], 1)
            pe.wait_ge(S["proj_ev"], 4)

            def bu(i):
                rows = slice(32 * (i % 4), 32 * (i % 4) + 32)
                blk = i // 4
                if i >= 2:
                    pe.wait_ge(S["bu_used"], i - 1)
                for r in range(2):
                    w = bT[rows, r, P * blk:P * blk + P]
                    at = 64 * (i // 2) + NS * r
                    mm(ps[:, i % 2, at:at + NS], w, qkvu[rows, 12 + blk, SEQ:], start=True, stop=True)
                    ins = mm(ps[:, 6 + i % 2, SEQ * r:SEQ * r + SEQ], w, qkvu[rows, 12 + blk, 0:SEQ], start=True, stop=True)
                ins.then_inc(S["bu"], 1)

            def c_h(i):
                blk, q = i // 4, 32 * (i % 4)
                if blk >= 2 and i % 4 == 0:
                    pe.wait_ge(S["yS_ready"], blk - 1)
                pe.wait_ge(S["hlo"], i + 1)
                pe.wait_ge(S["hhi"], i + 1)
                for r in range(2):
                    ins = mm(ps[q:q + 32, 2 + blk % 2, 0:SEQ], cT[:, r, P * blk + q:P * blk + q + 32], ssm_h[:, i % 2, r, :],
                             start=(r == 0), stop=(r == 1), skip_group_check=True)
                ins.then_inc(S["yps"], 1)

            def kv_tokens(n):
                a, t = divmod(n, 3)
                t0, rows = TILES[t]
                if n == 0:
                    pe.wait_ge(S["proj_ev"], 16)
                if n >= 2:
                    pe.wait_ge(S["kvr"], n - 1)
                for b in range(4):
                    ins = tp(ps[0:rows, 4 + n % 2, P * b:P * b + P], qkvu[:, 4 + 4 * a + b, t0:t0 + rows], ident)
                ins.then_inc(S["kvr_ps"], 1)

            bu(0)
            bu(1)
            for n in range(4, 8):
                project(n)
            for i in range(1, NI):
                if i + 1 < NI:
                    bu(i + 1)
                if i <= 8:
                    project(7 + i)
                elif i > 12:
                    kv_tokens(2 * (i - 13))
                    kv_tokens(2 * (i - 13) + 1)
                c_h(i - 1)
            c_h(NI - 1)

            def key_tile(n):
                b = n // 5
                if n % 5 == 0:
                    pe.wait_ge(S[f"kload{b % 2}"], 80 * (b // 2 + 1))
                if n >= 2:
                    pe.wait_ge(S["ktD"] if n % 2 else S["ktA"], n // 2)
                for hp in range(4):
                    at = 512 * (n % 5) + P * hp
                    ins = tp(ps[:, 4 + n % 2, P * hp:P * hp + P], k_cache[:, b % 2, at:at + P], ident)
                ins.then_inc(S["kt_ps"], 1)

            pe.wait_ge(S["bu_used"], NI)
            pe.wait_ge(S["bus"], 1)
            pe.wait_ge(S["kvr"], 6)
            def prompt_scores(hh):
                b, hp, rows = hh % 2, hh // 2, slice(64 * (hh % 2), 64 * (hh % 2) + 64)
                if hh >= 2:
                    pe.wait_ge(S["nm"], hh - 1)
                mm(ps[:, 6 + b, 0:P], qkvu[rows, hp, 0:P], qkvu[rows, 4 + hp, 0:P], start=True, stop=True)
                mm(ps[:, 6 + b, P:3 * P], qkvu[rows, hp, P:SEQ], qkvu[rows, 4 + hp, 0:SEQ], start=True, stop=True).then_inc(S["s_ps"], 1)

            prompt_scores(0)
            for hh in range(H + 1):
                if hh + 1 < H:
                    prompt_scores(hh + 1)
                key_tile(hh)
                if hh >= 1:
                    g = hh - 1
                    b, hp, rows = g % 2, g // 2, slice(64 * (g % 2), 64 * (g % 2) + 64)
                    pe.wait_ge(S["pn"], g + 1)
                    tp(ps[:, b, 0:P], prb[:, b, 0:P], ident)
                    tp(ps[:, b, P:2 * P], prb[:, b, P:2 * P], ident)
                    tp(ps[:, b, 2 * P:3 * P], prb[:, b, 2 * P:3 * P], ident).then_inc(S["pt_ps"], 1)
                    pe.wait_ge(S["pt"], g + 1)
                    if g == 0:
                        pe.wait_ge(S["yS_ready"], 4)
                    if g >= 4 and g % 2 == 0:
                        pe.wait_ge(S["aT"], hp - 1)
                    mm(ps[rows, 2 + hp % 2, 0:SEQ], kv_rows[:, 1, 0, 64 * g:64 * g + 64], ptb[:, b, 0:SEQ], start=True, stop=False, skip_group_check=True)
                    mm(ps[rows, 2 + hp % 2, P:SEQ], kv_rows[:, 1, 1, 64 * g:64 * g + 64], ptb[:, b, SEQ:], start=False, stop=True, skip_group_check=True).then_inc(S["o_ps"], 1)
            pe.wait_ge(S["hs"], 1)
            pe.wait_ge(S["hfin"], 1)
            for i in range(NI):
                blk, q = i // 4, 32 * (i % 4)
                for r in range(2):
                    ins = mm(ps[q:q + 32, 0, NS * blk:NS * blk + NS], cT[:, r, P * blk + q:P * blk + q + 32], hs[:, r, i, :],
                             start=(r == 0), stop=(r == 1), skip_group_check=True)
            ins.then_inc(S["ysps"], 1)
            for r in range(2):
                tp(ps[0:NI, 1, P * r:P * r + P], hf[:, r, :], ident)
                ins = tp(ps[:, 1, SEQ + P * r:SEQ + P * r + P], sf[:, r, :], ident)
            ins.then_inc(S["sto_ps"], 1)

            pe.wait_ge(S["aT"], 4)
            pe.wait_ge(S["qbd"], 1)

            def keys(b):
                for n in range(5 * b, 5 * b + 5):
                    key_tile(n)

            def scores(b):
                rows = slice(32 * (b % 4), 32 * (b % 4) + 32)
                tiles = 5 * (b + 1)
                pe.wait_ge(S["ktA"], (tiles + 1) // 2)
                pe.wait_ge(S["ktD"], tiles // 2)
                if b == 4:
                    pe.wait_ge(S["nms"], 1)
                for hp in range(4):
                    first, last = hp == 0, hp == 3
                    mm(ps[rows, 6, :], qz[:, hp, b, :], kT4[:, b % 2, hp, :], start=first, stop=last, skip_group_check=True)
                for hp in range(4):
                    mm(ps[rows, 7, 0:P], qz[:, hp, b, :], kT1[:, b % 2, hp, :], start=hp == 0, stop=hp == 3, skip_group_check=True)
                for hp in range(4):
                    ins = mm(ps[rows, 7, P:P + NS], qz[:, hp, b, :], qkvu[:, 4 + hp, SEQ:], start=hp == 0, stop=hp == 3, skip_group_check=True)
                ins.then_inc(S["sc"], 1)

            def probs(half):
                pe.wait_ge(S["pns"], half + 1)
                if half == 0:
                    pe.wait_ge(S["ysv"], 1)
                    pe.wait_ge(S["sto"], 1)
                for rt in range(5):
                    tp(ps[:, rt // 4, P * (rt % 4):P * (rt % 4) + P], p_s[:, P * rt:P * rt + P], ident)
                tp(ps[0:NS, 1, P:2 * P], p_s[:, 640:672], ident).then_inc(S["pts_ps"], 1)

            def values(b):
                half, b4 = divmod(b, 4)
                pe.wait_ge(S["pts"], half + 1)
                pe.wait_ge(S[f"vload{b4}"], 80 * (half + 1))
                dst = ps[32 * b4:32 * b4 + 32, 2 + half, :]
                for rt in range(5):
                    mm(dst, p_T[:, P * rt + 32 * b4:P * rt + 32 * b4 + 32], v_cache[:, b4, 512 * rt:512 * rt + 512],
                       start=(rt == 0), stop=False, skip_group_check=True)
                mm(dst, p_T[0:NS, 640 + 32 * b4:672 + 32 * b4], kv_rows[0:NS, 1, 2, :], start=False, stop=True,
                   skip_group_check=True).then_inc(S["pv"], 1)

            key_tile(H + 1)
            for b in range(NB):
                if 1 <= b < NB - 1:
                    keys(b + 1)
                scores(b)
                if b == 4:
                    probs(0)
                if b >= 4:
                    values(b - 4)
            probs(1)
            for b in range(4, NB):
                values(b)
            pe.wait_ge(S["o_ev"], 2)
            for half in range(2):
                for hp in range(4):
                    own = ident.rearrange("p (b r) -> p b r", b=4)[:, :, 8 * hp:8 * hp + 8]
                    at = P * half + 32 * hp
                    ins = mm(ps[:, 0, at:at + 32], o_s[half][:, P * hp:P * hp + P], own, start=True, stop=True)
            ins.then_inc(S["osel"], 1)
            pe.wait_ge(S["wglu"], 32)
            pe.wait_ge(S["gg"], 1)
            for ob in range(4):
                for kb in range(4):
                    ins = mm(ps[:, 4 + ob, 0:NTOK], w_glu[:, kb, P * ob:P * ob + P], yS[:, kb, :], start=(kb == 0), stop=(kb == 3))
                ins.then_inc(S["glu_ps"], 1)
            pe.wait_ge(S["sto"], 1)
            pe.wait_ge(S["sqA"], 1)
            for t, (t0, n) in enumerate(TILES):
                for a, sq in enumerate((sqa, sqs)):
                    for kb in range(4):
                        ins = mm(ps[0:n, 0, 2 * t + a:2 * t + a + 1], sq[:, kb, t0:t0 + n], ones[:, 0:1], start=(kb == 0), stop=(kb == 3))
            ins.then_inc(S["ssq"], 1)
            pe.wait_ge(S["wout"], 16)
            pe.wait_ge(S["mix"], 1)
            pe.wait_ge(S["ms2"], 1)
            for t, (t0, n) in enumerate(TILES):
                b0 = 4 * (t % 2)
                if t == 2:
                    pe.wait_ge(S["x2"], 1)
                for a, src in enumerate((aT, yS)):
                    for kb in range(4):
                        for c in range(2):
                            ins = mm(ps[0:n, b0 + 2 * a + c, :], src[:, kb, t0:t0 + n], w_out[:, 4 * a + kb, 512 * c:512 * c + 512],
                                     start=(kb == 0), stop=(kb == 3))
                ins.then_inc(S["wo_ps"], 1)
            pe.wait_ge(S["h"], 3)
            for j in range(J):
                for t, (t0, n) in enumerate(TILES):
                    ins = tp(ps[:, j, t0:t0 + n], h[0:n, t, j::J], ident[0:n, 0:n])
                ins.then_inc(S["hT_ps"], 1)
            pe.wait_ge(S["xT_a"], 8)
            pe.wait_ge(S["xT_d"], 8)
            for t, (t0, n) in enumerate(TILES):
                for j in range(J):
                    ins = mm(ps[0:n, 0, 32 * t:32 * t + 32], accT[:, j, t0:t0 + n], wr[:, j, :], start=(j == 0), stop=(j == J - 1))
                ins.then_inc(S["lg"], 1)
            pe.wait_ge(S["posm"], 3)
            for t, (t0, n) in enumerate(TILES):
                for u in range(t + 1):
                    m = TILES[u][1]
                    w = tri[0:m, 0:n] if u == t else ones[0:m, 0:n]
                    mm(ps[0:n, 1, 32 * t:32 * t + 32], w, rt_s[0:m, u, 1, :], start=(u == 0), stop=(u == t))
            for u in range(3):
                m = TILES[u][1]
                ins = mm(ps[:, 1, 96:128], ones[0:m, :], rt_s[0:m, u, 1, :], start=(u == 0), stop=(u == 2))
                if u == 0:
                    ins.then_inc(S["selT_ps"], 1)
            ins.then_inc(S["posps"], 1)
            for t, (t0, n) in enumerate(TILES):
                ins = tp(ps[0:NEXP, 4, t0:t0 + n], rt_s[0:n, t, 2, :], ident[0:n, 0:n])
            ins.then_inc(S["gT_ps"], 1)
            pe.wait_ge(S["gT"], 1)
            pe.wait_ge(S["b2"], 16)
            for j in range(J):
                if j >= 2:
                    pe.wait_ge(S["acc0"], j - 1)
                mm(ps[:, 2 + j % 2, 0:NTOK], b2_rows[:, P * j:P * j + P], gT[:, :], start=True, stop=True).then_inc(S["b2ps"], 1)
            pe.wait_ge(S["cntr"], 1)
            pe.wait_ge(S["acc0"], J)

            def sum_back(n, half):
                pe.wait_ge(S["y_lo"], n + 1)
                pe.wait_ge(S["selT"], n + 1)
                for j in range(4 * half, 4 * half + 4):
                    if j % 2 == 0 and j >= 4:
                        pe.wait_ge(S["acc"], n * (J // 2) + j // 2)
                    mm(ps[:, j % 4, 0:NTOK], y_hi[:, P * j:P * j + P], selT[:, :], start=True, stop=False)
                    ins = mm(ps[:, j % 4, 0:NTOK], y_lo[:, P * j:P * j + P], selT[:, :], start=False, stop=True)
                    if j % 2:
                        ins.then_inc(S["comb"], 1)

            def pe_pass(n, e, first, last):
                def three(out, x_hi, x_lo, w, start, stop):
                    for c, o in enumerate(out):
                        mm(o, x_hi, w[0][c], start=start, stop=False)
                    for c, o in enumerate(out):
                        mm(o, x_hi, w[1][c], start=False, stop=False)
                    for c, o in enumerate(out):
                        ins = mm(o, x_lo, w[0][c], start=False, stop=stop)
                    return ins

                def first_product(k):
                    wait_low(pe, n, k)
                    b = k // 4
                    for jj in range(2):
                        j = 2 * (k % 4) + jj
                        w = [[t[:, k % 4, 1024 * jj + 512 * g:1024 * jj + 512 * g + 512] for g in range(2)] for t in (w_hi, w_lo)]
                        ins = three([ps[:, 2 * b + g, :] for g in range(2)], xe_hi[:, j, :], xe_lo[:, j, :], w, j == 0, j == J - 1)
                    ins.then_inc(S["w_used"], 1)

                def mid_transposed(b):
                    pe.wait_ge(S["midr"], n * 2 + (b + 2))
                    for m in range(4):
                        op = mm if m == 0 else tp
                        ins = op(ps[:, 4 + b, CAP * m:CAP * m + CAP], mid[:, b, P * m:P * m + P], ident)
                    ins.then_inc(S["mt_ps"], 1)

                def second_product(k):
                    wait_low(pe, n, k)
                    for mm_ in range(2):
                        m = 2 * (k - 8) + mm_
                        w = [[t[:, k % 4, 1024 * mm_ + 512 * c:1024 * mm_ + 512 * c + 512] for c in range(2)] for t in (w_hi, w_lo)]
                        ins = three([ps[:, 6 + c, :] for c in range(2)], mt_hi[:, m, :], mt_lo[:, m, :], w, m == 0, m == J - 1)
                    ins.then_inc(S["w_used"], 1)

                pe.wait_ge(S["selT"], n + 1)
                pe.wait_ge(S["sel"], n * 2 + 1)
                for a in range(2):
                    for j in range(4 * a, 4 * a + 4):
                        for t, (t0, k) in enumerate(TILES):
                            ins = mm(ps[:, 4 + a, CAP * (j % 4):CAP * (j % 4) + CAP], h[0:k, t, j::J], sel[0:k, t, :], start=(t == 0), stop=(t == 2))
                    ins.then_inc(S["gath"], 1)
                pe.wait_ge(S["xe_lo"], n * 2 + 1)
                pe.wait_ge(S["acc"], n * (J // 2) + 1)
                first_product(0)
                first_product(1)
                pe.wait_ge(S["xe_lo"], n * 2 + 2)
                first_product(2)
                first_product(3)
                first_product(4)
                first_product(5)
                first_product(6)
                mid_transposed(0)
                first_product(7)
                pe.wait_ge(S["mt_lo"], n * 2 + 1)
                pe.wait_ge(S["y_lo"], n + 1)
                second_product(8)
                second_product(9)
                mid_transposed(1)
                sum_back(n, 0)
                pe.wait_ge(S["sel"], n * 2 + 2)
                for t, (t0, k) in enumerate(TILES):
                    op = mm if t == 0 else tp
                    ins = op(ps[:, 4, t0:t0 + k], selg[0:k, t, :], ident[0:k, 0:k])
                ins.then_inc(S["selT_ps"], 1)
                pe.wait_ge(S["mt_lo"], n * 2 + 2)
                second_product(10)
                sum_back(n, 1)
                second_product(11)

            pe.wait_ge(S["zero"], 1)
            total = run_experts(pe, pe_pass)
            pe.wait_ge(S["acc"], total * (J // 2) + 1)
            sum_back(total, 0)
            sum_back(total, 1)
            pe.wait_ge(S["acc"], total * (J // 2) + (J // 2 + 1))
            for t, (t0, n) in enumerate(TILES):
                for j in range(J):
                    ins = tp(ps[0:n, 2 * t + j // 4, P * (j % 4):P * (j % 4) + P], accT[:, j, t0:t0 + n], ident)
                ins.then_inc(S["fin_ps"], 1)


_INS = """x_prompt x_sample cache_k cache_v state_ssm_re state_ssm_im norm_mix_g w_in attn_out_norm_g
    ssm_a_re ssm_a_im ssm_log_dt ssm_b_re ssm_b_im ssm_c_re ssm_c_im ssm_d w_glu b_glu ssm_out_norm_g
    w_out norm_ffn_g w_router b_router w_moe1 b_moe1 w_moe2 b_moe2 norm_final_g""".split()
_OUTS = [("y_p", (1, SEQ, D)), ("y_s", (NB, NSEQ, D)), ("k_p", (1, 1, SEQ, H, HD)), ("v_p", (1, 1, SEQ, H, HD)),
         ("re_p", (1, 1, 32, 64)), ("im_p", (1, 1, 32, 64)), ("k_s", (1, NB, NSEQ, H, HD)), ("v_s", (1, NB, NSEQ, H, HD)),
         ("re_s", (1, NB, 32, 64)), ("im_s", (1, NB, 32, 64))]


def kernel(**inputs):
    import numpy as _np
    import concourse.bacc as _bacc
    from concourse import mybir as _mybir
    from concourse.bass_utils import run_bass_kernel_spmd as _run

    nc = _bacc.Bacc("TRN2", target_bir_lowering=False, num_devices=1, dynamic_dma_scratch_size=1024)
    arrays, ins, outs = {}, {}, {}
    for name in _INS + ["con"]:
        a = constants() if name == "con" else _np.ascontiguousarray(inputs[name])
        arrays[f"in_{name}_dram"] = a
        ins[name] = nc.dram_tensor(f"in_{name}_dram", a.shape, _mybir.dt.from_np(a.dtype), kind="ExternalInput").ap()
    for name, shape in _OUTS:
        outs[name] = nc.dram_tensor(f"out_{name}_dram", shape, _mybir.dt.float32, kind="ExternalOutput").ap()
    decoder_step(nc, ins, outs)
    r = _run(nc, [arrays], core_ids=[0])
    return tuple(r.results[0][f"out_{name}_dram"] for name, _ in _OUTS)
```
